# Optimizing a Trainium2 kernel written in Bass

```python
import jax, jax.numpy as jnp
from jax import lax
import numpy as np

D_MODEL = 1024
BATCH = 1
SEQ = 1024
DEPTH = 1
DEC_BATCH = 8
DEC_SEQ = 1
PAST_LEN = 2048
PAGE_SIZE = 128

HEAD_DIM = 64
N_HEADS_SB = 8
SB_WIDTH = N_HEADS_SB * HEAD_DIM
SB_BLOCK = 128
SB_BIAS_INIT = -6.0
DIL_CONFIGS = ((128, 1), (512, 4), (2048, 16))
N_DIL_GROUPS = len(DIL_CONFIGS)
HEADS_PER_GROUP = 4
DIL_GROUP_WIDTH = HEADS_PER_GROUP * HEAD_DIM
DIL_WIDTH = N_DIL_GROUPS * DIL_GROUP_WIDTH
IN_SPLITS = (SB_WIDTH,) * 3 + (DIL_WIDTH,) * 3 + (D_MODEL,) * 2
IN_WIDTH = sum(IN_SPLITS)
ROPE_THETA = 10000.0
RMS_EPS = 1e-6
N_EXPERTS = 64
N_EXPERT_GROUPS = 8
TOPK_GROUPS = 4
TOP_K = 8
D_EXPERT = 256
D_SHARED = 256
ROUTED_SCALE = 2.5
MOE_BLOCK_PROMPT = 128
MOE_BLOCK_SAMPLE = 8

kernel_name = 'hybrid_stickbreak_dilated_moe_step'

F32 = jnp.float32

def rmsnorm(x, g):
    xf = x.astype(F32)
    y = xf * lax.rsqrt(jnp.mean(xf * xf, axis=-1, keepdims=True) + RMS_EPS)
    return (y * g.astype(F32)).astype(x.dtype)

def rope(x, pos):
    half = x.shape[-1] // 2
    inv = ROPE_THETA ** (-jnp.arange(half, dtype=F32) / half)
    ang = pos.astype(F32)[:, None] * inv[None, :]
    cos = jnp.cos(ang)[None, :, None, :]
    sin = jnp.sin(ang)[None, :, None, :]
    xf = x.astype(F32)
    x1, x2 = xf[..., :half], xf[..., half:]
    return jnp.concatenate([x1 * cos - x2 * sin, x2 * cos + x1 * sin], axis=-1).astype(x.dtype)

def project_inputs(h, pos, w_in, qn_g, kn_g):
    B, S, _ = h.shape
    offs = np.cumsum(IN_SPLITS)[:-1].tolist()
    sq, sk, sv, dq, dk, dv, ga, gb = jnp.split(h @ w_in, offs, axis=-1)
    n_dil = N_DIL_GROUPS * HEADS_PER_GROUP
    grp = (B, S, N_DIL_GROUPS, HEADS_PER_GROUP, HEAD_DIM)
    dq = rope(rmsnorm(dq.reshape(B, S, n_dil, HEAD_DIM), qn_g), pos).reshape(grp)
    dk = rope(rmsnorm(dk.reshape(B, S, n_dil, HEAD_DIM), kn_g), pos).reshape(grp)
    dv = dv.reshape(grp)
    sb = lambda a: a.reshape(B, S, N_HEADS_SB, HEAD_DIM)
    return (sb(sq), sb(sk), sb(sv), dq, dk, dv, jax.nn.sigmoid(ga), jax.nn.sigmoid(gb))

def stick_breaking(q, k, v, q_pos, k_pos, bias):
    z = jnp.einsum('bqhd,bkhd->bhqk', q.astype(F32), k.astype(F32)) * HEAD_DIM ** -0.5
    z = z + bias.astype(F32)[None, :, None, None]
    causal = (k_pos[None, :] < q_pos[:, None])[None, None]
    log_stay = jnp.where(causal, jax.nn.log_sigmoid(-z), 0.0)
    between = lax.cumsum(log_stay, axis=3, reverse=True) - log_stay
    a = jnp.where(causal, jnp.exp(jax.nn.log_sigmoid(z) + between), 0.0)
    return jnp.einsum('bhqk,bkhd->bqhd', a, v.astype(F32))

def stick_breaking_prompt(q, k, v, bias):
    B, S, H, D = q.shape
    nq = S // SB_BLOCK
    pos = jnp.arange(S)
    qb = q.reshape(B, nq, SB_BLOCK, H, D).transpose(1, 0, 2, 3, 4)
    ob = lax.map(lambda a: stick_breaking(a[0], k, v, a[1], pos, bias), (qb, pos.reshape(nq, SB_BLOCK)))
    return ob.transpose(1, 0, 2, 3, 4).reshape(B, S, H, D), jnp.stack([k, v], axis=2)

def stick_breaking_sample(q, k, v, bias, pool, page_table):
    DB, T, H, D = q.shape
    past_len = page_table.shape[1] * pool.shape[1]
    past = pool[page_table].reshape(DB, past_len, 2, H, D)
    new = jnp.stack([k, v], axis=2).astype(pool.dtype)
    kv = jnp.concatenate([past, new], axis=1)
    o = stick_breaking(q, kv[:, :, 0], kv[:, :, 1], past_len + jnp.arange(T), jnp.arange(past_len + T), bias)
    return o, new

def masked_softmax_attend(s, valid, v, spec):
    s = jnp.where(valid, s, -jnp.inf)
    m = jnp.max(s, axis=-1, keepdims=True)
    e = jnp.exp(s - m)
    den = jnp.sum(e, axis=-1, keepdims=True)
    o = jnp.einsum(spec, e / den, v.astype(F32))
    return o, (m + jnp.log(den))[..., 0]

def dilated_band_attn(q, k, v, window, dil):
    B, S, H, D = q.shape
    n = window // dil
    L = S // dil
    nb = -(-L // n)
    pad = nb * n - L

    def residues(a):
        return a.reshape(B, L, dil, H, D).transpose(0, 2, 1, 3, 4)

    qb = jnp.pad(residues(q), ((0, 0), (0, 0), (0, pad), (0, 0), (0, 0))).reshape(B, dil, nb, n, H, D)

    def band(a):
        ap = jnp.pad(residues(a), ((0, 0), (0, 0), (n, pad), (0, 0), (0, 0)))
        prev = ap[:, :, :nb * n].reshape(B, dil, nb, n, H, D)
        cur = ap[:, :, n:].reshape(B, dil, nb, n, H, D)
        return jnp.concatenate([prev, cur], axis=3)

    kb, vb = band(k), band(v)
    s = jnp.einsum('brcqhd,brckhd->brchqk', qb.astype(F32), kb.astype(F32)) * HEAD_DIM ** -0.5
    qi = jnp.arange(n)[:, None]
    ki = jnp.arange(2 * n)[None, :]
    dist = qi + n - ki
    key_idx = jnp.arange(nb)[:, None, None] * n + ki - n
    valid = (dist >= 0) & (dist <= n) & (key_idx >= 0)
    o, lse = masked_softmax_attend(s, valid[None, None, :, None], vb, 'brchqk,brckhd->brcqhd')
    o = o.reshape(B, dil, nb * n, H, D)[:, :, :L].transpose(0, 2, 1, 3, 4).reshape(B, S, H, D)
    lse = lse.transpose(0, 1, 2, 4, 3).reshape(B, dil, nb * n, H)[:, :, :L].transpose(0, 2, 1, 3).reshape(B, S, H)
    return o, lse

def dilated_step(q, k_new, v_new, buf, window, dil):
    T = q.shape[1]
    n = window // dil
    kv = jnp.concatenate([buf, jnp.stack([k_new, v_new], axis=2).astype(buf.dtype)], axis=1)
    idx = buf.shape[1] + jnp.arange(T)[:, None] - dil * jnp.arange(n + 1)[None, :]
    g = kv[:, jnp.maximum(idx, 0)]
    s = jnp.einsum('bthd,btjhd->bhtj', q.astype(F32), g[:, :, :, 0].astype(F32)) * HEAD_DIM ** -0.5
    o, lse = masked_softmax_attend(s, (idx >= 0)[None, None], g[:, :, :, 1], 'bhtj,btjhd->bthd')
    keep = min(window, kv.shape[1])
    return o, lse.transpose(0, 2, 1), kv[:, kv.shape[1] - keep:]

def combine_by_denominator(outs, lses):
    w = jax.nn.softmax(jnp.stack(lses), axis=0)
    return jnp.sum(w[..., None] * jnp.stack(outs), axis=0)

def dilated_prompt(q, k, v):
    outs, lses, bufs = [], [], []
    for g, (win, dil) in enumerate(DIL_CONFIGS):
        o, l = dilated_band_attn(q[:, :, g], k[:, :, g], v[:, :, g], win, dil)
        outs.append(o)
        lses.append(l)
        kv = jnp.stack([k[:, :, g], v[:, :, g]], axis=2)
        bufs.append(kv[:, kv.shape[1] - min(win, kv.shape[1]):])
    return combine_by_denominator(outs, lses), bufs

def dilated_sample(q, k, v, bufs):
    outs, lses, new_bufs = [], [], []
    for g, (win, dil) in enumerate(DIL_CONFIGS):
        o, l, nbuf = dilated_step(q[:, :, g], k[:, :, g], v[:, :, g], bufs[g], win, dil)
        outs.append(o)
        lses.append(l)
        new_bufs.append(nbuf)
    return combine_by_denominator(outs, lses), new_bufs

def swiglu(x, wg, wu, wd):
    return (jax.nn.silu(x @ wg) * (x @ wu)) @ wd

def route(h, w_router, router_bias):
    M = h.shape[0]
    scores = jax.nn.sigmoid((h @ w_router).astype(F32))
    sel = scores + router_bias.astype(F32)
    per = N_EXPERTS // N_EXPERT_GROUPS
    grp = lax.top_k(sel.reshape(M, N_EXPERT_GROUPS, per), 2)[0].sum(-1)
    _, gidx = lax.top_k(grp, TOPK_GROUPS)
    gmask = jax.nn.one_hot(gidx, N_EXPERT_GROUPS, dtype=F32).sum(1) > 0
    sel = jnp.where(jnp.repeat(gmask, per, axis=1), sel, -jnp.inf)
    _, eidx = lax.top_k(sel, TOP_K)
    w = jnp.take_along_axis(scores, eidx, axis=1)
    return eidx, w / jnp.sum(w, axis=-1, keepdims=True) * ROUTED_SCALE

def routed_experts(h, eidx, gate_w, w_e_gate, w_e_up, w_e_down, blk):
    M, D = h.shape
    A = M * TOP_K
    flat_e = eidx.reshape(A)
    order = jnp.argsort(flat_e)
    se = flat_e[order]
    st = (order // TOP_K).astype(jnp.int32)
    sw = gate_w.reshape(A)[order].astype(h.dtype)
    counts = jnp.bincount(flat_e, length=N_EXPERTS)
    padded = (counts + blk - 1) // blk * blk
    pend = jnp.cumsum(padded)
    dest = (pend - padded)[se] + jnp.arange(A) - (jnp.cumsum(counts) - counts)[se]
    n_blocks = (A + N_EXPERTS * (blk - 1) + blk - 1) // blk
    n_rows = n_blocks * blk
    row_tok = jnp.full((n_rows,), M, jnp.int32).at[dest].set(st)
    row_w = jnp.zeros((n_rows,), h.dtype).at[dest].set(sw)
    block_e = jnp.minimum(jnp.searchsorted(pend, jnp.arange(n_blocks) * blk, side='right'), N_EXPERTS - 1)
    h_pad = jnp.concatenate([h, jnp.zeros((1, D), h.dtype)], axis=0)

    def expert_block(args):
        tok, e = args
        return swiglu(h_pad[tok], w_e_gate[e], w_e_up[e], w_e_down[e])

    ys = lax.map(expert_block, (row_tok.reshape(n_blocks, blk), block_e)).reshape(n_rows, D)
    out = jnp.zeros((M + 1, D), ys.dtype).at[row_tok].add(ys * row_w[:, None])
    return out[:M]

def moe(h, blk, w_router, router_bias, w_e_gate, w_e_up, w_e_down, w_s_gate, w_s_up, w_s_down):
    B, S, D = h.shape
    hf = h.reshape(B * S, D)
    eidx, gw = route(hf, w_router, router_bias)
    routed = routed_experts(hf, eidx, gw, w_e_gate, w_e_up, w_e_down, blk)
    shared = swiglu(hf, w_s_gate, w_s_up, w_s_down)
    return (routed + shared).astype(h.dtype).reshape(B, S, D)

def decoder_layer(x, pos, sb_attn, dil_attn, moe_blk, norm1_g, w_in, qn_g, kn_g, sb_bias, w_br_a, w_br_b, w_out,
                  norm2_g, w_router, router_bias, w_e_gate, w_e_up, w_e_down, w_s_gate, w_s_up, w_s_down):
    B, S, _ = x.shape
    h = rmsnorm(x, norm1_g)
    sq, sk, sv, dq, dk, dv, ga, gb = project_inputs(h, pos, w_in, qn_g, kn_g)
    o_sb, sb_rows = sb_attn(sq, sk, sv, sb_bias)
    o_dil, win_bufs = dil_attn(dq, dk, dv)
    y_a = o_sb.astype(x.dtype).reshape(B, S, SB_WIDTH) @ w_br_a
    y_b = o_dil.astype(x.dtype).reshape(B, S, DIL_GROUP_WIDTH) @ w_br_b
    x = x + (ga * y_a + gb * y_b) @ w_out
    x = x + moe(rmsnorm(x, norm2_g), moe_blk, w_router, router_bias, w_e_gate, w_e_up, w_e_down,
                w_s_gate, w_s_up, w_s_down)
    return x, sb_rows, win_bufs

def setup_inputs(seed: int = 0) -> dict:
    key = jax.random.key(seed)
    ks = iter(jax.random.split(key, 32))

    def nrm(shape, scale=1.0):
        return jax.random.normal(next(ks), shape, jnp.float32) * scale

    def gain(shape):
        return 1.0 + nrm(shape, 0.02)

    n_pages = PAST_LEN // PAGE_SIZE
    n_used = DEC_BATCH * n_pages
    n_pool = n_used + max(1, n_used // 4)
    inp = {}
    inp['x_prompt'] = nrm((BATCH, SEQ, D_MODEL))
    inp['x_sample'] = nrm((DEC_BATCH, DEC_SEQ, D_MODEL))
    inp['cache_sb_kv'] = nrm((DEPTH, n_pool, PAGE_SIZE, 2, N_HEADS_SB, HEAD_DIM))
    inp['page_table'] = jax.random.permutation(next(ks), n_pool)[:n_used].reshape(DEC_BATCH, n_pages).astype(jnp.int32)
    for g, (win, _) in enumerate(DIL_CONFIGS):
        inp['cache_win%d_kv' % g] = nrm((DEPTH, DEC_BATCH, min(win, PAST_LEN), 2, HEADS_PER_GROUP, HEAD_DIM))
    inp['norm1_g'] = gain((DEPTH, D_MODEL))
    inp['w_in'] = nrm((DEPTH, D_MODEL, IN_WIDTH), D_MODEL ** -0.5)
    inp['qn_g'] = gain((DEPTH, HEAD_DIM))
    inp['kn_g'] = gain((DEPTH, HEAD_DIM))
    inp['sb_bias'] = SB_BIAS_INIT + nrm((DEPTH, N_HEADS_SB), 0.1)
    inp['w_br_a'] = nrm((DEPTH, SB_WIDTH, D_MODEL), SB_WIDTH ** -0.5)
    inp['w_br_b'] = nrm((DEPTH, DIL_GROUP_WIDTH, D_MODEL), DIL_GROUP_WIDTH ** -0.5)
    inp['w_out'] = nrm((DEPTH, D_MODEL, D_MODEL), D_MODEL ** -0.5)
    inp['norm2_g'] = gain((DEPTH, D_MODEL))
    inp['w_router'] = nrm((DEPTH, D_MODEL, N_EXPERTS), D_MODEL ** -0.5)
    inp['router_bias'] = nrm((DEPTH, N_EXPERTS), 0.01)
    inp['w_e_gate'] = nrm((DEPTH, N_EXPERTS, D_MODEL, D_EXPERT), D_MODEL ** -0.5)
    inp['w_e_up'] = nrm((DEPTH, N_EXPERTS, D_MODEL, D_EXPERT), D_MODEL ** -0.5)
    inp['w_e_down'] = nrm((DEPTH, N_EXPERTS, D_EXPERT, D_MODEL), D_EXPERT ** -0.5)
    inp['w_s_gate'] = nrm((DEPTH, D_MODEL, D_SHARED), D_MODEL ** -0.5)
    inp['w_s_up'] = nrm((DEPTH, D_MODEL, D_SHARED), D_MODEL ** -0.5)
    inp['w_s_down'] = nrm((DEPTH, D_SHARED, D_MODEL), D_SHARED ** -0.5)
    return inp

def reference(x_prompt, x_sample, cache_sb_kv, page_table, cache_win0_kv, cache_win1_kv, cache_win2_kv,
              norm1_g, w_in, qn_g, kn_g, sb_bias, w_br_a, w_br_b, w_out, norm2_g, w_router, router_bias,
              w_e_gate, w_e_up, w_e_down, w_s_gate, w_s_up, w_s_down):
    win_caches = (cache_win0_kv, cache_win1_kv, cache_win2_kv)
    S = x_prompt.shape[1]
    T = x_sample.shape[1]
    past_len = page_table.shape[1] * cache_sb_kv.shape[2]
    pos_p = jnp.arange(S)
    pos_s = past_len + jnp.arange(T)
    yp, ys = x_prompt, x_sample
    sb_p, sb_s = [], []
    win_p = [[] for _ in DIL_CONFIGS]
    win_s = [[] for _ in DIL_CONFIGS]
    for layer in range(DEPTH):
        lw = (norm1_g[layer], w_in[layer], qn_g[layer], kn_g[layer], sb_bias[layer], w_br_a[layer], w_br_b[layer],
              w_out[layer], norm2_g[layer], w_router[layer], router_bias[layer], w_e_gate[layer], w_e_up[layer],
              w_e_down[layer], w_s_gate[layer], w_s_up[layer], w_s_down[layer])
        pool = cache_sb_kv[layer]
        bufs = [c[layer] for c in win_caches]
        sb_sample_fn = lambda q, k, v, b, pool=pool: stick_breaking_sample(q, k, v, b, pool, page_table)
        dil_sample_fn = lambda q, k, v, bufs=bufs: dilated_sample(q, k, v, bufs)
        yp, rows_p, bufs_p = decoder_layer(yp, pos_p, stick_breaking_prompt, dilated_prompt, MOE_BLOCK_PROMPT, *lw)
        ys, rows_s, bufs_s = decoder_layer(ys, pos_s, sb_sample_fn, dil_sample_fn, MOE_BLOCK_SAMPLE, *lw)
        sb_p.append(rows_p)
        sb_s.append(rows_s)
        for g in range(N_DIL_GROUPS):
            win_p[g].append(bufs_p[g])
            win_s[g].append(bufs_s[g])
    sb_kv_prompt = jnp.stack(sb_p)
    sb_kv_sample = jnp.stack(sb_s)
    win0_prompt, win1_prompt, win2_prompt = [jnp.stack(w) for w in win_p]
    win0_sample, win1_sample, win2_sample = [jnp.stack(w) for w in win_s]
    return (yp, ys, sb_kv_prompt, sb_kv_sample, win0_prompt, win0_sample, win1_prompt, win1_sample, win2_prompt, win2_sample)


_drawn_inputs = setup_inputs


def setup_inputs(seed=0):
    import zlib

    import numpy as np

    out = dict(_drawn_inputs(seed))
    spreads = {}
    factors = {'qn_g': 3.554, 'kn_g': 3.178}
    for name, (base, spread) in spreads.items():
        noise = np.random.default_rng([zlib.crc32(name.encode()), seed]).standard_normal(out[name].shape)
        drawn = base * np.exp(spread * noise) if base else spread * noise
        out[name] = __import__('jax').numpy.asarray(drawn.astype(out[name].dtype))
    for name, factor in factors.items():
        out[name] = (out[name] * factor).astype(out[name].dtype)
    return out
```

```python
import math
from contextlib import ExitStack

import numpy as np
import concourse.bass as bass
from concourse import mybir

ALU = mybir.AluOpType
ACT = mybir.ActivationFunctionType
F32 = mybir.dt.float32
F32R = mybir.dt.float32r
I32 = mybir.dt.int32
AX_X = mybir.AxisListType.X
P = 128

D = 1024
S = 1024
NS = 8
T = S + NS
NT = S // P + 1
PAST = 2048
PAGE = 128
NPAGES = PAST // PAGE
HD = 64
SBH = 8
SBW = SBH * HD
WIN = (128, 512, 2048)
DIL = (1, 4, 16)
NG = 3
GH = 4
GW = GH * HD
DW = NG * GW
KC = D // P
E = 64
EG = 8
PER = E // EG
TOPG = 4
TOPK = 8
DE = 256
BLK = 160
TURN = 2
NBLK = -(-((T * TOPK + E * (BLK - 1)) // BLK) // TURN) * TURN
SLOTS = NBLK * BLK
WHOLE = 4
SURE = T * TOPK // BLK // WHOLE * WHOLE
EPS = 1e-6
BIG = 1e30


def rows_of(t):
    return P if t < NT - 1 else NS


def plan_projection():
    items = []
    for n in range(8):
        width = 512 if n < 7 else 256
        for t in range(NT):
            items.append(dict(n=n, t=t, w=width, normed=3 <= n <= 5,
                              turned=n in (0, 1, 3, 4, 5) and t < NT - 1))
    return items


TURN_BASE = {0: 0, 1: 4, 3: 8, 4: 12, 5: 16}


def build(nc, a, o):
    (y_prompt, y_sample, sb_prompt, sb_sample, win0_p, win0_s, win1_p, win1_s, win2_p, win2_s) = o
    win_p, win_s = (win0_p, win1_p, win2_p), (win0_s, win1_s, win2_s)
    caches = (a["cache_win0_kv"], a["cache_win1_kv"], a["cache_win2_kv"])

    def dram(name, shape, dt=F32):
        return nc.dram_tensor(name, shape, dt).ap()

    scratch = dict(
        ht=dram("ht_scratch", [P, KC * T]),
        samp=dram("samp_scratch", [NS, 3 * SBW + 3 * DW]),
        dv=dram("dv_scratch", [S, DW]),
        znew=dram("znew_scratch", [NS, NG * GH]),
        mde=dram("mde_scratch", [NS * NG * GH, 3]),
        od=dram("od_scratch", [NG, T, GW + 2 * GH]),
        x1=dram("x1_scratch", [T, D]),
        x2=dram("x2_scratch", [T, D]),
        h2=dram("h2_scratch", [T + 1, D]),
        table=dram("table_scratch", [SLOTS, 1], I32),
        eb=dram("eb_scratch", [1, NBLK + 1], I32),
        y=dram("y_scratch", [SLOTS, D]),
    )
    with ExitStack() as ctx:
        sb = lambda name, shape, dt=F32: ctx.enter_context(nc.sbuf_tensor(name, shape, dt))
        held = []

        def semaphore(name):
            held.append(nc.alloc_semaphore(name=name))
            return held[-1]

        scratch["semaphore"] = semaphore
        ident = sb("ident", [P, P])
        scores = sb("scores", [P, NT, E])
        dest = sb("dest", [P, NT * TOPK], I32)
        weight = sb("weight", [P, NT * TOPK])
        expert_row = sb("expert_row", [1, NBLK + 1], I32)
        slot_token = sb("slot_token", [P, NBLK], I32)
        slot_token_tail = sb("slot_token_tail", [BLK - P, NBLK], I32)
        with ExitStack() as attention:
            turned = attention.enter_context(nc.sbuf_tensor("turned", [P, 20, S], F32))
            phase_project(nc, a, o, scratch, ident, turned)
            oT = attention.enter_context(nc.sbuf_tensor("oT", [P, SBH // 2, T], F32))
            odT = attention.enter_context(nc.sbuf_tensor("odT", [P, GW // P, T], F32))
            phase_sample_stick(nc, a, o, scratch, ident, oT)
            phase_prompt_stick(nc, a, o, scratch, turned, oT)
            phase_sample_window(nc, a, o, scratch, ident)
            phase_prompt_window(nc, a, o, scratch, ident, turned, odT)
            nc.clear_and_free_semaphores(held)
            nc.all_engine_barrier()
            phase_gate(nc, a, o, scratch, turned, oT, odT)
            phase_out(nc, a, o, scratch, ident, turned, scores)
            phase_shared(nc, a, o, scratch, turned)
        phase_route(nc, a, o, scratch, ident, scores, dest, weight, expert_row, slot_token, slot_token_tail)
        phase_experts(nc, a, o, scratch, ident, expert_row, slot_token, slot_token_tail)
        phase_combine(nc, a, o, scratch, dest, weight)


def phase_project(nc, a, o, sc, ident, turned):
    (y_prompt, y_sample, sb_prompt, sb_sample, win0_p, win0_s, win1_p, win1_s, win2_p, win2_s) = o
    win_p, win_s = (win0_p, win1_p, win2_p), (win0_s, win1_s, win2_s)
    caches = (a["cache_win0_kv"], a["cache_win1_kv"], a["cache_win2_kv"])
    items = plan_projection()
    NI = len(items)
    NSTAGE = 4
    w_view = a["w_in"][0].rearrange("(p c) n -> p c n", c=KC)

    with ExitStack() as ctx:
        sb = lambda name, shape, dt=F32: ctx.enter_context(nc.sbuf_tensor(name, shape, dt))
        sem = sc["semaphore"]
        xin = sb("xin", [P, 2, D])
        junk = sb("junk", [P, D])
        h = sb("h", [P, 2, D])
        gain = sb("gain", [P, D])
        ss = sb("ss", [P, NT])
        rms = sb("rms", [P, NT])
        rstd = sb("rstd", [P, NT])
        eps = sb("eps", [P, 1])
        hT = sb("hT", [P, KC, T])
        wbuf = sb("wbuf", [P, 2, KC, 512])
        stage = sb("stage", [P, NSTAGE, 512])
        sqr = sb("sqr", [P, 512])
        ropeA = sb("ropeA", [P, 512])
        ropeB = sb("ropeB", [P, 512])
        hss = sb("hss", [P, 8])
        hrms = sb("hrms", [P, 8])
        hrs = sb("hrs", [P, 8])
        qkgain = sb("qkgain", [P, 3, 512])
        cos = sb("cos", [P, NT, 32])
        sin = sb("sin", [P, NT, 32])
        pP = ctx.enter_context(nc.psum_tensor("pP", [P, 4, 512], F32))
        pT = ctx.enter_context(nc.psum_tensor("pT", [P, 4, 512], F32))

        consts_in = sem("consts_in")
        x_in = [sem(f"x_in{i}") for i in range(2)]
        w_loaded = [sem(f"w_loaded{i}") for i in range(2)]
        stored = [sem(f"stored{i}") for i in range(NSTAGE)]
        ht_out = sem("ht_out")
        copies_out = sem("copies_out")
        ss_ready = sem("ss_ready")
        rms_ready = sem("rms_ready")
        hrms_ready = sem("hrms_ready")
        eps_set = sem("eps_set")
        dve_step = sem("dve_step")
        h_ready = sem("h_ready")
        hT_psum = sem("hT_psum")
        hT_copied = sem("hT_copied")
        p_ready = sem("p_ready")
        stage_ready = sem("stage_ready")
        sqr_ready = sem("sqr_ready")
        sqr_used = sem("sqr_used")
        normed = sem("normed")
        turn_psum = sem("turn_psum")
        turn_copied = sem("turn_copied")

        n_normed = [sum(x["normed"] for x in items[:i]) for i in range(NI + 1)]
        n_turned = [sum(x["turned"] for x in items[:i]) for i in range(NI + 1)]

        def stores(i):
            n, t = items[i]["n"], items[i]["t"]
            r0, out = t * P, []
            if t == NT - 1:
                w = items[i]["w"]
                out.append((sc["samp"][:, n * 512:n * 512 + w], 0, w))
            if n in (1, 2):
                dst = (sb_prompt[0, 0, r0:r0 + P, n - 1] if t < NT - 1 else sb_sample[0, :, 0, n - 1])
                out.append((dst.rearrange("s h d -> s (h d)"), 0, SBW))
            if n >= 3:
                for half in range(items[i]["w"] // GW):
                    part, g = divmod(2 * (n - 3) + half, NG)
                    if part == 0:
                        continue
                    if t == NT - 1:
                        out.append((win_s[g][0, :, WIN[g] - 1, part - 1].rearrange("s h d -> s (h d)"), half * GW, GW))
                        continue
                    if part == 2:
                        out.append((sc["dv"][r0:r0 + P, g * GW:(g + 1) * GW], half * GW, GW))
                    w0 = r0 - (S - min(WIN[g], S))
                    if w0 >= 0:
                        out.append((win_p[g][0, 0, w0:w0 + P, part - 1].rearrange("s h d -> s (h d)"), half * GW, GW))
            return out

        plan = [stores(i) for i in range(NI)]
        store_value = [16 * sum(len(plan[j]) for j in range(i % NSTAGE, i + 1, NSTAGE)) for i in range(NI)]

        with nc.Block() as block:
            @block.sync
            def _(sp):
                sp.dma_start(ident[:, :], a["ident"]).then_inc(consts_in, 16)
                sp.dma_start(gain[:, :], a["norm1_g"].broadcast_to([P, D])).then_inc(consts_in, 16)
                sp.dma_start(cos[:, :, :], a["cos"]).then_inc(consts_in, 16)
                sp.dma_start(sin[:, :, :], a["sin"]).then_inc(consts_in, 16)
                for j in range(24):
                    src = a["qn_g"] if j < 12 else a["kn_g"]
                    sp.dma_start(qkgain[:, j // 8, (j % 8) * HD:(j % 8 + 1) * HD], src.broadcast_to([P, HD])).then_inc(consts_in, 16)
                for t in range(NT):
                    if t >= 2:
                        sp.wait_ge(h_ready, t - 1)
                    n = rows_of(t)
                    src = a["x_prompt"][0, t * P:t * P + P] if t < NT - 1 else a["x_sample"][:, 0]
                    sp.dma_start(xin[:n, t % 2, :], src).then_inc(x_in[t % 2], 16)

                def load_w(n):
                    w = 512 if n < 7 else 256
                    sp.dma_start(wbuf[:, n % 2, :, :w], w_view[:, :, n * 512:n * 512 + w]).then_inc(w_loaded[n % 2], 16)

                def move_windows(s):
                    for g in range(NG):
                        src = caches[g][0, s].rearrange("w a h d -> (w a h d)")[2 * GW:]
                        dst = win_s[g][0, s].rearrange("w a h d -> (w a h d)")[:(WIN[g] - 1) * 2 * GW]
                        sp.dma_start(dst.rearrange("(p n) -> p n", p=P), src.rearrange("(p n) -> p n", p=P)).then_inc(copies_out, 16)

                load_w(0)
                load_w(1)
                sp.wait_ge(hT_copied, NT)
                sp.dma_start(sc["ht"], hT[:, :, :].rearrange("p c t -> p (c t)")).then_inc(ht_out, 16)
                for i in range(NI):
                    n, t = items[i]["n"], items[i]["t"]
                    if t == 2 and 1 <= n <= 6:
                        load_w(n + 1)
                    if t == 3:
                        move_windows(n)
                    if plan[i]:
                        if items[i]["normed"]:
                            sp.wait_ge(normed, n_normed[i + 1])
                        else:
                            sp.wait_ge(stage_ready, i + 1)
                        m = rows_of(t)
                        for dst, c0, w in plan[i]:
                            sp.dma_start(dst, stage[:m, i % NSTAGE, c0:c0 + w]).then_inc(stored[i % NSTAGE], 16)
                    if t == 1 and 1 <= n <= 6:
                        sp.wait_ge(p_ready, 9 * n)
                for slot in range(NSTAGE):
                    last = max(i for i in range(NI) if i % NSTAGE == slot)
                    sp.wait_ge(stored[slot], store_value[last])
                sp.wait_ge(ht_out, 16)
                sp.wait_ge(copies_out, 16 * NG * NS)

            @block.gpsimd
            def _(pool):
                pool.memset(eps[:, :], EPS).then_inc(eps_set, 1)
                for i in range(NI):
                    if not items[i]["normed"]:
                        continue
                    m = rows_of(items[i]["t"])
                    pool.wait_ge(stage_ready, i + 1)
                    if n_normed[i]:
                        pool.wait_ge(sqr_used, n_normed[i])
                    s_ = stage[:m, i % NSTAGE, :]
                    pool.tensor_tensor(sqr[:m, :], s_, s_, ALU.mult).then_inc(sqr_ready, 1)

            @block.scalar
            def _(act):
                act.wait_ge(consts_in, 28 * 16)
                act.wait_ge(eps_set, 1)
                for t in range(NT + 1):
                    if t < NT:
                        m = rows_of(t)
                        act.wait_ge(x_in[t % 2], 16 * (t // 2 + 1))
                        act.activation(junk[:m, :], xin[:m, t % 2, :], ACT.Square, accum_out=ss[:m, t:t + 1]).then_inc(ss_ready, 1)
                        act.wait_ge(ss_ready, t + 1)
                        act.activation(rms[:m, t:t + 1], ss[:m, t:t + 1], ACT.Sqrt, scale=1.0 / D, bias=eps[:m, :]).then_inc(rms_ready, 1)
                    if t >= 1:
                        u = t - 1
                        m = rows_of(u)
                        act.wait_ge(hT_psum, u + 1)
                        b = 2 * (u % 2)
                        act.activation(hT[:, :, u * P:u * P + m],
                                       pT[:, b:b + 2, :].rearrange("p a (c t) -> p (a c) t", t=P)[:, :, :m],
                                       ACT.Copy).then_inc(hT_copied, 1)
                for i in range(NI + 3):
                    if i < NI:
                        m, w = rows_of(items[i]["t"]), items[i]["w"]
                        act.wait_ge(p_ready, i + 1)
                        if i >= NSTAGE:
                            if store_value[i - NSTAGE]:
                                act.wait_ge(stored[i % NSTAGE], store_value[i - NSTAGE])
                            if n_turned[i - NSTAGE + 1]:
                                act.wait_ge(turn_psum, n_turned[i - NSTAGE + 1])
                            if n_normed[i - NSTAGE + 1]:
                                act.wait_ge(normed, n_normed[i - NSTAGE + 1])
                        scale = HD ** -0.5 if items[i]["n"] == 0 else 1.0
                        act.activation(stage[:m, i % NSTAGE, :w], pP[:m, i % 4, :w], ACT.Copy, scale=scale).then_inc(stage_ready, 1)
                    j = i - 1
                    if 0 <= j < NI and items[j]["normed"]:
                        m = rows_of(items[j]["t"])
                        act.wait_ge(sqr_used, n_normed[j + 1])
                        act.activation(hrms[:m, :], hss[:m, :], ACT.Sqrt, scale=1.0 / HD, bias=eps[:m, :]).then_inc(hrms_ready, 1)
                    j = i - 3
                    if j >= 0 and items[j]["turned"]:
                        n, t = items[j]["n"], items[j]["t"]
                        act.wait_ge(turn_psum, n_turned[j + 1])
                        act.activation(turned[:, TURN_BASE[n]:TURN_BASE[n] + 4, t * P:(t + 1) * P],
                                       pT[:, n_turned[j] % 4, :].rearrange("p (c t) -> p c t", t=P),
                                       ACT.Copy).then_inc(turn_copied, 1)

            @block.vector
            def _(dve):
                steps = [0]

                def chain(ins):
                    steps[0] += 1
                    ins.then_inc(dve_step, 1)
                    dve.wait_ge(dve_step, steps[0])

                dve.wait_ge(consts_in, 28 * 16)
                qg = qkgain[:, :, :].rearrange("p a b -> p (a b)")[:, :12 * HD]
                chain(dve.tensor_scalar(qg, qg, HD ** -0.5, None, ALU.mult))
                for t in range(NT):
                    m = rows_of(t)
                    r = rstd[:m, t:t + 1]
                    dve.wait_ge(rms_ready, t + 1)
                    chain(dve.reciprocal(r, rms[:m, t:t + 1]))
                    if t >= 2:
                        dve.wait_ge(hT_psum, t - 1)
                    dve.scalar_tensor_tensor(h[:m, t % 2, :], xin[:m, t % 2, :], r, gain[:m, :], ALU.mult, ALU.mult).then_inc(h_ready, 1)
                for i in range(NI):
                    if not items[i]["normed"]:
                        continue
                    n, t = items[i]["n"], items[i]["t"]
                    m = rows_of(t)
                    x = stage[:m, i % NSTAGE, :]
                    xh = x.rearrange("p (h d) -> p h d", d=HD)
                    dve.wait_ge(sqr_ready, n_normed[i + 1])
                    dve.tensor_reduce(hss[:m, :], sqr[:m, :].rearrange("p (h d) -> p h d", d=HD), AX_X, ALU.add).then_inc(sqr_used, 1)
                    dve.wait_ge(hrms_ready, n_normed[i + 1])
                    chain(dve.reciprocal(hrs[:m, :], hrms[:m, :]))
                    chain(dve.tensor_tensor(xh, xh, hrs[:m, :].unsqueeze(2).broadcast_to([m, 8, HD]), ALU.mult))
                    chain(dve.tensor_tensor(x, x, qkgain[:m, n - 3, :], ALU.mult))
                    x4 = x.rearrange("p (h a d) -> p h a d", a=2, d=32)
                    A = ropeA[:m, :].rearrange("p (h a d) -> p h a d", a=2, d=32)
                    B = ropeB[:m, :].rearrange("p (h a d) -> p h a d", a=2, d=32)
                    c3 = cos[:m, t, :].unsqueeze(1).broadcast_to([m, 16, 32])
                    s3 = sin[:m, t, :].unsqueeze(1).broadcast_to([m, 8, 32])
                    dve.tensor_tensor(ropeA[:m, :].rearrange("p (h d) -> p h d", d=32), x.rearrange("p (h d) -> p h d", d=32), c3, ALU.mult)
                    dve.tensor_tensor(B[:, :, 0, :], x4[:, :, 1, :], s3, ALU.mult)
                    chain(dve.tensor_tensor(B[:, :, 1, :], x4[:, :, 0, :], s3, ALU.mult))
                    dve.tensor_tensor(x4[:, :, 0, :], A[:, :, 0, :], B[:, :, 0, :], ALU.subtract)
                    dve.tensor_tensor(x4[:, :, 1, :], A[:, :, 1, :], B[:, :, 1, :], ALU.add).then_inc(normed, 1)

            @block.tensor
            def _(pe):
                pe.wait_ge(consts_in, 28 * 16)
                for t in range(NT):
                    m = rows_of(t)
                    pe.wait_ge(h_ready, t + 1)
                    if t >= 2:
                        pe.wait_ge(hT_copied, t - 1)
                    hv = h[:m, t % 2, :].rearrange("p (q c) -> p c q", c=KC)
                    for c in range(KC):
                        last = pe.transpose(pT[:, 2 * (t % 2) + c // 4, (c % 4) * P:(c % 4) * P + m], hv[:, c, :], ident[:m, :m])
                    last.then_inc(hT_psum, 1)
                pe.wait_ge(hT_copied, NT)
                for i in range(NI + 2):
                    if i < NI:
                        n, t, w = items[i]["n"], items[i]["t"], items[i]["w"]
                        m = rows_of(t)
                        if t == 0:
                            pe.wait_ge(w_loaded[n % 2], 16 * (n // 2 + 1))
                        if i >= 4:
                            pe.wait_ge(stage_ready, i - 3)
                        for c in range(KC):
                            last = pe.matmul(pP[:m, i % 4, :w], hT[:, c, t * P:t * P + m], wbuf[:, n % 2, c, :w],
                                             start=(c == 0), stop=(c == KC - 1))
                        last.then_inc(p_ready, 1)
                    j = i - 2
                    if j >= 0 and items[j]["turned"]:
                        if items[j]["normed"]:
                            pe.wait_ge(normed, n_normed[j + 1])
                        else:
                            pe.wait_ge(stage_ready, j + 1)
                        if n_turned[j] >= 4:
                            pe.wait_ge(turn_copied, n_turned[j] - 3)
                        for c in range(4):
                            last = pe.transpose(pT[:, n_turned[j] % 4, c * P:(c + 1) * P],
                                                stage[:, j % NSTAGE, c * P:(c + 1) * P], ident[:, :])
                        last.then_inc(turn_psum, 1)


def phase_sample_stick(nc, a, o, sc, ident, oT):
    HALF = NPAGES // 2
    NKB, NVB, GP = 2, 3, 4
    pool_kv = a["cache_sb_kv"][0].rearrange("n p a h d -> n p a (h d)")
    n_pool = pool_kv.shape[0]
    with ExitStack() as ctx:
        sb = lambda name, shape, dt=F32: ctx.enter_context(nc.sbuf_tensor(name, shape, dt))
        sem = sc["semaphore"]
        pages = sb("pages", [1, NS * NPAGES], I32)
        kbuf = sb("kbuf", [P, NKB, HALF, SBW])
        vbuf = sb("vbuf", [P, NVB, HALF, SBW])
        q = sb("q_rows", [P, 2, SBW])
        prod = sb("prod", [P, GP, SBW])
        bias = sb("bias", [P, SBH])
        ntri = sb("ntri", [P, P])
        nones = sb("nones", [P, P])
        z = sb("z", [P, NPAGES, SBH])
        lo = sb("lo", [P, NPAGES, SBH])
        hi = sb("hi", [P, NPAGES, SBH])
        soft = sb("soft", [P, 2, NPAGES, SBH])
        logit = sb("logit", [P, NPAGES, SBH])
        prob = sb("prob", [P, 2, NPAGES, SBH])
        pC = ctx.enter_context(nc.psum_tensor("pC", [P, 2, 512], F32))
        pO = ctx.enter_context(nc.psum_tensor("pO", [P, 512], F32))

        consts_in = sem("s_consts_in")
        pages_in = sem("s_pages_in")
        q_in = [sem(f"s_q_in{i}") for i in range(2)]
        k_in = [sem(f"s_k_in{i}") for i in range(NKB)]
        v_in = [sem(f"s_v_in{i}") for i in range(NVB)]
        k_used = sem("s_k_used")
        v_used = sem("s_v_used")
        dve_step = sem("s_dve_step")
        lo_ready = sem("s_lo_ready")
        exp_ready = sem("s_exp_ready")
        ln_ready = sem("s_ln_ready")
        soft_ready = sem("s_soft_ready")
        sums_ready = sem("s_sums_ready")
        logit_ready = sem("s_logit_ready")
        prob_ready = sem("s_prob_ready")
        out_copied = sem("s_out_copied")

        with nc.Block() as block:
            @block.sync
            def _(sp):
                sp.dma_start(pages[:, :], a["page_table"].rearrange("s (n a) -> a (s n)", a=1)).then_inc(pages_in, 16)
                sp.dma_start(bias[:, :], a["sb_bias"].broadcast_to([P, SBH])).then_inc(consts_in, 16)
                sp.dma_start(ntri[:, :], a["ntri"]).then_inc(consts_in, 16)
                sp.dma_start(nones[:, :], a["nones"]).then_inc(consts_in, 16)
                sp.wait_ge(pages_in, 16)
                for u in range(2 * NS + 2):
                    if u < 2 * NS:
                        s, half = divmod(u, 2)
                        if half == 0:
                            if s >= 2:
                                sp.wait_ge(k_used, 2 * (s - 1))
                            sp.dma_start(q[:, s % 2, :], sc["samp"][s:s + 1, 0:SBW].broadcast_to([P, SBW])).then_inc(q_in[s % 2], 16)
                        if u >= NKB:
                            sp.wait_ge(k_used, u - NKB + 1)
                        for j in range(HALF):
                            pg = sp.value_load(pages[0:1, u * HALF + j:u * HALF + j + 1], min_val=0, max_val=n_pool - 1)
                            sp.dma_start(kbuf[:, u % NKB, j, :], pool_kv[bass.ds(pg, 1), :, 0, :].rearrange("n p d -> (n p) d")).then_inc(k_in[u % NKB], 16)
                    v = u - 1
                    if 0 <= v < 2 * NS:
                        if v >= NVB:
                            sp.wait_ge(v_used, v - NVB + 1)
                        for j in range(HALF):
                            pg = sp.value_load(pages[0:1, v * HALF + j:v * HALF + j + 1], min_val=0, max_val=n_pool - 1)
                            sp.dma_start(vbuf[:, v % NVB, j, :], pool_kv[bass.ds(pg, 1), :, 1, :].rearrange("n p d -> (n p) d")).then_inc(v_in[v % NVB], 16)

            @block.vector
            def _(dve):
                steps = [0]

                def chain(ins):
                    steps[0] += 1
                    ins.then_inc(dve_step, 1)
                    dve.wait_ge(dve_step, steps[0])

                dve.wait_ge(consts_in, 48)
                b3 = bias[:, :].unsqueeze(1).broadcast_to([P, NPAGES, SBH])
                for s in range(NS):
                    dve.wait_ge(q_in[s % 2], 16 * (s // 2 + 1))
                    for half in range(2):
                        u = 2 * s + half
                        dve.wait_ge(k_in[u % NKB], 16 * HALF * (u // NKB + 1))
                        for c in range(HALF // GP):
                            qb = q[:, s % 2, :].unsqueeze(1).broadcast_to([P, GP, SBW])
                            chain(dve.tensor_tensor(prod[:, :, :], kbuf[:, u % NKB, c * GP:(c + 1) * GP, :], qb, ALU.mult))
                            p0 = half * HALF + c * GP
                            last = dve.tensor_reduce(z[:, p0:p0 + GP, :].rearrange("p a h -> p (a h)"),
                                                     prod[:, :, :].rearrange("p a (h d) -> p (a h) d", d=HD), AX_X, ALU.add)
                            if c < HALF // GP - 1:
                                chain(last)
                        last.then_inc(k_used, 1)
                        dve.wait_ge(k_used, u + 1)
                    chain(dve.tensor_tensor(z[:, :, :], z[:, :, :], b3, ALU.add))
                    dve.tensor_scalar(lo[:, :, :], z[:, :, :], 30.0, None, ALU.min).then_inc(lo_ready, 1)
                    chain(dve.tensor_scalar(hi[:, :, :], z[:, :, :], 30.0, -30.0, ALU.max, ALU.add))
                    dve.wait_ge(ln_ready, s + 1)
                    if s >= 2:
                        dve.wait_ge(sums_ready, s - 1)
                    dve.tensor_tensor(soft[:, s % 2, :, :], lo[:, :, :], hi[:, :, :], ALU.add).then_inc(soft_ready, 1)
                    dve.wait_ge(sums_ready, s + 1)
                    dve.tensor_tensor(logit[:, :, :], pC[:, s % 2, :NPAGES * SBH].rearrange("p (a h) -> p a h", h=SBH),
                                      z[:, :, :], ALU.add).then_inc(logit_ready, 1)
                    dve.wait_ge(logit_ready, s + 1)
                dve.wait_ge(v_used, 2 * NS)
                view = pO[:, :NS * 8].rearrange("p (s c b) -> p b c s", c=4, b=2)
                for b in range(2):
                    dve.tensor_copy(oT[64 * b:64 * b + 64, :, S:T], view[64 * b:64 * b + 64, b, :, :]).then_inc(out_copied, 1)

            @block.scalar
            def _(act):
                for s in range(NS):
                    act.wait_ge(lo_ready, s + 1)
                    act.activation(lo[:, :, :], lo[:, :, :], ACT.Exp).then_inc(exp_ready, 1)
                    act.wait_ge(exp_ready, s + 1)
                    act.activation(lo[:, :, :], lo[:, :, :], ACT.Ln, bias=1.0).then_inc(ln_ready, 1)
                    act.wait_ge(logit_ready, s + 1)
                    if s >= 2:
                        act.wait_ge(v_used, 2 * (s - 1))
                    act.activation(prob[:, s % 2, :, :], logit[:, :, :], ACT.Exp).then_inc(prob_ready, 1)

            @block.tensor
            def _(pe):
                pe.wait_ge(consts_in, 48)
                for s in range(NS + 1):
                    if s < NS:
                        pe.wait_ge(soft_ready, s + 1)
                        if s >= 2:
                            pe.wait_ge(logit_ready, s - 1)
                        out = pC[:, s % 2, :NPAGES * SBH]
                        pe.matmul(out, ntri[:, :], soft[:, s % 2, :, :].rearrange("p a h -> p (a h)"), start=True, stop=True)
                        for p in range(1, NPAGES):
                            last = pe.matmul(out[:, :p * SBH].rearrange("p (a h) -> p a h", h=SBH), nones[:, :],
                                             soft[:, s % 2, p:p + 1, :].broadcast_to([P, p, SBH]),
                                             start=False, stop=True, skip_group_check=True)
                        last.then_inc(sums_ready, 1)
                    r = s - 1
                    if r < 0:
                        continue
                    pe.wait_ge(prob_ready, r + 1)
                    for half in range(2):
                        v = 2 * r + half
                        pe.wait_ge(v_in[v % NVB], 16 * HALF * (v // NVB + 1))
                        for c in range(4):
                            for j in range(HALF):
                                last = pe.matmul(pO[:, (r * 4 + c) * 2:(r * 4 + c) * 2 + 2],
                                                 vbuf[:, v % NVB, j, c * P:(c + 1) * P],
                                                 prob[:, r % 2, half * HALF + j, 2 * c:2 * c + 2],
                                                 start=(half == 0 and c == 0 and j == 0),
                                                 stop=(half == 1 and j == HALF - 1), skip_group_check=True)
                        last.then_inc(v_used, 1)


def phase_prompt_stick(nc, a, o, sc, turned, oT):
    QC = 512
    R = 4
    items = []
    for hp in range(SBH // 2):
        for c in range(S // QC):
            top = (c + 1) * QC // P - 1
            for kb in range(top, -1, -1):
                for par in range(2):
                    off = max(0, kb * P - c * QC)
                    items.append(dict(hp=hp, c=c, kb=kb, par=par, h=2 * hp + par, off=off, first=kb == top,
                                      last=kb == 0, diag=kb * P >= c * QC, prev=min(QC, off + P) if kb * P >= c * QC else 0))
    NI = len(items)
    with ExitStack() as ctx:
        sb = lambda name, shape, dt=F32: ctx.enter_context(nc.sbuf_tensor(name, shape, dt))
        sem = sc["semaphore"]
        v = sb("v_rows", [P, S // P, SBW])
        bias = sb("bias2", [P, SBH])
        bias30 = sb("bias30", [P, SBH])
        ntri = sb("ntri2", [P, P])
        nones = sb("nones2", [P, P])
        before = sb("before", [P, P])
        low = sb("low", [P, R, QC])
        high = sb("high", [P, R, QC])
        soft = sb("soft2", [P, R, QC])
        later = sb("later", [P, 2, 2, QC])
        prob = sb("prob2", [P, R, QC])
        zero = sb("zero", [P, D])
        pZ = ctx.enter_context(nc.psum_tensor("pZ", [P, 6, QC], F32))
        pO = ctx.enter_context(nc.psum_tensor("pO2", [P, 2, QC], F32))

        consts_in = sem("p_consts_in")
        v_in = sem("p_v_in")
        bias30_ready = sem("p_bias30_ready")
        z_ready = sem("p_z_ready")
        low_ready = sem("p_low_ready")
        exp_ready = sem("p_exp_ready")
        high_ready = sem("p_high_ready")
        ln_ready = sem("p_ln_ready")
        pool_step = sem("p_pool_step")
        soft_ready = sem("p_soft_ready")
        later_ready = sem("p_later_ready")
        sums_ready = sem("p_sums_ready")
        prob_ready = sem("p_prob_ready")
        masked = sem("p_masked")
        pv_done = sem("p_pv_done")
        out_copied = sem("p_out_copied")
        zero_set = sem("p_zero_set")
        zero_out = sem("p_zero_out")
        n_diag = [sum(x["diag"] for x in items[:i]) for i in range(NI + 1)]

        with nc.Block() as block:
            @block.sync
            def _(sp):
                sp.dma_start(bias[:, :], a["sb_bias"].broadcast_to([P, SBH])).then_inc(consts_in, 16)
                sp.dma_start(ntri[:, :], a["ntri"]).then_inc(consts_in, 16)
                sp.dma_start(nones[:, :], a["nones"]).then_inc(consts_in, 16)
                sp.dma_start(before[:, :], a["before"]).then_inc(consts_in, 16)
                sp.dma_start(v[:, :, :], o[2][0, 0, :, 1].rearrange("(t p) h d -> p t (h d)", p=P)).then_inc(v_in, 16)
                spare = sc["y"][SURE * BLK:, :].rearrange("(n p a) d -> n p a d", p=P, n=WHOLE * BLK // P)
                sp.wait_ge(zero_set, 1)
                for n in range(spare.shape[0]):
                    sp.dma_start(spare[n], zero[:, :].unsqueeze(1).broadcast_to([P, spare.shape[2], D])).then_inc(zero_out, 16)
                sp.wait_ge(zero_out, 16 * spare.shape[0])

            @block.vector
            def _(dve):
                dve.wait_ge(consts_in, 64)
                dve.tensor_scalar(bias30[:, :], bias[:, :], -30.0, None, ALU.add).then_inc(bias30_ready, 1)
                for i in range(NI + 4):
                    if i < NI:
                        it = items[i]
                        dve.wait_ge(z_ready, i + 1)
                        if i >= R:
                            dve.wait_ge(ln_ready, i - R + 1)
                        dve.tensor_scalar(low[:, i % R, it["off"]:], pZ[:, i % 6, it["off"]:], bias[:, it["h"]:it["h"] + 1], 30.0,
                                          ALU.add, ALU.min).then_inc(low_ready, 1)
                    j = i - 1
                    if 0 <= j < NI:
                        it = items[j]
                        kk = it["kb"] % 2
                        dve.wait_ge(soft_ready, j + 1)
                        if j >= 4:
                            dve.wait_ge(sums_ready, j - 1)
                        dst, old, s_ = later[:, it["par"], kk], later[:, it["par"], 1 - kk], soft[:, j % R]
                        off, prev = it["off"], it["prev"]
                        last = None
                        if prev > off:
                            last = dve.tensor_copy(dst[:, off:prev], s_[:, off:prev])
                        if prev < QC:
                            dve.wait_ge(later_ready, j - 1)
                            last = dve.tensor_tensor(dst[:, prev:], old[:, prev:], s_[:, prev:], ALU.add)
                        last.then_inc(later_ready, 1)
                    j = i - 4
                    if j >= 0 and items[j]["last"] and items[j]["par"]:
                        it = items[j]
                        n = it["hp"] * (S // QC) + it["c"]
                        dve.wait_ge(pv_done, j + 1)
                        dve.tensor_copy(oT[:, it["hp"], it["c"] * QC:(it["c"] + 1) * QC], pO[:, n % 2, :]).then_inc(out_copied, 1)

            @block.gpsimd
            def _(pool):
                steps = [0]
                pool.memset(zero[:, :], 0.0).then_inc(zero_set, 1)
                pool.wait_ge(consts_in, 64)
                for i in range(NI + 2):
                    if i < NI:
                        it = items[i]
                        pool.wait_ge(ln_ready, i + 1)
                        pool.wait_ge(high_ready, i + 1)
                        if i >= R:
                            pool.wait_ge(sums_ready, i - R + 1)
                            pool.wait_ge(later_ready, i - R + 1)
                        off = it["off"]
                        ins = pool.tensor_tensor(soft[:, i % R, off:], low[:, i % R, off:], high[:, i % R, off:], ALU.add)
                        if it["diag"]:
                            steps[0] += 1
                            ins.then_inc(pool_step, 1)
                            pool.wait_ge(pool_step, steps[0])
                            d = soft[:, i % R, off:off + P]
                            ins = pool.tensor_tensor(d, d, before[:, :], ALU.mult)
                        ins.then_inc(soft_ready, 1)
                    j = i - 2
                    if j >= 0 and items[j]["diag"]:
                        pool.wait_ge(prob_ready, j + 1)
                        d = prob[:, j % R, items[j]["off"]:items[j]["off"] + P]
                        pool.tensor_tensor(d, d, before[:, :], ALU.mult).then_inc(masked, 1)

            @block.scalar
            def _(act):
                act.wait_ge(bias30_ready, 1)
                for i in range(NI + 2):
                    if i < NI:
                        it = items[i]
                        off, h = it["off"], it["h"]
                        act.wait_ge(low_ready, i + 1)
                        act.activation(low[:, i % R, off:], low[:, i % R, off:], ACT.Exp).then_inc(exp_ready, 1)
                        if i >= R:
                            act.wait_ge(soft_ready, i - R + 1)
                        act.activation(high[:, i % R, off:], pZ[:, i % 6, off:], ACT.Relu, bias=bias30[:, h:h + 1]).then_inc(high_ready, 1)
                        act.wait_ge(exp_ready, i + 1)
                        act.activation(low[:, i % R, off:], low[:, i % R, off:], ACT.Ln, bias=1.0).then_inc(ln_ready, 1)
                    j = i - 2
                    if j >= 0:
                        it = items[j]
                        off, h = it["off"], it["h"]
                        act.wait_ge(sums_ready, j + 1)
                        if j >= R:
                            act.wait_ge(pv_done, j - R + 1)
                        act.activation(prob[:, j % R, off:], pZ[:, j % 6, off:], ACT.Exp, bias=bias[:, h:h + 1]).then_inc(prob_ready, 1)

            @block.tensor
            def _(pe):
                pe.wait_ge(consts_in, 64)
                pe.wait_ge(v_in, 16)
                for i in range(NI + 4):
                    if i < NI:
                        it = items[i]
                        b = 64 * it["par"]
                        if i >= 6:
                            pe.wait_ge(prob_ready, i - 5)
                        pe.matmul(pZ[:, i % 6, it["off"]:], turned[b:b + 64, 4 + it["hp"], it["kb"] * P:(it["kb"] + 1) * P],
                                  turned[b:b + 64, it["hp"], it["c"] * QC + it["off"]:(it["c"] + 1) * QC],
                                  start=True, stop=True, skip_group_check=True).then_inc(z_ready, 1)
                    j = i - 2
                    if 0 <= j < NI:
                        it = items[j]
                        off, prev = it["off"], it["prev"]
                        pe.wait_ge(soft_ready, j + 1)
                        pe.wait_ge(high_ready, j + 1)
                        last = pe.matmul(pZ[:, j % 6, off:], ntri[:, :], soft[:, j % R, off:], start=False, stop=True, skip_group_check=True)
                        if not it["first"] and prev < QC:
                            pe.wait_ge(later_ready, j - 1)
                            last = pe.matmul(pZ[:, j % 6, prev:], nones[:, :], later[:, it["par"], 1 - it["kb"] % 2, prev:],
                                             start=False, stop=True, skip_group_check=True)
                        last.then_inc(sums_ready, 1)
                    j = i - 4
                    if j >= 0:
                        it = items[j]
                        off, b = it["off"], 64 * it["par"]
                        n = it["hp"] * (S // QC) + it["c"]
                        pe.wait_ge(prob_ready, j + 1)
                        if it["diag"]:
                            pe.wait_ge(masked, n_diag[j + 1])
                        if it["first"] and n >= 2:
                            pe.wait_ge(out_copied, n - 1)
                        pe.matmul(pO[b:b + 64, n % 2, off:], v[:, it["kb"], it["h"] * HD:(it["h"] + 1) * HD], prob[:, j % R, off:],
                                  start=it["first"], stop=it["last"], skip_group_check=True).then_inc(pv_done, 1)


def phase_sample_window(nc, a, o, sc, ident):
    NR = NS * NG * GH
    caches = (a["cache_win0_kv"], a["cache_win1_kv"], a["cache_win2_kv"])
    Q0, K0, V0 = 3 * SBW, 3 * SBW + DW, 3 * SBW + 2 * DW
    with ExitStack() as ctx:
        sb = lambda name, shape, dt=F32: ctx.enter_context(nc.sbuf_tensor(name, shape, dt))
        sem = sc["semaphore"]
        kv = sb("kv_win", [P, NS, NG, 2 * GW])
        q = sb("q_win", [P, NS, DW])
        new = sb("new_rows", [NS, 3 * DW])
        prod = sb("prod_win", [P, 2, GW])
        prodn = sb("prod_new", [NS, DW])
        z = sb("z_win", [P, NR])
        znew = sb("z_new", [NS, NG * GH])
        zt = sb("z_turned", [NR, P + 1])
        mde = sb("mde", [NR, 3])
        nmax = sb("nmax", [NR, 1])
        mden = sb("mden", [NS, NG * GH, 3])
        em = sb("em", [P, NS, NG * GH, NS])
        vnew = sb("v_new_part", [NS, NG, GW])
        packed = sb("packed_win", [NS, NG, GW + 2 * GH])
        pA = ctx.enter_context(nc.psum_tensor("pA_win", [P, 512], F32))
        pB = ctx.enter_context(nc.psum_tensor("pB_win", [P, 512], F32))
        pV = ctx.enter_context(nc.psum_tensor("pV_win", [P, 2, 512], F32))
        q_in = sem("w_q_in")
        new_in = sem("w_new_in")
        kv_in = [sem(f"w_kv_in{g}") for g in range(NG)]
        prod_ready = sem("w_prod_ready")
        z_ready = sem("w_z_ready")
        step = sem("w_step")
        znew_ready = sem("w_znew_ready")
        znew_out = sem("w_znew_out")
        znew_back = sem("w_znew_back")
        zt_psum = sem("w_zt_psum")
        nmax_ready = sem("w_nmax_ready")
        e_ready = sem("w_e_ready")
        mde_ready = sem("w_mde_ready")
        mde_out = sem("w_mde_out")
        mde_back = sem("w_mde_back")
        e_psum = sem("w_e_psum")
        em_zero = sem("w_em_zero")
        em_ready = sem("w_em_ready")
        pv_done = sem("w_pv_done")
        packed_ready = sem("w_packed_ready")
        packed_out = sem("w_packed_out")

        with nc.Block() as block:
            @block.sync
            def _(sp):
                sp.dma_start(new[:, :], sc["samp"][:, Q0:]).then_inc(new_in, 16)
                for s in range(NS):
                    sp.dma_start(q[:, s, :], sc["samp"][s:s + 1, Q0:Q0 + DW].broadcast_to([P, DW])).then_inc(q_in, 16)
                for g in range(NG):
                    for s in range(NS):
                        src = caches[g][0, s].rearrange("(p r) a h d -> p r (a h d)", r=DIL[g])[:, 0, :]
                        sp.dma_start(kv[:, s, g, :], src).then_inc(kv_in[g], 16)
                sp.wait_ge(znew_ready, 1)
                sp.dma_start(sc["znew"], znew[:, :]).then_inc(znew_out, 16)
                sp.wait_ge(znew_out, 16)
                sp.dma_start(zt[:, P:P + 1], sc["znew"].rearrange("s (n a) -> (s n) a", a=1)).then_inc(znew_back, 16)
                sp.wait_ge(mde_ready, 1)
                sp.dma_start(sc["mde"], mde[:, :]).then_inc(mde_out, 16)
                sp.wait_ge(mde_out, 16)
                sp.dma_start(mden[:, :, :], sc["mde"].rearrange("(s n) c -> s n c", s=NS)).then_inc(mde_back, 16)
                sp.wait_ge(packed_ready, 1)
                for g in range(NG):
                    sp.dma_start(sc["od"][g, S:T, :], packed[:, g, :]).then_inc(packed_out, 16)
                sp.wait_ge(packed_out, 16 * NG)

            @block.gpsimd
            def _(pool):
                pool.memset(em[:, :, :, :], 0.0).then_inc(em_zero, 1)

            @block.vector
            def _(dve):
                steps = [0]

                def chain(ins):
                    steps[0] += 1
                    ins.then_inc(step, 1)
                    dve.wait_ge(step, steps[0])

                dve.wait_ge(new_in, 16)
                chain(dve.tensor_tensor(prodn[:, :], new[:, :DW], new[:, DW:2 * DW], ALU.mult))
                dve.tensor_reduce(znew[:, :], prodn[:, :].rearrange("p (n d) -> p n d", d=HD), AX_X, ALU.add).then_inc(znew_ready, 1)
                dve.wait_ge(q_in, 16 * NS)
                k = 0
                for g in range(NG):
                    dve.wait_ge(kv_in[g], 16 * NS)
                    for s in range(NS):
                        dve.tensor_tensor(prod[:, k % 2, :], kv[:, s, g, :GW], q[:, s, g * GW:(g + 1) * GW], ALU.mult).then_inc(prod_ready, 1)
                        dve.wait_ge(prod_ready, k + 1)
                        c = (s * NG + g) * GH
                        dve.tensor_reduce(z[:, c:c + GH], prod[:, k % 2, :].rearrange("p (h d) -> p h d", d=HD), AX_X, ALU.add).then_inc(z_ready, 1)
                        k += 1
                dve.wait_ge(zt_psum, 1)
                chain(dve.tensor_copy(zt[:, :P], pA[:NR, :P]))
                dve.wait_ge(znew_back, 16)
                chain(dve.tensor_reduce(mde[:, 0:1], zt[:, :], AX_X, ALU.max))
                dve.tensor_scalar(nmax[:, :], mde[:, 0:1], -1.0, None, ALU.mult).then_inc(nmax_ready, 1)
                dve.wait_ge(e_ready, 1)
                dve.tensor_copy(mde[:, 2:3], zt[:, P:P + 1]).then_inc(mde_ready, 1)
                dve.wait_ge(e_psum, 1)
                dve.wait_ge(em_zero, 1)
                for s in range(NS):
                    last = dve.tensor_copy(em[:, s, :, s], pB[:, s * 12:(s + 1) * 12])
                last.then_inc(em_ready, 1)
                dve.wait_ge(mde_back, 16)
                w3 = mden[:, :, 2:3].broadcast_to([NS, NG * GH, HD])
                chain(dve.tensor_tensor(vnew[:, :, :].rearrange("p g (h d) -> p (g h) d", d=HD),
                                        new[:, 2 * DW:].rearrange("p (n d) -> p n d", d=HD), w3, ALU.mult))
                dve.wait_ge(pv_done, 1)
                for g in range(NG):
                    dve.tensor_tensor(packed[:, g, :GW], pV[:NS, g // 2, (g % 2) * GW:(g % 2 + 1) * GW], vnew[:, g, :], ALU.add)
                for k in range(2):
                    last = dve.tensor_copy(packed[:, :, GW + k * GH:GW + (k + 1) * GH],
                                           mden[:, :, k].rearrange("p (g h) -> p g h", h=GH))
                last.then_inc(packed_ready, 1)

            @block.scalar
            def _(act):
                act.wait_ge(nmax_ready, 1)
                act.activation(zt[:, :], zt[:, :], ACT.Exp, bias=nmax[:, :], accum_out=mde[:, 1:2]).then_inc(e_ready, 1)

            @block.tensor
            def _(pe):
                pe.wait_ge(z_ready, NS * NG)
                pe.transpose(pA[:NR, :P], z[:, :], ident[:, :]).then_inc(zt_psum, 1)
                pe.wait_ge(e_ready, 1)
                pe.transpose(pB[:, :NR], zt[:, :P], ident[:NR, :NR]).then_inc(e_psum, 1)
                pe.wait_ge(em_ready, 1)
                for g in range(NG):
                    pe.wait_ge(kv_in[g], 16 * NS)
                    for h in range(GH):
                        for s in range(NS):
                            last = pe.matmul(pV[:NS, g // 2, (g % 2) * GW + h * HD:(g % 2) * GW + (h + 1) * HD],
                                             em[:, s, g * GH + h, :], kv[:, s, g, GW + h * HD:GW + (h + 1) * HD],
                                             start=(s == 0), stop=(s == NS - 1))
                last.then_inc(pv_done, 1)


def phase_prompt_window(nc, a, o, sc, ident, turned, odT):
    STEP = [min(d, S // P) for d in DIL]
    items = []
    for g in range(NG):
        for r in range(STEP[g]):
            for b in range(S // STEP[g] // P):
                items.append(dict(g=g, r=r, b=b, nk=2 if b else 1))
    NI = len(items)
    PW = GW + 2 * GH

    def tokens(ap, it, first_block, blocks):
        v = ap.rearrange("p (l r) -> p r l", r=STEP[it["g"]])
        return v[:, it["r"], first_block * P:(first_block + blocks) * P]

    def token_rows(ap, it, block):
        v = ap.rearrange("(l r) n -> r l n", r=STEP[it["g"]])
        return v[it["r"], block * P:(block + 1) * P, :]

    with ExitStack() as ctx:
        sb = lambda name, shape, dt=F32: ctx.enter_context(nc.sbuf_tensor(name, shape, dt))
        sem = sc["semaphore"]
        band = sb("band", [P, 2 * P])
        pairs = sb("pairs", [P, P])
        v = sb("v_win", [P, 3, 2, GW])
        e = sb("e_win", [P, 2, GH, 2 * P])
        nmax = sb("nmax2", [P, 2, GH])
        eT = sb("eT", [P, 2, GH * 2 * P])
        packed = sb("packed", [P, 3, PW])
        comb = sb("comb", [P, 2, NG, PW])
        top = sb("top", [P, GH])
        wg = sb("wg", [P, NG, GH])
        wd = sb("wd", [P, NG, GH])
        den = sb("den", [P, GH])
        part = sb("part", [P, NG, GW])
        mixed = sb("mixed", [P, 2, GW])
        pS = ctx.enter_context(nc.psum_tensor("pS_d", [P, 2, 2, GH // 2, 2 * P], F32))
        pT = ctx.enter_context(nc.psum_tensor("pT_d", [P, GH * 2 * P], F32))
        pO = ctx.enter_context(nc.psum_tensor("pO_d", [P, 2, 512], F32))
        consts_in = sem("d_consts_in")
        v_in = [sem(f"d_v_in{i}") for i in range(3)]
        packed_out = [sem(f"d_packed_out{i}") for i in range(3)]
        comb_in = [sem(f"d_comb_in{i}") for i in range(2)]
        s_ready = sem("d_s_ready")
        s_masked = sem("d_s_masked")
        step = sem("d_step")
        nmax_ready = sem("d_nmax_ready")
        e_ready = sem("d_e_ready")
        eT_psum = sem("d_eT_psum")
        eT_ready = sem("d_eT_ready")
        pv_done = sem("d_pv_done")
        packed_ready = sem("d_packed_ready")
        wg_sub = sem("d_wg_sub")
        wg_ready = sem("d_wg_ready")
        mixed_ready = sem("d_mixed_ready")
        mixed_psum = sem("d_mixed_psum")
        odT_ready = sem("d_odT_ready")
        v_value = [16 * sum(items[j]["nk"] for j in range(i % 3, i + 1, 3)) for i in range(NI)]
        out_value = [16 * (i // 3 + 1) for i in range(NI)]

        with nc.Block() as block:
            @block.sync
            def _(sp):
                sp.dma_start(band[:, :], a["band"]).then_inc(consts_in, 16)
                sp.dma_start(pairs[:, :], a["pairs"]).then_inc(consts_in, 16)
                for i in range(NI + 2):
                    if i < NI:
                        it = items[i]
                        g = it["g"]
                        if i >= 3:
                            sp.wait_ge(pv_done, i - 2)
                        for k in range(it["nk"]):
                            rows = token_rows(sc["dv"][:, g * GW:(g + 1) * GW], it, it["b"] - it["nk"] + 1 + k)
                            sp.dma_start(v[:, i % 3, k, :], rows).then_inc(v_in[i % 3], 16)
                    j = i - 2
                    if j >= 0:
                        it = items[j]
                        sp.wait_ge(packed_ready, j + 1)
                        sp.dma_start(token_rows(sc["od"][it["g"], :S, :], it, it["b"]), packed[:, j % 3, :]).then_inc(packed_out[j % 3], 16)
                for k in range(3):
                    sp.wait_ge(packed_out[k], out_value[max(i for i in range(NI) if i % 3 == k)])
                for t in range(NT):
                    m = rows_of(t)
                    if t >= 2:
                        sp.wait_ge(mixed_ready, t - 1)
                    sp.dma_start(comb[:m, t % 2, :, :], sc["od"][:, t * P:t * P + m, :].rearrange("g t n -> t g n")).then_inc(comb_in[t % 2], 16)

            @block.tensor
            def _(pe):
                for i in range(NI + 2):
                    if i < NI:
                        it = items[i]
                        g, nk = it["g"], it["nk"]
                        if i >= 2:
                            pe.wait_ge(s_masked, i - 1)
                        for h in range(GH):
                            b = 64 * (h % 2)
                            qt = tokens(turned[b:b + 64, 8 + 2 * g + h // 2, :], it, it["b"], 1)
                            kt = tokens(turned[b:b + 64, 14 + 2 * g + h // 2, :], it, it["b"] - nk + 1, nk)
                            last = pe.matmul(pS[:, i % 2, h % 2, h // 2, :nk * P], qt, kt, start=True, stop=True)
                        last.then_inc(s_ready, 1)
                    j = i - 1
                    if 0 <= j < NI:
                        nk = items[j]["nk"]
                        pe.wait_ge(e_ready, j + 1)
                        if j >= 1:
                            pe.wait_ge(eT_ready, j)
                        for h in range(GH):
                            for k in range(nk):
                                last = pe.transpose(pT[:, (h * nk + k) * P:(h * nk + k + 1) * P], e[:, j % 2, h, k * P:(k + 1) * P], ident[:, :])
                        last.then_inc(eT_psum, 1)
                    j = i - 2
                    if j >= 0:
                        nk = items[j]["nk"]
                        pe.wait_ge(eT_ready, j + 1)
                        pe.wait_ge(v_in[j % 3], v_value[j])
                        if j >= 2:
                            pe.wait_ge(packed_ready, j - 1)
                        for h in range(GH):
                            for k in range(nk):
                                last = pe.matmul(pO[:, j % 2, h * HD:(h + 1) * HD], eT[:, j % 2, (h * nk + k) * P:(h * nk + k + 1) * P],
                                                 v[:, j % 3, k, h * HD:(h + 1) * HD], start=(k == 0), stop=(k == nk - 1))
                        last.then_inc(pv_done, 1)
                for t in range(NT):
                    m = rows_of(t)
                    pe.wait_ge(mixed_ready, t + 1)
                    if t >= 2:
                        pe.wait_ge(odT_ready, t - 1)
                    for c in range(2):
                        last = pe.transpose(pO[:, t % 2, c * P:c * P + m], mixed[:m, t % 2, c * P:(c + 1) * P], ident[:m, :m])
                    last.then_inc(mixed_psum, 1)

            @block.scalar
            def _(act):
                for i in range(NI + 1):
                    if i < NI:
                        nk = items[i]["nk"]
                        act.wait_ge(nmax_ready, i + 1)
                        if i >= 3:
                            act.wait_ge(packed_out[i % 3], out_value[i - 3])
                        for h in range(GH):
                            last = act.activation(e[:, i % 2, h, :nk * P], e[:, i % 2, h, :nk * P], ACT.Exp, bias=nmax[:, i % 2, h:h + 1],
                                                  accum_out=packed[:, i % 3, GW + GH + h:GW + GH + h + 1])
                        last.then_inc(e_ready, 1)
                    j = i - 1
                    if j >= 0:
                        nk = items[j]["nk"]
                        act.wait_ge(eT_psum, j + 1)
                        if j >= 2:
                            act.wait_ge(pv_done, j - 1)
                        act.activation(eT[:, j % 2, :GH * nk * P], pT[:, :GH * nk * P], ACT.Copy).then_inc(eT_ready, 1)
                for t in range(NT + 1):
                    if t < NT:
                        m = rows_of(t)
                        act.wait_ge(wg_sub, t + 1)
                        act.activation(wg[:m, :, :], wg[:m, :, :], ACT.Exp).then_inc(wg_ready, 1)
                    if t >= 1:
                        u = t - 1
                        m = rows_of(u)
                        act.wait_ge(mixed_psum, u + 1)
                        act.activation(odT[:, :, u * P:u * P + m], pO[:, u % 2, :2 * P].rearrange("p (c t) -> p c t", c=2)[:, :, :m],
                                       ACT.Copy).then_inc(odT_ready, 1)

            @block.vector
            def _(dve):
                steps = [0]

                def chain(ins):
                    steps[0] += 1
                    ins.then_inc(step, 1)
                    dve.wait_ge(step, steps[0])

                dve.wait_ge(consts_in, 32)
                for i in range(NI + 2):
                    if i < NI:
                        it = items[i]
                        nk = it["nk"]
                        if it["g"] == 2:
                            mask = pairs[:, :]
                        else:
                            mask = band[:, (2 - nk) * P:]
                        dve.wait_ge(s_ready, i + 1)
                        if i >= 2:
                            dve.wait_ge(eT_psum, i - 1)
                        ev = e[:, i % 2, :, :nk * P]
                        dve.tensor_tensor(e[:, i % 2, :, :nk * P].rearrange("p (a b) n -> p b a n", b=2), pS[:, i % 2, :, :, :nk * P],
                                          mask.unsqueeze(1).unsqueeze(1).broadcast_to([P, 2, GH // 2, nk * P]), ALU.add).then_inc(s_masked, 1)
                        dve.wait_ge(s_masked, i + 1)
                        if i >= 3:
                            dve.wait_ge(packed_out[i % 3], out_value[i - 3])
                        chain(dve.tensor_reduce(packed[:, i % 3, GW:GW + GH], ev, AX_X, ALU.max))
                        dve.tensor_scalar(nmax[:, i % 2, :], packed[:, i % 3, GW:GW + GH], -1.0, None, ALU.mult).then_inc(nmax_ready, 1)
                    j = i - 2
                    if j >= 0:
                        dve.wait_ge(pv_done, j + 1)
                        dve.tensor_copy(packed[:, j % 3, :GW], pO[:, j % 2, :GW]).then_inc(packed_ready, 1)
                for t in range(NT):
                    m = rows_of(t)
                    cb = comb[:m, t % 2, :, :]
                    dve.wait_ge(comb_in[t % 2], 16 * (t // 2 + 1))
                    chain(dve.tensor_tensor(top[:m, :], cb[:, 0, GW:GW + GH], cb[:, 1, GW:GW + GH], ALU.max))
                    chain(dve.tensor_tensor(top[:m, :], top[:m, :], cb[:, 2, GW:GW + GH], ALU.max))
                    dve.tensor_tensor(wg[:m, :, :], cb[:, :, GW:GW + GH], top[:m, :].unsqueeze(1).broadcast_to([m, NG, GH]), ALU.subtract).then_inc(wg_sub, 1)
                    dve.wait_ge(wg_ready, t + 1)
                    chain(dve.tensor_tensor(wd[:m, :, :], wg[:m, :, :], cb[:, :, GW + GH:], ALU.mult))
                    chain(dve.tensor_tensor(den[:m, :], wd[:m, 0, :], wd[:m, 1, :], ALU.add))
                    chain(dve.tensor_tensor(den[:m, :], den[:m, :], wd[:m, 2, :], ALU.add))
                    chain(dve.reciprocal(den[:m, :], den[:m, :]))
                    chain(dve.tensor_tensor(wg[:m, :, :], wg[:m, :, :], den[:m, :].unsqueeze(1).broadcast_to([m, NG, GH]), ALU.mult))
                    for g in range(NG):
                        last = dve.tensor_tensor(part[:m, g, :].rearrange("p (h d) -> p h d", d=HD), cb[:, g, :GW].rearrange("p (h d) -> p h d", d=HD),
                                                 wg[:m, g, :].unsqueeze(2).broadcast_to([m, GH, HD]), ALU.mult)
                    chain(last)
                    if t >= 2:
                        dve.wait_ge(mixed_psum, t - 1)
                    chain(dve.tensor_tensor(part[:m, 0, :], part[:m, 0, :], part[:m, 1, :], ALU.add))
                    dve.tensor_tensor(mixed[:m, t % 2, :], part[:m, 0, :], part[:m, 2, :], ALU.add).then_inc(mixed_ready, 1)


def phase_gate(nc, a, o, sc, turned, oT, odT):
    NC = T // 3
    G0 = 3 * SBW + 3 * DW
    flat = turned[:, :, :].rearrange("p a b -> p (a b)")
    hT = flat[:, :KC * T].rearrange("p (c t) -> p c t", c=KC)
    mixT = flat[:, KC * T:2 * KC * T].rearrange("p (c t) -> p c t", c=KC)
    w_view = a["w_in"][0].rearrange("(p c) n -> p c n", c=KC)
    NI = KC * 3
    with ExitStack() as ctx:
        sb = lambda name, shape, dt=F32: ctx.enter_context(nc.sbuf_tensor(name, shape, dt))
        sem = sc["semaphore"]
        wg = sb("w_gates", [P, 2, 2, KC, 2 * P])
        wa = sb("w_a", [P, SBW // P, D])
        wb = sb("w_b", [P, GW // P, D])
        sig = sb("sig", [P, 2, 2, NC])
        half = sb("halves", [P, 2, 2, NC])
        pG = ctx.enter_context(nc.psum_tensor("pG", [P, 2, 4, 512], F32))
        h_in = sem("g_h_in")
        br_in = sem("g_br_in")
        w_loaded = [sem(f"g_w_loaded{i}") for i in range(2)]
        gates_ready = sem("g_gates_ready")
        br_ready = sem("g_br_ready")
        sig_ready = sem("g_sig_ready")
        half_ready = sem("g_half_ready")
        mix_ready = sem("g_mix_ready")
        with nc.Block() as block:
            @block.sync
            def _(sp):
                sp.dma_start(flat[:, :KC * T], sc["ht"]).then_inc(h_in, 16)
                for u in range(KC // 2):
                    if u >= 2:
                        sp.wait_ge(gates_ready, 6 * (u - 1))
                    for k in range(2):
                        c0 = G0 + k * D + u * 2 * P
                        sp.dma_start(wg[:, u % 2, k, :, :], w_view[:, :, c0:c0 + 2 * P]).then_inc(w_loaded[u % 2], 16)
                    if u == 0:
                        sp.dma_start(wa[:, :, :], a["w_br_a"][0].rearrange("(c p) n -> p c n", p=P)).then_inc(br_in, 16)
                        sp.dma_start(wb[:, :, :], a["w_br_b"][0].rearrange("(c p) n -> p c n", p=P)).then_inc(br_in, 16)

            @block.tensor
            def _(pe):
                pe.wait_ge(h_in, 16)
                for i in range(NI):
                    f, n = divmod(i, 3)
                    cols = slice(n * NC, (n + 1) * NC)
                    if n == 0 and f % 2 == 0:
                        pe.wait_ge(w_loaded[f // 2 % 2], 32 * (f // 4 + 1))
                    if i >= 2:
                        pe.wait_ge(half_ready, 2 * (i - 1))
                    for k in range(2):
                        for c in range(KC):
                            last = pe.matmul(pG[:, i % 2, k, :NC], wg[:, f // 2 % 2, k, c, (f % 2) * P:(f % 2 + 1) * P], hT[:, c, cols],
                                             start=(c == 0), stop=(c == KC - 1))
                    last.then_inc(gates_ready, 1)
                    if i == 0:
                        pe.wait_ge(br_in, 32)
                    for k, (w, x, nk) in enumerate(((wa, oT, SBW // P), (wb, odT, GW // P))):
                        for c in range(nk):
                            last = pe.matmul(pG[:, i % 2, 2 + k, :NC], w[:, c, f * P:(f + 1) * P], x[:, c, cols],
                                             start=(c == 0), stop=(c == nk - 1))
                    last.then_inc(br_ready, 1)

            @block.scalar
            def _(act):
                for i in range(NI):
                    act.wait_ge(gates_ready, i + 1)
                    if i >= 2:
                        act.wait_ge(half_ready, 2 * (i - 1))
                    for k in range(2):
                        last = act.activation(sig[:, i % 2, k, :], pG[:, i % 2, k, :NC], ACT.Sigmoid)
                    last.then_inc(sig_ready, 1)

            @block.vector
            def _(dve):
                for i in range(NI):
                    dve.wait_ge(br_ready, i + 1)
                    dve.wait_ge(sig_ready, i + 1)
                    if i >= 2:
                        dve.wait_ge(mix_ready, i - 1)
                    for k in range(2):
                        dve.tensor_tensor(half[:, i % 2, k, :], sig[:, i % 2, k, :], pG[:, i % 2, 2 + k, :NC], ALU.mult).then_inc(half_ready, 1)

            @block.gpsimd
            def _(pool):
                for i in range(NI):
                    f, n = divmod(i, 3)
                    pool.wait_ge(half_ready, 2 * (i + 1))
                    pool.tensor_tensor(mixT[:, f, n * NC:(n + 1) * NC], half[:, i % 2, 0, :], half[:, i % 2, 1, :], ALU.add).then_inc(mix_ready, 1)


def phase_out(nc, a, o, sc, ident, turned, scores):
    flat = turned[:, :, :].rearrange("p a b -> p (a b)")
    h2T = flat[:, :KC * T].rearrange("p (c t) -> p c t", c=KC)
    mixT = flat[:, KC * T:2 * KC * T].rearrange("p (c t) -> p c t", c=KC)
    with ExitStack() as ctx:
        sb = lambda name, shape, dt=F32: ctx.enter_context(nc.sbuf_tensor(name, shape, dt))
        sem = sc["semaphore"]
        wo = sb("w_o", [P, KC, D])
        wr = sb("w_r", [P, KC, E])
        gain = sb("gain2", [P, D])
        x = sb("x_again", [P, 2, D])
        x1 = sb("x1", [P, 2, D])
        h2 = sb("h2", [P, 2, D])
        junk = sb("junk2", [P, D])
        zero = sb("zero_row", [1, D])
        ss = sb("ss2", [P, NT])
        rms = sb("rms2", [P, NT])
        rstd = sb("rstd2", [P, NT])
        eps = sb("eps2", [P, 1])
        pY = ctx.enter_context(nc.psum_tensor("pY", [P, 2, D], F32))
        pT = ctx.enter_context(nc.psum_tensor("pT2", [P, D], F32))
        pR = ctx.enter_context(nc.psum_tensor("pR", [P, 2, 512], F32))
        w_in = sem("o_w_in")
        x_in = [sem(f"o_x_in{i}") for i in range(2)]
        stored = [sem(f"o_stored{i}") for i in range(2)]
        zero_out = sem("o_zero_out")
        set_up = sem("o_set_up")
        step = sem("o_step")
        y_ready = sem("o_y_ready")
        x1_ready = sem("o_x1_ready")
        ss_ready = sem("o_ss_ready")
        rms_ready = sem("o_rms_ready")
        h2_ready = sem("o_h2_ready")
        h2T_psum = sem("o_h2T_psum")
        h2T_ready = sem("o_h2T_ready")
        logits_ready = sem("o_logits_ready")
        scores_ready = sem("o_scores_ready")
        with nc.Block() as block:
            @block.sync
            def _(sp):
                sp.dma_start(wo[:, :, :], a["w_out"][0].rearrange("(c p) n -> p c n", p=P)).then_inc(w_in, 16)
                sp.dma_start(gain[:, :], a["norm2_g"].broadcast_to([P, D])).then_inc(w_in, 16)
                sp.dma_start(wr[:, :, :], a["w_router"][0].rearrange("(p c) n -> p c n", c=KC)).then_inc(w_in, 16)
                sp.wait_ge(set_up, 3)
                sp.dma_start(sc["h2"][T:T + 1, :], zero[:, :]).then_inc(zero_out, 16)
                for t in range(NT + 1):
                    if t < NT:
                        m = rows_of(t)
                        if t >= 2:
                            sp.wait_ge(x1_ready, t - 1)
                        src = a["x_prompt"][0, t * P:t * P + P] if t < NT - 1 else a["x_sample"][:, 0]
                        sp.dma_start(x[:m, t % 2, :], src).then_inc(x_in[t % 2], 16)
                    if t >= 1:
                        u = t - 1
                        m = rows_of(u)
                        sp.wait_ge(h2_ready, u + 1)
                        sp.dma_start(sc["x1"][u * P:u * P + m, :], x1[:m, u % 2, :]).then_inc(stored[u % 2], 16)
                        sp.dma_start(sc["h2"][u * P:u * P + m, :], h2[:m, u % 2, :]).then_inc(stored[u % 2], 16)
                for i in range(2):
                    sp.wait_ge(stored[i], 32 * len(range(i, NT, 2)))
                sp.wait_ge(zero_out, 16)

            @block.gpsimd
            def _(pool):
                pool.memset(eps[:, :], EPS).then_inc(set_up, 1)
                pool.memset(zero[:, :], 0.0).then_inc(set_up, 1)
                pool.memset(scores[:, :, :], 0.5).then_inc(set_up, 1)

            @block.tensor
            def _(pe):
                pe.wait_ge(w_in, 48)
                for t in range(NT + 2):
                    if t < NT:
                        m = rows_of(t)
                        if t >= 2:
                            pe.wait_ge(x1_ready, t - 1)
                        for k in range(2):
                            for c in range(KC):
                                last = pe.matmul(pY[:m, t % 2, k * 512:(k + 1) * 512], mixT[:, c, t * P:t * P + m], wo[:, c, k * 512:(k + 1) * 512],
                                                 start=(c == 0), stop=(c == KC - 1))
                        last.then_inc(y_ready, 1)
                    u = t - 1
                    if 0 <= u < NT:
                        m = rows_of(u)
                        pe.wait_ge(h2_ready, u + 1)
                        if u >= 1:
                            pe.wait_ge(h2T_ready, u)
                        hv = h2[:m, u % 2, :].rearrange("p (q c) -> p c q", c=KC)
                        for c in range(KC):
                            last = pe.transpose(pT[:, c * P:c * P + m], hv[:, c, :], ident[:m, :m])
                        last.then_inc(h2T_psum, 1)
                    u = t - 2
                    if u >= 0:
                        m = rows_of(u)
                        pe.wait_ge(h2T_ready, u + 1)
                        for c in range(KC):
                            last = pe.matmul(pR[:m, u // 8, (u % 8) * E:(u % 8 + 1) * E], h2T[:, c, u * P:u * P + m], wr[:, c, :],
                                             start=(c == 0), stop=(c == KC - 1))
                        last.then_inc(logits_ready, 1)

            @block.scalar
            def _(act):
                act.wait_ge(set_up, 3)
                for t in range(NT + 1):
                    if t < NT:
                        m = rows_of(t)
                        act.wait_ge(x1_ready, t + 1)
                        act.activation(junk[:m, :], x1[:m, t % 2, :], ACT.Square, accum_out=ss[:m, t:t + 1]).then_inc(ss_ready, 1)
                        act.wait_ge(ss_ready, t + 1)
                        act.activation(rms[:m, t:t + 1], ss[:m, t:t + 1], ACT.Sqrt, scale=1.0 / D, bias=eps[:m, :]).then_inc(rms_ready, 1)
                    if t >= 1:
                        u = t - 1
                        m = rows_of(u)
                        act.wait_ge(h2T_psum, u + 1)
                        act.activation(h2T[:, :, u * P:u * P + m], pT[:, :].rearrange("p (c t) -> p c t", t=P)[:, :, :m], ACT.Copy).then_inc(h2T_ready, 1)
                act.wait_ge(logits_ready, NT)
                act.activation(scores[:, :8, :].rearrange("p t e -> p (t e)"), pR[:, 0, :], ACT.Sigmoid).then_inc(scores_ready, 1)
                act.activation(scores[:NS, 8, :], pR[:NS, 1, :E], ACT.Sigmoid).then_inc(scores_ready, 1)

            @block.vector
            def _(dve):
                steps = [0]

                def chain(ins):
                    steps[0] += 1
                    ins.then_inc(step, 1)
                    dve.wait_ge(step, steps[0])

                dve.wait_ge(w_in, 48)
                for t in range(NT):
                    m = rows_of(t)
                    dve.wait_ge(y_ready, t + 1)
                    dve.wait_ge(x_in[t % 2], 16 * (t // 2 + 1))
                    if t >= 2:
                        dve.wait_ge(stored[t % 2], 32 * (t // 2))
                    dve.tensor_tensor(x1[:m, t % 2, :], pY[:m, t % 2, :], x[:m, t % 2, :], ALU.add).then_inc(x1_ready, 1)
                    dve.wait_ge(rms_ready, t + 1)
                    chain(dve.reciprocal(rstd[:m, t:t + 1], rms[:m, t:t + 1]))
                    if t >= 2:
                        dve.wait_ge(h2T_psum, t - 1)
                    dve.scalar_tensor_tensor(h2[:m, t % 2, :], x1[:m, t % 2, :], rstd[:m, t:t + 1], gain[:m, :], ALU.mult, ALU.mult).then_inc(h2_ready, 1)


def phase_shared(nc, a, o, sc, turned):
    NC = T // 3
    NF = DE // P
    h2T = turned[:, :, :].rearrange("p a b -> p (a b)")[:, :KC * T].rearrange("p (c t) -> p c t", c=KC)
    with ExitStack() as ctx:
        sb = lambda name, shape, dt=F32: ctx.enter_context(nc.sbuf_tensor(name, shape, dt))
        sem = sc["semaphore"]
        wgu = sb("ws_gu", [P, 2, KC, DE])
        wd = sb("ws_d", [P, NF, D])
        silu = sb("silu_s", [P, 2, NC])
        hid = sb("hid_s", [P, NF, T])
        x1 = sb("x1_again", [P, 2, D])
        x2 = sb("x2", [P, 2, D])
        pG = ctx.enter_context(nc.psum_tensor("pG_s", [P, 2, 2, 512], F32))
        pY = ctx.enter_context(nc.psum_tensor("pY_s", [P, 2, D], F32))
        w_in = sem("h_w_in")
        x_in = [sem(f"h_x_in{i}") for i in range(2)]
        stored = [sem(f"h_stored{i}") for i in range(2)]
        gu_ready = sem("h_gu_ready")
        silu_ready = sem("h_silu_ready")
        hid_ready = sem("h_hid_ready")
        y_ready = sem("h_y_ready")
        x2_ready = sem("h_x2_ready")
        with nc.Block() as block:
            @block.sync
            def _(sp):
                for k, name in enumerate(("w_s_gate", "w_s_up")):
                    sp.dma_start(wgu[:, k, :, :], a[name][0].rearrange("(p c) f -> p c f", c=KC)).then_inc(w_in, 16)
                sp.dma_start(wd[:, :, :], a["w_s_down"][0].rearrange("(c p) n -> p c n", p=P)).then_inc(w_in, 16)
                for t in range(NT + 1):
                    if t < NT:
                        m = rows_of(t)
                        if t >= 2:
                            sp.wait_ge(x2_ready, t - 1)
                        sp.dma_start(x1[:m, t % 2, :], sc["x1"][t * P:t * P + m, :]).then_inc(x_in[t % 2], 16)
                    if t >= 1:
                        u = t - 1
                        m = rows_of(u)
                        sp.wait_ge(x2_ready, u + 1)
                        sp.dma_start(sc["x2"][u * P:u * P + m, :], x2[:m, u % 2, :]).then_inc(stored[u % 2], 16)
                for i in range(2):
                    sp.wait_ge(stored[i], 16 * len(range(i, NT, 2)))

            @block.tensor
            def _(pe):
                pe.wait_ge(w_in, 48)
                for i in range(3 * NF):
                    n, f = divmod(i, NF)
                    if i >= 2:
                        pe.wait_ge(hid_ready, i - 1)
                    for k in range(2):
                        for c in range(KC):
                            last = pe.matmul(pG[:, i % 2, k, :NC], wgu[:, k, c, f * P:(f + 1) * P], h2T[:, c, n * NC:(n + 1) * NC],
                                             start=(c == 0), stop=(c == KC - 1))
                    last.then_inc(gu_ready, 1)
                pe.wait_ge(hid_ready, 3 * NF)
                for t in range(NT):
                    m = rows_of(t)
                    if t >= 2:
                        pe.wait_ge(x2_ready, t - 1)
                    for k in range(2):
                        for f in range(NF):
                            last = pe.matmul(pY[:m, t % 2, k * 512:(k + 1) * 512], hid[:, f, t * P:t * P + m], wd[:, f, k * 512:(k + 1) * 512],
                                             start=(f == 0), stop=(f == NF - 1))
                    last.then_inc(y_ready, 1)

            @block.scalar
            def _(act):
                for i in range(3 * NF):
                    act.wait_ge(gu_ready, i + 1)
                    if i >= 2:
                        act.wait_ge(hid_ready, i - 1)
                    act.activation(silu[:, i % 2, :], pG[:, i % 2, 0, :NC], ACT.Silu).then_inc(silu_ready, 1)

            @block.vector
            def _(dve):
                for i in range(3 * NF):
                    n, f = divmod(i, NF)
                    dve.wait_ge(silu_ready, i + 1)
                    dve.tensor_tensor(hid[:, f, n * NC:(n + 1) * NC], silu[:, i % 2, :], pG[:, i % 2, 1, :NC], ALU.mult).then_inc(hid_ready, 1)
                for t in range(NT):
                    m = rows_of(t)
                    dve.wait_ge(y_ready, t + 1)
                    dve.wait_ge(x_in[t % 2], 16 * (t // 2 + 1))
                    if t >= 2:
                        dve.wait_ge(stored[t % 2], 16 * (t // 2))
                    dve.tensor_tensor(x2[:m, t % 2, :], pY[:m, t % 2, :], x1[:m, t % 2, :], ALU.add).then_inc(x2_ready, 1)


def phase_route(nc, a, o, sc, ident, scores, dest, weight, expert_row, slot_token, slot_token_tail):
    W = NT * E
    with ExitStack() as ctx:
        sb = lambda name, shape, dt=F32: ctx.enter_context(nc.sbuf_tensor(name, shape, dt))
        sem = sc["semaphore"]
        rbias = sb("rbias", [P, E])
        before = sb("before_r", [P, P])
        ones = sb("ones_r", [P, P])
        earlier = sb("earlier", [P, EG, EG])
        valid = sb("valid", [P, NT])
        number = sb("number", [P, 1])
        tokid = sb("tokid", [P, NT], I32)
        sel = sb("sel", [P, NT, E])
        tops = sb("tops", [P, NT * EG, 8])
        grp = sb("grp", [P, NT, EG])
        gt = sb("gt", [P, NT, EG, EG])
        eq = sb("eq", [P, NT, EG, EG])
        rank = sb("rank", [P, NT, EG])
        gpen = sb("gpen", [P, NT, EG])
        best = sb("best", [P, NT, 8])
        marked = sb("marked", [P, NT, E])
        mask = sb("mask", [P, NT, E])
        w = sb("w_r8", [P, NT, E])
        wsum = sb("wsum", [P, NT])
        cum = sb("cum", [P, NT + 1, E])
        count = sb("count", [P, E])
        nblk = sb("nblk", [P, E])
        end = sb("end", [P, E])
        begin = sb("begin", [P, E])
        slot = sb("slot", [P, NT, E])
        d8 = sb("d8", [P, NT, 8])
        hit = sb("hit", [P, E])
        picked = sb("picked", [P, NT * TOPK, E])
        eb = sb("eb", [P, 2])
        ebi = sb("ebi", [P, 1], I32)
        turn_first = sb("turn_first", [P, NBLK // TURN])
        turn_used = sb("turn_used", [P, NBLK // TURN])
        turns = sb("turns", [P, 1])
        turnsi = sb("turnsi", [P, 1], I32)
        fill = sb("fill", [NBLK, BLK], I32)
        table = sb("table", [NBLK, BLK], I32)
        tablef = sb("tablef", [NBLK, BLK])
        pP = ctx.enter_context(nc.psum_tensor("pP_r", [P, 2, 512], F32))
        pC = ctx.enter_context(nc.psum_tensor("pC_r", [P, 512], F32))
        pT = ctx.enter_context(nc.psum_tensor("pT_r", [P, 512], F32))
        consts_in = sem("r_consts_in")
        fill_set = sem("r_fill_set")
        fill_out = sem("r_fill_out")
        step = sem("r_step")
        mask_ready = sem("r_mask_ready")
        cum_ready = sem("r_cum_ready")
        pos_ready = sem("r_pos_ready")
        dest_ready = sem("r_dest_ready")
        scattered = sem("r_scattered")
        eb_ready = sem("r_eb_ready")
        eb_out = sem("r_eb_out")
        eb_back = sem("r_eb_back")
        table_in = sem("r_table_in")
        tablef_ready = sem("r_tablef_ready")
        table_psum = sem("r_table_psum")
        slots_ready = sem("r_slots_ready")
        with nc.Block() as block:
            @block.sync
            def _(sp):
                for dst, src in ((before[:, :], a["before"]), (ones[:, :], a["ones"]), (earlier[:, :, :], a["earlier"]),
                                 (valid[:, :], a["valid"]), (number[:, :], a["number"]), (tokid[:, :], a["tokid"]), (turn_first[:, :], a["turn_first"]),
                                 (rbias[:, :], a["router_bias"].broadcast_to([P, E]))):
                    sp.dma_start(dst, src).then_inc(consts_in, 16)
                sp.wait_ge(fill_set, 1)
                sp.dma_start(sc["table"].rearrange("(b p) a -> b (p a)", b=NBLK), fill[:, :]).then_inc(fill_out, 16)
                sp.wait_ge(eb_ready, 2)
                sp.dma_start(sc["eb"][:, :NBLK].rearrange("a n -> n a"), ebi[:NBLK, :], allow_slow_non_contiguous=True).then_inc(eb_out, 16)
                sp.dma_start(sc["eb"][:, NBLK:], turnsi[0:1, :]).then_inc(eb_out, 16)
                sp.wait_ge(eb_out, 32)
                sp.dma_start(expert_row[:, :], sc["eb"]).then_inc(eb_back, 16)
                sp.wait_ge(scattered, 16 * NT * TOPK)
                sp.dma_start(table[:, :], sc["table"].rearrange("(b p) a -> b (p a)", b=NBLK)).then_inc(table_in, 16)
                sp.wait_ge(eb_back, 16)

            @block.gpsimd
            def _(pool):
                pool.memset(fill[:, :], T).then_inc(fill_set, 1)
                pool.wait_ge(consts_in, 8 * 16)
                pool.wait_ge(fill_out, 16)
                pool.wait_ge(dest_ready, 1)
                for t in range(NT):
                    m = rows_of(t)
                    for k in range(TOPK):
                        pool.indirect_dma_start(sc["table"], bass.IndirectOffsetOnAxis(ap=dest[:m, t * 8 + k:t * 8 + k + 1], axis=0),
                                                tokid[:m, t:t + 1], None).then_inc(scattered, 16)

            @block.tensor
            def _(pe):
                pe.wait_ge(consts_in, 8 * 16)
                pe.wait_ge(cum_ready, 1)
                for t in range(NT):
                    out = pP[:, t // 8, (t % 8) * E:(t % 8 + 1) * E]
                    pe.matmul(out, before[:, :], mask[:, t, :], start=True, stop=False)
                    last = pe.matmul(out, ones[:, :], cum[:, t, :], start=False, stop=True)
                last = pe.matmul(pC[:, :E], ones[:, :], cum[:, NT, :], start=True, stop=True)
                last.then_inc(pos_ready, 1)
                pe.wait_ge(tablef_ready, 1)
                pe.transpose(pT[:, :NBLK], tablef[:, :P], ident[:NBLK, :NBLK])
                pe.transpose(pT[:BLK - P, P:P + NBLK], tablef[:, P:], ident[:NBLK, :NBLK]).then_inc(table_psum, 1)

            @block.vector
            def _(dve):
                steps = [0]

                def chain(ins):
                    steps[0] += 1
                    ins.then_inc(step, 1)
                    dve.wait_ge(step, steps[0])

                dve.wait_ge(consts_in, 8 * 16)
                bc = lambda ap, shape: ap.broadcast_to(shape)
                chain(dve.tensor_tensor(sel[:, :, :], scores[:, :, :], bc(rbias[:, :].unsqueeze(1), [P, NT, E]), ALU.add))
                for j in range(NT * EG):
                    last = dve.max(tops[:, j, :], sel[:, j // EG, (j % EG) * PER:(j % EG + 1) * PER])
                chain(last)
                chain(dve.tensor_tensor(grp[:, :, :].rearrange("p t g -> p (t g)"), tops[:, :, 0], tops[:, :, 1], ALU.add))
                for t in range(NT):
                    this, other = bc(grp[:, t, :].unsqueeze(2), [P, EG, EG]), bc(grp[:, t, :].unsqueeze(1), [P, EG, EG])
                    dve.tensor_tensor(gt[:, t, :, :], other, this, ALU.is_gt)
                    last = dve.tensor_tensor(eq[:, t, :, :], other, this, ALU.is_equal)
                chain(last)
                chain(dve.tensor_tensor(eq[:, :, :, :], eq[:, :, :, :], bc(earlier[:, :, :].unsqueeze(1), [P, NT, EG, EG]), ALU.mult))
                chain(dve.tensor_tensor(gt[:, :, :, :], gt[:, :, :, :], eq[:, :, :, :], ALU.add))
                chain(dve.tensor_reduce(rank[:, :, :].rearrange("p t g -> p (t g)"), gt[:, :, :, :].rearrange("p t g h -> p (t g) h"), AX_X, ALU.add))
                chain(dve.tensor_scalar(rank[:, :, :], rank[:, :, :], float(TOPG), None, ALU.is_lt))
                chain(dve.tensor_scalar(gpen[:, :, :], rank[:, :, :], BIG, -BIG, ALU.mult, ALU.add))
                s4 = sel[:, :, :].rearrange("p t (g e) -> p (t g) e", e=PER)
                r4 = bc(rank[:, :, :].rearrange("p t g -> p (t g)").unsqueeze(2), [P, NT * EG, PER])
                g4 = bc(gpen[:, :, :].rearrange("p t g -> p (t g)").unsqueeze(2), [P, NT * EG, PER])
                chain(dve.tensor_tensor(s4, s4, r4, ALU.mult))
                chain(dve.tensor_tensor(s4, s4, g4, ALU.add))
                for t in range(NT):
                    last = dve.max(best[:, t, :], sel[:, t, :])
                chain(last)
                for t in range(NT):
                    last = dve.match_replace(marked[:, t, :], best[:, t, :], sel[:, t, :], BIG)
                chain(last)
                chain(dve.tensor_scalar(mask[:, :, :], marked[:, :, :], 0.5 * BIG, None, ALU.is_ge))
                chain(dve.tensor_tensor(mask[:, :, :], mask[:, :, :], bc(valid[:, :].unsqueeze(2), [P, NT, E]), ALU.mult))
                chain(dve.tensor_tensor(w[:, :, :], scores[:, :, :], mask[:, :, :], ALU.mult))
                chain(dve.tensor_reduce(wsum[:, :], w[:, :, :], AX_X, ALU.add))
                chain(dve.scalar_tensor_tensor(wsum[:, :], wsum[:, :], 1.0, valid[:, :], ALU.add, ALU.subtract))
                chain(dve.reciprocal(wsum[:, :], wsum[:, :]))
                chain(dve.tensor_tensor(w[:, :, :], w[:, :, :], bc(wsum[:, :].unsqueeze(2), [P, NT, E]), ALU.mult))
                chain(dve.tensor_scalar(w[:, :, :], w[:, :, :], 2.5, None, ALU.mult))
                chain(dve.memset(cum[:, 0, :], 0.0))
                for t in range(NT):
                    ins = dve.tensor_tensor(cum[:, t + 1, :], cum[:, t, :], mask[:, t, :], ALU.add)
                    if t < NT - 1:
                        chain(ins)
                ins.then_inc(cum_ready, 1)
                dve.wait_ge(pos_ready, 1)
                chain(dve.tensor_copy(count[:, :], pC[:, :E]))
                chain(dve.memset(nblk[:, :], 0.0))
                for j in range(-(-T // BLK)):
                    chain(dve.scalar_tensor_tensor(nblk[:, :], count[:, :], float(j * BLK), nblk[:, :], ALU.is_gt, ALU.add))
                chain(dve.tensor_tensor_scan(end[:, :], ones[:, :E], nblk[:, :], 0.0, ALU.mult, ALU.add))
                chain(dve.tensor_scalar(hit[:, :], end[:, :], number[:, 0:1], None, ALU.is_le))
                chain(dve.tensor_reduce(eb[:, 0:1], hit[:, :], AX_X, ALU.add))
                chain(dve.tensor_scalar(eb[:, 1:2], eb[:, 0:1], float(E - 1), None, ALU.min))
                chain(dve.tensor_scalar(turn_used[:, :], turn_first[:, :], end[:, E - 1:E], None, ALU.is_lt))
                chain(dve.tensor_reduce(turns[:, :], turn_used[:, :], AX_X, ALU.add))
                dve.tensor_copy(ebi[:, :], eb[:, 1:2]).then_inc(eb_ready, 1)
                dve.tensor_scalar(turnsi[:, :], turns[:, :], -2.0, None, ALU.add).then_inc(eb_ready, 1)
                chain(dve.tensor_tensor(begin[:, :], end[:, :], nblk[:, :], ALU.subtract))
                chain(dve.tensor_scalar(begin[:, :], begin[:, :], float(BLK), 1.0, ALU.mult, ALU.add))
                chain(dve.tensor_tensor(slot[:, :8, :], pP[:, 0, :].rearrange("p (t e) -> p t e", e=E), bc(begin[:, :].unsqueeze(1), [P, 8, E]), ALU.add))
                chain(dve.tensor_tensor(slot[:, 8, :], pP[:, 1, :E], begin[:, :], ALU.add))
                chain(dve.tensor_tensor(slot[:, :, :], slot[:, :, :], mask[:, :, :], ALU.mult))
                for t in range(NT):
                    last = dve.max(d8[:, t, :], slot[:, t, :])
                chain(last)
                dve.tensor_scalar(dest[:, :], d8[:, :, :].rearrange("p t k -> p (t k)"), -1.0, None, ALU.add).then_inc(dest_ready, 1)
                for t in range(NT):
                    for k in range(TOPK):
                        j = t * TOPK + k
                        dve.scalar_tensor_tensor(picked[:, j, :], slot[:, t, :], d8[:, t, k:k + 1], w[:, t, :], ALU.is_equal, ALU.mult,
                                                 accum_out=weight[:, j:j + 1])
                dve.wait_ge(table_in, 16)
                dve.tensor_copy(tablef[:, :], table[:, :]).then_inc(tablef_ready, 1)
                dve.wait_ge(table_psum, 1)
                dve.tensor_copy(slot_token[:, :], pT[:, :NBLK]).then_inc(slots_ready, 1)
                dve.tensor_copy(slot_token_tail[:, :], pT[:BLK - P, P:P + NBLK]).then_inc(slots_ready, 1)
                dve.wait_ge(slots_ready, 2)


def phase_experts(nc, a, o, sc, ident, expert_row, slot_token, slot_token_tail):
    U = TURN
    NF = DE // P
    TAIL = BLK - P
    SKIP = P - TAIL
    CH = (3, 3, 2)
    C0 = (0, 3, 6)
    w_views = [a[n][0].rearrange("e (p c) f -> e p (c f)", p=P) for n in ("w_e_gate", "w_e_up", "w_e_down")]
    with ExitStack() as ctx:
        sb = lambda name, shape, dt=F32: ctx.enter_context(nc.sbuf_tensor(name, shape, dt))
        sem = sc["semaphore"]
        w = sb("w_e", [P, 2, 3, KC * DE])
        whi = sb("w_e_hi", [P, 2, NF * D], F32R)
        wlo = sb("w_e_lo", [P, 2, NF * D], F32R)
        index = sb("index", [P, 2, 2], I32)
        rows = sb("rows", [P, 2, D])
        tail = sb("rows_tail", [TAIL, 2, D])
        xT = sb("xT", [P, 2, KC, BLK])
        silu = sb("silu_e", [P, NF, BLK])
        hid = sb("hid_e", [P, NF, BLK])
        hhi = sb("hid_hi", [P, 2, NF, BLK], F32R)
        hlo = sb("hid_lo", [P, 2, NF, BLK], F32R)
        y = sb("y_e", [P, 2, D])
        pX = ctx.enter_context(nc.psum_tensor("pX", [P, 2, 512], F32))
        pG = ctx.enter_context(nc.psum_tensor("pG_e", [P, 2, 512], F32))
        pY = ctx.enter_context(nc.psum_tensor("pY_e", [P, 2, D], F32))
        w_in = [[sem(f"e_w_in{k}{i}") for i in range(2)] for k in range(3)]
        rows_in = [sem(f"e_rows_in{i}") for i in range(2)]
        y_out = sem("e_y_out")
        index_ready = sem("e_index_ready")
        x_psum = sem("e_x_psum")
        xT_ready = sem("e_xT_ready")
        whi_ready = sem("e_whi_ready")
        wlo_ready = sem("e_wlo_ready")
        gu_ready = sem("e_gu_ready")
        silu_ready = sem("e_silu_ready")
        hid_ready = sem("e_hid_ready")
        hhi_ready = sem("e_hhi_ready")
        hlo_ready = sem("e_hlo_ready")
        y_ready = sem("e_y_ready")
        y_copied = sem("e_y_copied")

        def seen(it, j, back):
            return not isinstance(it, int) or it * U + j >= back

        with nc.Block() as block:
            def load_last(eng):
                assert T * TOPK > 2 * U * BLK
                return eng.value_load(expert_row[0:1, NBLK:NBLK + 1], min_val=1, max_val=NBLK // U - 2) + 1

            @block.sync
            def _(sp):
                def body(it):
                    for j in range(U):
                        r = j % 2
                        e = sp.value_load(expert_row[0:1, bass.ds(it * U + j, 1)], min_val=0, max_val=E - 1)
                        for k in range(3):
                            if seen(it, j, 2):
                                sp.wait_ge(wlo_ready if k == 2 else gu_ready, it * U + (j - 1))
                            sp.dma_start(w[:, r, k, :], w_views[k][bass.ds(e, 1)].rearrange("e p n -> (e p) n")).then_inc(w_in[k][r], 16)
                body(0)
                with sp.Fori(1, load_last(sp) + 1) as it:
                    body(it)

            @block.gpsimd
            def _(pool):
                def body(it):
                    for j in range(U):
                        r = j % 2
                        if seen(it, j, 2):
                            pool.wait_ge(x_psum, it * (3 * U) + 3 * (j - 1))
                        pool.tensor_copy(index[:, r, 0:1], slot_token[:, bass.ds(it * U + j, 1)]).then_inc(index_ready, 1)
                        pool.tensor_copy(index[:TAIL, r, 1:2], slot_token_tail[:, bass.ds(it * U + j, 1)]).then_inc(index_ready, 1)
                        pool.wait_ge(index_ready, it * (2 * U) + 2 * (j + 1))
                        pool.nop(nofuse=True)
                        pool.indirect_dma_start(rows[:, r, :], None, sc["h2"], bass.IndirectOffsetOnAxis(ap=index[:, r, 0:1], axis=0)).then_inc(rows_in[r], 16)
                        pool.indirect_dma_start(tail[:, r, :], None, sc["h2"], bass.IndirectOffsetOnAxis(ap=index[:TAIL, r, 1:2], axis=0)).then_inc(rows_in[r], 16)
                body(0)
                with pool.Fori(1, load_last(pool) + 1) as it:
                    body(it)

            @block.tensor
            def _(pe):
                def turn_rows(it, j, q):
                    r = j % 2
                    if q == 0:
                        pe.wait_ge(rows_in[r], it * (U * 16) + 32 * (j // 2 + 1))
                    if seen(it, j, 1) or q == 2:
                        pe.wait_ge(xT_ready, it * (3 * U) + (3 * j + q - 1))
                    for c in range(CH[q]):
                        for src, t0, n in ((rows, 0, P), (tail, P, TAIL)):
                            v = src[:, r, :].rearrange("p (q c) -> p c q", c=KC)
                            last = pe.transpose(pX[:, (3 * r + q) % 2, c * BLK + t0:c * BLK + t0 + n], v[:, C0[q] + c, :], ident[:n, :n])
                    last.then_inc(x_psum, 1)

                def gate_up(it, j, turn_next):
                    r = j % 2
                    pe.wait_ge(xT_ready, it * (3 * U) + (3 * j + 3))
                    if seen(it, j, 1):
                        pe.wait_ge(hid_ready, it * U + j)
                    for k in range(2):
                        pe.wait_ge(w_in[k][r], it * (U * 8) + 16 * (j // 2 + 1))
                        for f in range(NF):
                            wv = w[:, r, k, :].rearrange("p (c q f) -> p c f q", c=KC, f=NF)
                            for c in range(KC):
                                last = pe.matmul(pG[:, k, f * BLK:(f + 1) * BLK], wv[:, c, f, :], xT[:, r, c, :], start=(c == 0), stop=(c == KC - 1))
                            if k == 1 and f == NF - 1:
                                last.then_inc(gu_ready, 1)
                            elif turn_next:
                                turn_rows(it, j + 1, 2 * k + f)

                def down(it, j):
                    r = j % 2
                    pe.wait_ge(hlo_ready, it * U + (j + 1))
                    pe.wait_ge(wlo_ready, it * U + (j + 1))
                    if seen(it, j, 1):
                        pe.wait_ge(y_copied, it * (2 * U) + 2 * j)
                    for s in range(2):
                        for h in range(2):
                            n = 0
                            for ht, wt in ((hhi, whi), (hhi, wlo), (hlo, whi)):
                                for f in range(NF):
                                    last = pe.matmul(pY[:, s, h * 512:(h + 1) * 512], ht[:, r, f, s * TAIL:s * TAIL + P],
                                                     wt[:, r, f * D + h * 512:f * D + (h + 1) * 512], start=(n == 0), stop=(n == 3 * NF - 1))
                                    n += 1
                    last.then_inc(y_ready, 1)

                def body(it, which):
                    for j in range(U):
                        gate_up(it, j, which != "last" or j < U - 1)
                        if which != "first" or j > 0:
                            down(it, j - 1)
                for q in range(3):
                    turn_rows(0, 0, q)
                body(0, "first")
                last = load_last(pe)
                with pe.Fori(1, last) as it:
                    body(it, "middle")
                body(last, "last")
                down(last, U - 1)

            @block.scalar
            def _(act):
                def w_high(it, j):
                    r = j % 2
                    act.wait_ge(w_in[2][r], it * (U * 8) + 16 * (j // 2 + 1))
                    if seen(it, j, 2):
                        act.wait_ge(y_ready, it * U + (j - 1))
                    act.activation(whi[:, r, :], w[:, r, 2, :], ACT.Copy).then_inc(whi_ready, 1)

                def gate(it, j):
                    r = j % 2
                    act.wait_ge(gu_ready, it * U + (j + 1))
                    act.activation(silu[:, :, :].rearrange("p f t -> p (f t)"), pG[:, 0, :NF * BLK], ACT.Silu).then_inc(silu_ready, 1)

                def hid_high(it, j):
                    r = j % 2
                    act.wait_ge(hid_ready, it * U + (j + 1))
                    if seen(it, j, 2):
                        act.wait_ge(y_ready, it * U + (j - 1))
                    act.activation(hhi[:, r, :, :], hid[:, :, :], ACT.Copy).then_inc(hhi_ready, 1)

                def put(it, j):
                    act.wait_ge(y_ready, it * U + (j + 1))
                    if seen(it, j, 1):
                        act.wait_ge(y_out, it * (U * 32) + 32 * j)
                    act.activation(y[:, 0, :], pY[:, 0, :], ACT.Copy).then_inc(y_copied, 1)
                    act.activation(y[SKIP:, 1, :], pY[SKIP:, 1, :], ACT.Copy).then_inc(y_copied, 1)
                    act.wait_ge(y_copied, it * (2 * U) + 2 * (j + 1))
                    act.dma_start(sc["y"][bass.ds(it * (U * BLK) + j * BLK, P), :], y[:, 0, :]).then_inc(y_out, 16)
                    act.dma_start(sc["y"][bass.ds(it * (U * BLK) + (j * BLK + P), TAIL), :], y[SKIP:, 1, :]).then_inc(y_out, 16)

                def body(it, which):
                    for j in range(U):
                        w_high(it, j)
                        gate(it, j)
                        hid_high(it, j)
                        if which != "first" or j > 0:
                            put(it, j - 1)
                body(0, "first")
                last = load_last(act)
                with act.Fori(1, last + 1) as it:
                    body(it, "middle")
                put(last, U - 1)
                act.wait_ge(y_out, last * (U * 32) + U * 32)
                act.nop(nofuse=True)

            @block.vector
            def _(dve):
                def take_rows(it, j, q):
                    r = j % 2
                    dve.wait_ge(x_psum, it * (3 * U) + (3 * j + q + 1))
                    if seen(it, j, 2):
                        dve.wait_ge(gu_ready, it * U + (j - 1))
                    dve.tensor_copy(xT[:, r, C0[q]:C0[q] + CH[q], :],
                                    pX[:, (3 * r + q) % 2, :CH[q] * BLK].rearrange("p (c t) -> p c t", t=BLK)).then_inc(xT_ready, 1)

                def w_low(it, j):
                    r = j % 2
                    dve.wait_ge(whi_ready, it * U + (j + 1))
                    if seen(it, j, 2):
                        dve.wait_ge(y_ready, it * U + (j - 1))
                    dve.tensor_tensor(wlo[:, r, :], w[:, r, 2, :], whi[:, r, :].bitcast(F32), ALU.subtract).then_inc(wlo_ready, 1)

                def gate(it, j):
                    r = j % 2
                    dve.wait_ge(silu_ready, it * U + (j + 1))
                    if seen(it, j, 1):
                        dve.wait_ge(hlo_ready, it * U + j)
                    dve.tensor_tensor(hid[:, :, :].rearrange("p f t -> p (f t)"), silu[:, :, :].rearrange("p f t -> p (f t)"),
                                      pG[:, 1, :NF * BLK], ALU.mult).then_inc(hid_ready, 1)
                    dve.wait_ge(hhi_ready, it * U + (j + 1))
                    if seen(it, j, 2):
                        dve.wait_ge(y_ready, it * U + (j - 1))
                    dve.tensor_tensor(hlo[:, r, :, :], hid[:, :, :], hhi[:, r, :, :].bitcast(F32), ALU.subtract).then_inc(hlo_ready, 1)

                def body(it, which):
                    for j in range(U):
                        ahead = which != "last" or j < U - 1
                        if ahead:
                            take_rows(it, j + 1, 0)
                        w_low(it, j)
                        if ahead:
                            take_rows(it, j + 1, 1)
                            take_rows(it, j + 1, 2)
                        gate(it, j)
                for q in range(3):
                    take_rows(0, 0, q)
                body(0, "first")
                last = load_last(dve)
                with dve.Fori(1, last) as it:
                    body(it, "middle")
                body(last, "last")


def phase_combine(nc, a, o, sc, dest, weight):
    R = 8
    with ExitStack() as ctx:
        sb = lambda name, shape, dt=F32: ctx.enter_context(nc.sbuf_tensor(name, shape, dt))
        sem = sc["semaphore"]
        part = sb("part_y", [P, R, D])
        acc = sb("acc_y", [P, 2, D])
        acc_in = [sem(f"c_acc_in{i}") for i in range(2)]
        part_in = [sem(f"c_part_in{i}") for i in range(R)]
        out_stored = [sem(f"c_out_stored{i}") for i in range(2)]
        added = sem("c_added")
        with nc.Block() as block:
            @block.sync
            def _(sp):
                for t in range(NT + 1):
                    if t < NT:
                        m = rows_of(t)
                        if t >= 2:
                            sp.wait_ge(out_stored[t % 2], 16 * (t // 2))
                        sp.dma_start(acc[:m, t % 2, :], sc["x2"][t * P:t * P + m, :]).then_inc(acc_in[t % 2], 16)
                    if t >= 1:
                        u = t - 1
                        m = rows_of(u)
                        sp.wait_ge(added, TOPK * (u + 1))
                        dst = o[0][0, u * P:u * P + P] if u < NT - 1 else o[1][:, 0]
                        sp.dma_start(dst, acc[:m, u % 2, :]).then_inc(out_stored[u % 2], 16)
                for i in range(2):
                    sp.wait_ge(out_stored[i], 16 * len(range(i, NT, 2)))

            @block.gpsimd
            def _(pool):
                for t in range(NT):
                    m = rows_of(t)
                    for k in range(TOPK):
                        n = t * TOPK + k
                        if n >= R:
                            pool.wait_ge(added, n - R + 1)
                        pool.indirect_dma_start(part[:m, n % R, :], None, sc["y"],
                                                bass.IndirectOffsetOnAxis(ap=dest[:m, n:n + 1], axis=0)).then_inc(part_in[n % R], 16)

            @block.vector
            def _(dve):
                for t in range(NT):
                    m = rows_of(t)
                    dve.wait_ge(acc_in[t % 2], 16 * (t // 2 + 1))
                    for k in range(TOPK):
                        n = t * TOPK + k
                        dve.wait_ge(part_in[n % R], 16 * (n // R + 1))
                        dve.scalar_tensor_tensor(acc[:m, t % 2, :], part[:m, n % R, :], weight[:m, n:n + 1], acc[:m, t % 2, :],
                                                 ALU.mult, ALU.add).then_inc(added, 1)
                        dve.wait_ge(added, n + 1)


_INS = ['x_prompt', 'x_sample', 'cache_sb_kv', 'page_table', 'cache_win0_kv', 'cache_win1_kv', 'cache_win2_kv',
        'norm1_g', 'w_in', 'qn_g', 'kn_g', 'sb_bias', 'w_br_a', 'w_br_b', 'w_out', 'norm2_g', 'w_router', 'router_bias',
        'w_e_gate', 'w_e_up', 'w_e_down', 'w_s_gate', 'w_s_up', 'w_s_down']
_OUTS = ([(1, S, D), (NS, 1, D), (1, 1, S, 2, SBH, HD), (1, NS, 1, 2, SBH, HD)]
         + [s for w in WIN for s in ((1, 1, min(w, S), 2, GH, HD), (1, NS, w, 2, GH, HD))])


def shape_constants():
    c = {}
    i, j = np.arange(P)[:, None], np.arange(P)[None, :]
    c["ident"] = (i == j).astype(np.float32)
    c["ntri"] = -(i >= j).astype(np.float32)
    c["nones"] = -np.ones((P, P), np.float32)
    c["ones"] = np.ones((P, P), np.float32)
    g = np.arange(EG)
    c["earlier"] = np.broadcast_to((g[None, :] < g[:, None]).astype(np.float32), (P, EG, EG)).copy()
    tok = np.arange(NT)[None, :] * P + i
    c["valid"] = (tok < T).astype(np.float32)
    c["tokid"] = tok.astype(np.int32)
    c["turn_first"] = np.broadcast_to(np.arange(0, NBLK, TURN, dtype=np.float32), (P, NBLK // TURN)).copy()
    c["number"] = i.astype(np.float32)
    c["before"] = (i < j).astype(np.float32)
    jj = np.arange(2 * P)[None, :]
    c["band"] = np.where((jj >= i) & (jj <= i + P), 0, -BIG).astype(np.float32)
    share = DIL[2] // (S // P)
    c["pairs"] = np.where((i % share == j % share) & (j <= i), 0, -BIG).astype(np.float32)
    half = HD // 2
    inv = np.float32(10000.0) ** (-np.arange(half, dtype=np.float32) / np.float32(half))
    pos = np.zeros(NT * P, np.float32)
    pos[:S] = np.arange(S)
    pos[S:] = PAST
    ang = pos[:, None] * inv.astype(np.float32)[None, :]
    c["cos"] = np.cos(ang).astype(np.float32).reshape(NT, P, half).transpose(1, 0, 2).copy()
    c["sin"] = np.sin(ang).astype(np.float32).reshape(NT, P, half).transpose(1, 0, 2).copy()
    return c


def kernel(**inputs):
    import concourse.bacc as _bacc
    from concourse.bass_utils import run_bass_kernel_spmd as _run

    nc = _bacc.Bacc("TRN2", target_bir_lowering=False, num_devices=1)
    arrays, a = {}, {}
    given = {name: np.ascontiguousarray(inputs[name]) for name in _INS}
    given.update(shape_constants())
    for name, arr in given.items():
        arrays[f"in_{name}"] = arr
        a[name] = nc.dram_tensor(f"in_{name}", arr.shape, mybir.dt.from_np(arr.dtype), kind="ExternalInput").ap()
    o = [nc.dram_tensor(f"out_{i}", shape, F32, kind="ExternalOutput").ap() for i, shape in enumerate(_OUTS)]
    build(nc, a, o)
    r = _run(nc, [arrays], core_ids=[0])
    return tuple(r.results[0][f"out_{i}"] for i in range(len(_OUTS)))
```

```python
import math
from contextlib import ExitStack

import numpy as np
import concourse.bass as bass
from concourse import mybir

ALU = mybir.AluOpType
ACT = mybir.ActivationFunctionType
F32 = mybir.dt.float32
F32R = mybir.dt.float32r
I32 = mybir.dt.int32
AX_X = mybir.AxisListType.X
P = 128

D = 1024
S = 1024
NS = 8
T = S + NS
NT = S // P + 1
PAST = 2048
PAGE = 128
NPAGES = PAST // PAGE
HD = 64
SBH = 8
SBW = SBH * HD
WIN = (128, 512, 2048)
DIL = (1, 4, 16)
NG = 3
GH = 4
GW = GH * HD
DW = NG * GW
KC = D // P
E = 64
EG = 8
PER = E // EG
TOPG = 4
TOPK = 8
DE = 256
BLK = 160
TURN = 2
NBLK = -(-((T * TOPK + E * (BLK - 1)) // BLK) // TURN) * TURN
SLOTS = NBLK * BLK
WHOLE = 4
SURE = T * TOPK // BLK // WHOLE * WHOLE
EPS = 1e-6
BIG = 1e30


def rows_of(t):
    return P if t < NT - 1 else NS


def plan_projection():
    items = []
    for n in range(8):
        width = 512 if n < 7 else 256
        for t in range(NT):
            items.append(dict(n=n, t=t, w=width, normed=3 <= n <= 5,
                              turned=n in (0, 1, 3, 4, 5) and t < NT - 1))
    return items


TURN_BASE = {0: 0, 1: 4, 3: 8, 4: 12, 5: 16}


def build(nc, a, o):
    (y_prompt, y_sample, sb_prompt, sb_sample, win0_p, win0_s, win1_p, win1_s, win2_p, win2_s) = o
    win_p, win_s = (win0_p, win1_p, win2_p), (win0_s, win1_s, win2_s)
    caches = (a["cache_win0_kv"], a["cache_win1_kv"], a["cache_win2_kv"])

    def dram(name, shape, dt=F32):
        return nc.dram_tensor(name, shape, dt).ap()

    scratch = dict(
        ht=dram("ht_scratch", [P, KC * T]),
        samp=dram("samp_scratch", [NS, 3 * SBW + 3 * DW]),
        dv=dram("dv_scratch", [S, DW]),
        znew=dram("znew_scratch", [NS, NG * GH]),
        mde=dram("mde_scratch", [NS * NG * GH, 3]),
        od=dram("od_scratch", [NG, T, GW + 2 * GH]),
        x1=dram("x1_scratch", [T, D]),
        x2=dram("x2_scratch", [T, D]),
        h2=dram("h2_scratch", [T + 1, D]),
        table=dram("table_scratch", [SLOTS, 1], I32),
        eb=dram("eb_scratch", [1, NBLK + 1], I32),
        y=dram("y_scratch", [SLOTS, D]),
    )
    with ExitStack() as ctx:
        sb = lambda name, shape, dt=F32: ctx.enter_context(nc.sbuf_tensor(name, shape, dt))
        held = []

        def semaphore(name):
            held.append(nc.alloc_semaphore(name=name))
            return held[-1]

        scratch["semaphore"] = semaphore
        ident = sb("ident", [P, P])
        scores = sb("scores", [P, NT, E])
        dest = sb("dest", [P, NT * TOPK], I32)
        weight = sb("weight", [P, NT * TOPK])
        expert_row = sb("expert_row", [1, NBLK + 1], I32)
        slot_token = sb("slot_token", [P, NBLK], I32)
        slot_token_tail = sb("slot_token_tail", [BLK - P, NBLK], I32)
        with ExitStack() as attention:
            turned = attention.enter_context(nc.sbuf_tensor("turned", [P, 20, S], F32))
            phase_project(nc, a, o, scratch, ident, turned)
            oT = attention.enter_context(nc.sbuf_tensor("oT", [P, SBH // 2, T], F32))
            odT = attention.enter_context(nc.sbuf_tensor("odT", [P, GW // P, T], F32))
            phase_sample_window(nc, a, o, scratch, ident)
            phase_prompt_window(nc, a, o, scratch, ident, turned, odT)
            phase_stick(nc, a, o, scratch, turned, oT)
            nc.clear_and_free_semaphores(held)
            nc.all_engine_barrier()
            phase_gate(nc, a, o, scratch, turned, oT, odT)
            phase_out(nc, a, o, scratch, ident, turned, scores)
            phase_route(nc, a, o, scratch, ident, turned, scores, dest, weight, expert_row, slot_token, slot_token_tail)
        phase_experts(nc, a, o, scratch, ident, expert_row, slot_token, slot_token_tail)
        phase_combine(nc, a, o, scratch, dest, weight)


def phase_project(nc, a, o, sc, ident, turned):
    (y_prompt, y_sample, sb_prompt, sb_sample, win0_p, win0_s, win1_p, win1_s, win2_p, win2_s) = o
    win_p, win_s = (win0_p, win1_p, win2_p), (win0_s, win1_s, win2_s)
    caches = (a["cache_win0_kv"], a["cache_win1_kv"], a["cache_win2_kv"])
    items = plan_projection()
    NI = len(items)
    NSTAGE = 4
    w_view = a["w_in"][0].rearrange("(p c) n -> p c n", c=KC)

    with ExitStack() as ctx:
        sb = lambda name, shape, dt=F32: ctx.enter_context(nc.sbuf_tensor(name, shape, dt))
        sem = sc["semaphore"]
        xin = sb("xin", [P, 2, D])
        junk = sb("junk", [P, D])
        h = sb("h", [P, 2, D])
        gain = sb("gain", [P, D])
        ss = sb("ss", [P, NT])
        rms = sb("rms", [P, NT])
        rstd = sb("rstd", [P, NT])
        eps = sb("eps", [P, 1])
        hT = sb("hT", [P, KC, T])
        wbuf = sb("wbuf", [P, 2, KC, 512])
        stage = sb("stage", [P, NSTAGE, 512])
        sqr = sb("sqr", [P, 512])
        ropeA = sb("ropeA", [P, 512])
        ropeB = sb("ropeB", [P, 512])
        hss = sb("hss", [P, 8])
        hrms = sb("hrms", [P, 8])
        hrs = sb("hrs", [P, 8])
        qkgain = sb("qkgain", [P, 3, 512])
        cos = sb("cos", [P, NT, 32])
        sin = sb("sin", [P, NT, 32])
        pP = ctx.enter_context(nc.psum_tensor("pP", [P, 4, 512], F32))
        pT = ctx.enter_context(nc.psum_tensor("pT", [P, 4, 512], F32))

        consts_in = sem("consts_in")
        x_in = [sem(f"x_in{i}") for i in range(2)]
        w_loaded = [sem(f"w_loaded{i}") for i in range(2)]
        stored = [sem(f"stored{i}") for i in range(NSTAGE)]
        ht_out = sem("ht_out")
        copies_out = sem("copies_out")
        ss_ready = sem("ss_ready")
        rms_ready = sem("rms_ready")
        hrms_ready = sem("hrms_ready")
        eps_set = sem("eps_set")
        dve_step = sem("dve_step")
        h_ready = sem("h_ready")
        hT_psum = sem("hT_psum")
        hT_copied = sem("hT_copied")
        p_ready = sem("p_ready")
        stage_ready = sem("stage_ready")
        sqr_ready = sem("sqr_ready")
        sqr_used = sem("sqr_used")
        normed = sem("normed")
        turn_psum = sem("turn_psum")
        turn_copied = sem("turn_copied")

        n_normed = [sum(x["normed"] for x in items[:i]) for i in range(NI + 1)]
        n_turned = [sum(x["turned"] for x in items[:i]) for i in range(NI + 1)]

        def stores(i):
            n, t = items[i]["n"], items[i]["t"]
            r0, out = t * P, []
            if t == NT - 1:
                w = items[i]["w"]
                out.append((sc["samp"][:, n * 512:n * 512 + w], 0, w))
            if n in (1, 2):
                dst = (sb_prompt[0, 0, r0:r0 + P, n - 1] if t < NT - 1 else sb_sample[0, :, 0, n - 1])
                out.append((dst.rearrange("s h d -> s (h d)"), 0, SBW))
            if n >= 3:
                for half in range(items[i]["w"] // GW):
                    part, g = divmod(2 * (n - 3) + half, NG)
                    if part == 0:
                        continue
                    if t == NT - 1:
                        out.append((win_s[g][0, :, WIN[g] - 1, part - 1].rearrange("s h d -> s (h d)"), half * GW, GW))
                        continue
                    if part == 2:
                        out.append((sc["dv"][r0:r0 + P, g * GW:(g + 1) * GW], half * GW, GW))
                    w0 = r0 - (S - min(WIN[g], S))
                    if w0 >= 0:
                        out.append((win_p[g][0, 0, w0:w0 + P, part - 1].rearrange("s h d -> s (h d)"), half * GW, GW))
            return out

        plan = [stores(i) for i in range(NI)]
        store_value = [16 * sum(len(plan[j]) for j in range(i % NSTAGE, i + 1, NSTAGE)) for i in range(NI)]

        with nc.Block() as block:
            @block.sync
            def _(sp):
                sp.dma_start(ident[:, :], a["ident"]).then_inc(consts_in, 16)
                sp.dma_start(gain[:, :], a["norm1_g"].broadcast_to([P, D])).then_inc(consts_in, 16)
                sp.dma_start(cos[:, :, :], a["cos"]).then_inc(consts_in, 16)
                sp.dma_start(sin[:, :, :], a["sin"]).then_inc(consts_in, 16)
                for j in range(24):
                    src = a["qn_g"] if j < 12 else a["kn_g"]
                    sp.dma_start(qkgain[:, j // 8, (j % 8) * HD:(j % 8 + 1) * HD], src.broadcast_to([P, HD])).then_inc(consts_in, 16)
                for t in range(NT):
                    if t >= 2:
                        sp.wait_ge(h_ready, t - 1)
                    n = rows_of(t)
                    src = a["x_prompt"][0, t * P:t * P + P] if t < NT - 1 else a["x_sample"][:, 0]
                    sp.dma_start(xin[:n, t % 2, :], src).then_inc(x_in[t % 2], 16)

                def load_w(n):
                    w = 512 if n < 7 else 256
                    sp.dma_start(wbuf[:, n % 2, :, :w], w_view[:, :, n * 512:n * 512 + w]).then_inc(w_loaded[n % 2], 16)

                def move_windows(s):
                    for g in range(NG):
                        src = caches[g][0, s].rearrange("w a h d -> (w a h d)")[2 * GW:]
                        dst = win_s[g][0, s].rearrange("w a h d -> (w a h d)")[:(WIN[g] - 1) * 2 * GW]
                        sp.dma_start(dst.rearrange("(p n) -> p n", p=P), src.rearrange("(p n) -> p n", p=P)).then_inc(copies_out, 16)

                load_w(0)
                load_w(1)
                sp.wait_ge(hT_copied, NT)
                sp.dma_start(sc["ht"], hT[:, :, :].rearrange("p c t -> p (c t)")).then_inc(ht_out, 16)
                for i in range(NI):
                    n, t = items[i]["n"], items[i]["t"]
                    if t == 2 and 1 <= n <= 6:
                        load_w(n + 1)
                    if t == 3:
                        move_windows(n)
                    if plan[i]:
                        if items[i]["normed"]:
                            sp.wait_ge(normed, n_normed[i + 1])
                        else:
                            sp.wait_ge(stage_ready, i + 1)
                        m = rows_of(t)
                        for dst, c0, w in plan[i]:
                            sp.dma_start(dst, stage[:m, i % NSTAGE, c0:c0 + w]).then_inc(stored[i % NSTAGE], 16)
                    if t == 1 and 1 <= n <= 6:
                        sp.wait_ge(p_ready, 9 * n)
                for slot in range(NSTAGE):
                    last = max(i for i in range(NI) if i % NSTAGE == slot)
                    sp.wait_ge(stored[slot], store_value[last])
                sp.wait_ge(ht_out, 16)
                sp.wait_ge(copies_out, 16 * NG * NS)

            @block.gpsimd
            def _(pool):
                pool.memset(eps[:, :], EPS).then_inc(eps_set, 1)
                for i in range(NI):
                    if not items[i]["normed"]:
                        continue
                    m = rows_of(items[i]["t"])
                    pool.wait_ge(stage_ready, i + 1)
                    if n_normed[i]:
                        pool.wait_ge(sqr_used, n_normed[i])
                    s_ = stage[:m, i % NSTAGE, :]
                    pool.tensor_tensor(sqr[:m, :], s_, s_, ALU.mult).then_inc(sqr_ready, 1)

            @block.scalar
            def _(act):
                act.wait_ge(consts_in, 28 * 16)
                act.wait_ge(eps_set, 1)
                for t in range(NT + 1):
                    if t < NT:
                        m = rows_of(t)
                        act.wait_ge(x_in[t % 2], 16 * (t // 2 + 1))
                        act.activation(junk[:m, :], xin[:m, t % 2, :], ACT.Square, accum_out=ss[:m, t:t + 1]).then_inc(ss_ready, 1)
                        act.wait_ge(ss_ready, t + 1)
                        act.activation(rms[:m, t:t + 1], ss[:m, t:t + 1], ACT.Sqrt, scale=1.0 / D, bias=eps[:m, :]).then_inc(rms_ready, 1)
                    if t >= 1:
                        u = t - 1
                        m = rows_of(u)
                        act.wait_ge(hT_psum, u + 1)
                        b = 2 * (u % 2)
                        act.activation(hT[:, :, u * P:u * P + m],
                                       pT[:, b:b + 2, :].rearrange("p a (c t) -> p (a c) t", t=P)[:, :, :m],
                                       ACT.Copy).then_inc(hT_copied, 1)
                for i in range(NI + 3):
                    if i < NI:
                        m, w = rows_of(items[i]["t"]), items[i]["w"]
                        act.wait_ge(p_ready, i + 1)
                        if i >= NSTAGE:
                            if store_value[i - NSTAGE]:
                                act.wait_ge(stored[i % NSTAGE], store_value[i - NSTAGE])
                            if n_turned[i - NSTAGE + 1]:
                                act.wait_ge(turn_psum, n_turned[i - NSTAGE + 1])
                            if n_normed[i - NSTAGE + 1]:
                                act.wait_ge(normed, n_normed[i - NSTAGE + 1])
                        scale = HD ** -0.5 if items[i]["n"] == 0 else 1.0
                        act.activation(stage[:m, i % NSTAGE, :w], pP[:m, i % 4, :w], ACT.Copy, scale=scale).then_inc(stage_ready, 1)
                    j = i - 1
                    if 0 <= j < NI and items[j]["normed"]:
                        m = rows_of(items[j]["t"])
                        act.wait_ge(sqr_used, n_normed[j + 1])
                        act.activation(hrms[:m, :], hss[:m, :], ACT.Sqrt, scale=1.0 / HD, bias=eps[:m, :]).then_inc(hrms_ready, 1)
                    j = i - 3
                    if j >= 0 and items[j]["turned"]:
                        n, t = items[j]["n"], items[j]["t"]
                        act.wait_ge(turn_psum, n_turned[j + 1])
                        act.activation(turned[:, TURN_BASE[n]:TURN_BASE[n] + 4, t * P:(t + 1) * P],
                                       pT[:, n_turned[j] % 4, :].rearrange("p (c t) -> p c t", t=P),
                                       ACT.Copy).then_inc(turn_copied, 1)

            @block.vector
            def _(dve):
                steps = [0]

                def chain(ins):
                    steps[0] += 1
                    ins.then_inc(dve_step, 1)
                    dve.wait_ge(dve_step, steps[0])

                dve.wait_ge(consts_in, 28 * 16)
                qg = qkgain[:, :, :].rearrange("p a b -> p (a b)")[:, :12 * HD]
                chain(dve.tensor_scalar(qg, qg, HD ** -0.5, None, ALU.mult))
                for t in range(NT):
                    m = rows_of(t)
                    r = rstd[:m, t:t + 1]
                    dve.wait_ge(rms_ready, t + 1)
                    chain(dve.reciprocal(r, rms[:m, t:t + 1]))
                    if t >= 2:
                        dve.wait_ge(hT_psum, t - 1)
                    dve.scalar_tensor_tensor(h[:m, t % 2, :], xin[:m, t % 2, :], r, gain[:m, :], ALU.mult, ALU.mult).then_inc(h_ready, 1)
                for i in range(NI):
                    if not items[i]["normed"]:
                        continue
                    n, t = items[i]["n"], items[i]["t"]
                    m = rows_of(t)
                    x = stage[:m, i % NSTAGE, :]
                    xh = x.rearrange("p (h d) -> p h d", d=HD)
                    dve.wait_ge(sqr_ready, n_normed[i + 1])
                    dve.tensor_reduce(hss[:m, :], sqr[:m, :].rearrange("p (h d) -> p h d", d=HD), AX_X, ALU.add).then_inc(sqr_used, 1)
                    dve.wait_ge(hrms_ready, n_normed[i + 1])
                    chain(dve.reciprocal(hrs[:m, :], hrms[:m, :]))
                    chain(dve.tensor_tensor(xh, xh, hrs[:m, :].unsqueeze(2).broadcast_to([m, 8, HD]), ALU.mult))
                    chain(dve.tensor_tensor(x, x, qkgain[:m, n - 3, :], ALU.mult))
                    x4 = x.rearrange("p (h a d) -> p h a d", a=2, d=32)
                    A = ropeA[:m, :].rearrange("p (h a d) -> p h a d", a=2, d=32)
                    B = ropeB[:m, :].rearrange("p (h a d) -> p h a d", a=2, d=32)
                    c3 = cos[:m, t, :].unsqueeze(1).broadcast_to([m, 16, 32])
                    s3 = sin[:m, t, :].unsqueeze(1).broadcast_to([m, 8, 32])
                    dve.tensor_tensor(ropeA[:m, :].rearrange("p (h d) -> p h d", d=32), x.rearrange("p (h d) -> p h d", d=32), c3, ALU.mult)
                    dve.tensor_tensor(B[:, :, 0, :], x4[:, :, 1, :], s3, ALU.mult)
                    chain(dve.tensor_tensor(B[:, :, 1, :], x4[:, :, 0, :], s3, ALU.mult))
                    dve.tensor_tensor(x4[:, :, 0, :], A[:, :, 0, :], B[:, :, 0, :], ALU.subtract)
                    dve.tensor_tensor(x4[:, :, 1, :], A[:, :, 1, :], B[:, :, 1, :], ALU.add).then_inc(normed, 1)

            @block.tensor
            def _(pe):
                pe.wait_ge(consts_in, 28 * 16)
                for t in range(NT):
                    m = rows_of(t)
                    pe.wait_ge(h_ready, t + 1)
                    if t >= 2:
                        pe.wait_ge(hT_copied, t - 1)
                    hv = h[:m, t % 2, :].rearrange("p (q c) -> p c q", c=KC)
                    for c in range(KC):
                        last = pe.transpose(pT[:, 2 * (t % 2) + c // 4, (c % 4) * P:(c % 4) * P + m], hv[:, c, :], ident[:m, :m])
                    last.then_inc(hT_psum, 1)
                pe.wait_ge(hT_copied, NT)
                for i in range(NI + 2):
                    if i < NI:
                        n, t, w = items[i]["n"], items[i]["t"], items[i]["w"]
                        m = rows_of(t)
                        if t == 0:
                            pe.wait_ge(w_loaded[n % 2], 16 * (n // 2 + 1))
                        if i >= 4:
                            pe.wait_ge(stage_ready, i - 3)
                        for c in range(KC):
                            last = pe.matmul(pP[:m, i % 4, :w], hT[:, c, t * P:t * P + m], wbuf[:, n % 2, c, :w],
                                             start=(c == 0), stop=(c == KC - 1))
                        last.then_inc(p_ready, 1)
                    j = i - 2
                    if j >= 0 and items[j]["turned"]:
                        if items[j]["normed"]:
                            pe.wait_ge(normed, n_normed[j + 1])
                        else:
                            pe.wait_ge(stage_ready, j + 1)
                        if n_turned[j] >= 4:
                            pe.wait_ge(turn_copied, n_turned[j] - 3)
                        for c in range(4):
                            last = pe.transpose(pT[:, n_turned[j] % 4, c * P:(c + 1) * P],
                                                stage[:, j % NSTAGE, c * P:(c + 1) * P], ident[:, :])
                        last.then_inc(turn_psum, 1)


def phase_stick(nc, a, o, sc, turned, oT):
    QC = 512
    R = 2
    RZ = 3
    items = []
    for hp in range(SBH // 2):
        for c in range(S // QC):
            top = (c + 1) * QC // P - 1
            for kb in range(top, -1, -1):
                off = max(0, kb * P - c * QC)
                items.append(dict(hp=hp, c=c, kb=kb, off=off, first=kb == top, last=kb == 0, diag=kb * P >= c * QC,
                                  prev=min(QC, off + P) if kb * P >= c * QC else 0))
    NI = len(items)
    n_diag = [sum(x["diag"] for x in items[:i]) for i in range(NI + 1)]

    GP = 4
    NPC = NPAGES // GP
    NKB, NVB = 4, 5
    V_LAG = 7
    L = 5
    PRODUCT = [0, 1, 2, 3]
    SCORE = [1, 2, 3, 4]
    LOW, LN, SOFT, SUMS, LOGIT, PROB = L, L + 1, L + 2, L + 3, L + 4, L + 5
    VALUES = [L + 5, L + 6, L + 7, L + 8]
    TICKS = max(NI + 5, (NS - 1) * L + VALUES[-1] + 1)

    def at(i, step):
        s, rest = divmod(i - step, L)
        return s if rest == 0 and 0 <= s < NS else None

    pool_kv = a["cache_sb_kv"][0].rearrange("n p a h d -> n p a (h d)")
    n_pool = pool_kv.shape[0]
    with ExitStack() as ctx:
        sb = lambda name, shape, dt=F32: ctx.enter_context(nc.sbuf_tensor(name, shape, dt))
        sem = sc["semaphore"]
        v = sb("v_rows", [P, S // P, SBW])
        bias = sb("bias", [P, SBH])
        ntri = sb("ntri", [P, P])
        nones = sb("nones", [P, P])
        before = sb("before", [P, P])
        low = sb("low", [P, R, 2, QC])
        soft = sb("soft", [P, R, 2, QC])
        later = sb("later", [P, 2, 2, QC])
        prob = sb("prob", [P, R, 2, QC])
        spare = turned[:, 8:, :].rearrange("p a b -> p (a b)")
        K1, Q1 = NKB * GP * SBW, (NKB * GP + 2) * SBW
        kbuf = spare[:, :K1].rearrange("p (n j d) -> p n j d", n=NKB, j=GP)
        q = spare[:, K1:Q1].rearrange("p (n d) -> p n d", n=2)
        prod = spare[:, Q1:Q1 + GP * SBW].rearrange("p (j d) -> p j d", j=GP)
        vbuf = sb("vbuf", [P, NVB, GP, SBW])
        pages = sb("pages", [1, NS * NPAGES], I32)
        s_z = sb("s_z", [P, 2, NPAGES, SBH])
        s_low = sb("s_low", [P, NPAGES, SBH])
        s_soft = sb("s_soft", [P, 2, NPAGES + 2, SBH])
        s_span = sb("s_span", [P, 2, NPAGES + NPAGES // 2, SBH])
        s_after = sb("s_after", [P, NPAGES, SBH])
        s_logit = sb("s_logit", [P, NPAGES, SBH])
        s_prob = sb("s_prob", [P, 2, NPAGES, SBH])
        pZ = ctx.enter_context(nc.psum_tensor("pZ", [P, RZ, 2, QC], F32))
        pO = ctx.enter_context(nc.psum_tensor("pO", [P, QC], F32))
        pS = ctx.enter_context(nc.psum_tensor("pS", [P, 512], F32))
        s_sums = pS[:, :NPAGES * SBH]
        s_out = pS[:, NPAGES * SBH:NPAGES * SBH + NS * 8 * NPC].rearrange("p (n b c) -> p n b c", b=2, c=NPC)

        consts_in = sem("p_consts_in")
        v_in = sem("p_v_in")
        z_ready = sem("p_z_ready")
        low_ready = sem("p_low_ready")
        exp_ready = sem("p_exp_ready")
        ln_ready = sem("p_ln_ready")
        soft_ready = sem("p_soft_ready")
        soft_masked = sem("p_soft_masked")
        later_ready = sem("p_later_ready")
        sums_ready = sem("p_sums_ready")
        prob_ready = sem("p_prob_ready")
        prob_masked = sem("p_prob_masked")
        pv_done = sem("p_pv_done")
        out_copied = sem("p_out_copied")

        pages_in = sem("s_pages_in")
        q_in = [sem(f"s_q_in{i}") for i in range(2)]
        k_in = [sem(f"s_k_in{i}") for i in range(NKB)]
        vs_in = [sem(f"s_v_in{i}") for i in range(NVB)]
        s_prod_ready = sem("s_prod_ready")
        s_score_ready = sem("s_score_ready")
        s_z_ready = sem("s_z_ready")
        s_low_ready = sem("s_low_ready")
        s_exp_ready = sem("s_exp_ready")
        s_ln_ready = sem("s_ln_ready")
        s_soft_ready = sem("s_soft_ready")
        s_zeros_set = sem("s_zeros_set")
        s_span_ready = sem("s_span_ready")
        s_after_ready = sem("s_after_ready")
        s_sums_ready = sem("s_sums_ready")
        s_logit_ready = sem("s_logit_ready")
        s_prob_ready = sem("s_prob_ready")
        s_v_used = sem("s_v_used")
        s_out_copied = sem("s_out_copied")

        with nc.Block() as block:
            @block.sync
            def _(sp):
                sp.dma_start(pages[:, :], a["page_table"].rearrange("s (n a) -> a (s n)", a=1)).then_inc(pages_in, 16)
                sp.dma_start(bias[:, :], a["sb_bias"].broadcast_to([P, SBH])).then_inc(consts_in, 16)
                sp.dma_start(ntri[:, :], a["ntri"]).then_inc(consts_in, 16)
                sp.dma_start(nones[:, :], a["nones"]).then_inc(consts_in, 16)
                sp.dma_start(before[:, :], a["before"]).then_inc(consts_in, 16)
                sp.dma_start(v[:, :, :], o[2][0, 0, :, 1].rearrange("(t p) h d -> p t (h d)", p=P)).then_inc(v_in, 16)
                sp.wait_ge(pages_in, 16)
                for n in range(NS * NPC + V_LAG):
                    if n < NS * NPC:
                        s, c = divmod(n, NPC)
                        if c == 0:
                            if s >= 2:
                                sp.wait_ge(s_prod_ready, NPC * (s - 1))
                            sp.dma_start(q[:, s % 2, :], sc["samp"][s:s + 1, 0:SBW].broadcast_to([P, SBW])).then_inc(q_in[s % 2], 16)
                        if n >= NKB:
                            sp.wait_ge(s_prod_ready, n - NKB + 1)
                        for j in range(GP):
                            pg = sp.value_load(pages[0:1, n * GP + j:n * GP + j + 1], min_val=0, max_val=n_pool - 1)
                            sp.dma_start(kbuf[:, n % NKB, j, :], pool_kv[bass.ds(pg, 1), :, 0, :].rearrange("n p d -> (n p) d")).then_inc(k_in[n % NKB], 16)
                    m = n - V_LAG
                    if m >= 0:
                        if m >= NVB:
                            sp.wait_ge(s_v_used, m - NVB + 1)
                        for j in range(GP):
                            pg = sp.value_load(pages[0:1, m * GP + j:m * GP + j + 1], min_val=0, max_val=n_pool - 1)
                            sp.dma_start(vbuf[:, m % NVB, j, :], pool_kv[bass.ds(pg, 1), :, 1, :].rearrange("n p d -> (n p) d")).then_inc(vs_in[m % NVB], 16)

            @block.vector
            def _(dve):
                dve.wait_ge(consts_in, 64)
                for i in range(-1, TICKS):
                    j = i - 1
                    if 0 <= j < NI:
                        off, h = items[j]["off"], 2 * items[j]["hp"]
                        dve.wait_ge(ln_ready, j + 1)
                        if j >= R:
                            dve.wait_ge(sums_ready, j - R + 1)
                            dve.wait_ge(later_ready, j - R + 1)
                        for par in range(2):
                            last = dve.scalar_tensor_tensor(soft[:, j % R, par, off:], pZ[:, j % RZ, par, off:], bias[:, h + par:h + par + 1],
                                                            low[:, j % R, par, off:], ALU.add, ALU.max)
                        last.then_inc(soft_ready, 1)
                    j = i - 3
                    if 0 <= j < NI and items[j]["last"]:
                        it = items[j]
                        dve.wait_ge(pv_done, j + 1)
                        dve.tensor_copy(oT[:, it["hp"], it["c"] * QC:(it["c"] + 1) * QC], pO[:, :]).then_inc(out_copied, 1)

                    for c in range(NPC):
                        s = at(i, PRODUCT[c])
                        if s is not None:
                            n = s * NPC + c
                            if c == 0:
                                dve.wait_ge(q_in[s % 2], 16 * (s // 2 + 1))
                            dve.wait_ge(k_in[n % NKB], 16 * GP * (n // NKB + 1))
                            if n:
                                dve.wait_ge(s_score_ready, n)
                            dve.tensor_tensor(prod[:, :, :], kbuf[:, n % NKB], q[:, s % 2, :].unsqueeze(1).broadcast_to([P, GP, SBW]),
                                              ALU.mult).then_inc(s_prod_ready, 1)
                        s = at(i, SCORE[c])
                        if s is not None:
                            n = s * NPC + c
                            dve.wait_ge(s_prod_ready, n + 1)
                            if s >= 2:
                                dve.wait_ge(s_logit_ready, s - 1)
                            dve.tensor_reduce(s_z[:, s % 2, c * GP:(c + 1) * GP, :].rearrange("p a h -> p (a h)"),
                                              prod[:, :, :].rearrange("p a (h d) -> p (a h) d", d=HD), AX_X, ALU.add).then_inc(s_score_ready, 1)
                    s = at(i, LOW)
                    if s is not None:
                        z = s_z[:, s % 2, :, :]
                        dve.wait_ge(s_score_ready, NPC * (s + 1))
                        dve.tensor_tensor(z, z, bias[:, :].unsqueeze(1).broadcast_to([P, NPAGES, SBH]), ALU.add).then_inc(s_z_ready, 1)
                        dve.wait_ge(s_z_ready, s + 1)
                        if s:
                            dve.wait_ge(s_soft_ready, s)
                        dve.tensor_scalar(s_low[:, :, :], z, 30.0, None, ALU.min).then_inc(s_low_ready, 1)
                    s = at(i, SOFT)
                    if s is not None:
                        dve.wait_ge(s_ln_ready, s + 1)
                        if s >= 2:
                            dve.wait_ge(s_sums_ready, s - 1)
                            dve.wait_ge(s_after_ready, s - 1)
                        dve.tensor_tensor(s_soft[:, s % 2, :NPAGES, :], s_low[:, :, :], s_z[:, s % 2, :, :], ALU.max).then_inc(s_soft_ready, 1)
                    s = at(i, LOGIT)
                    if s is not None:
                        dve.wait_ge(s_sums_ready, s + 1)
                        if s:
                            dve.wait_ge(s_prob_ready, s)
                        dve.tensor_tensor(s_logit[:, :, :], s_sums.rearrange("p (a h) -> p a h", h=SBH), s_z[:, s % 2, :, :],
                                          ALU.add).then_inc(s_logit_ready, 1)
                    j = i + 1
                    if j < NI:
                        off, h = items[j]["off"], 2 * items[j]["hp"]
                        dve.wait_ge(z_ready, j + 1)
                        if j >= R:
                            dve.wait_ge(soft_ready, j - R + 1)
                        for par in range(2):
                            last = dve.tensor_scalar(low[:, j % R, par, off:], pZ[:, j % RZ, par, off:], bias[:, h + par:h + par + 1], 30.0,
                                                     ALU.add, ALU.min)
                        last.then_inc(low_ready, 1)
                dve.wait_ge(s_v_used, NS * NPC)
                view = s_out.rearrange("p (s n) b c -> p b n s c", n=SBH // 2)
                for b in range(2):
                    dve.tensor_reduce(oT[64 * b:64 * b + 64, :, S:T], view[64 * b:64 * b + 64, b], AX_X, ALU.add).then_inc(s_out_copied, 1)

            @block.gpsimd
            def _(pool):
                pool.memset(s_soft[:, :, NPAGES:, :], 0.0)
                pool.memset(s_span[:, :, NPAGES:, :], 0.0).then_inc(s_zeros_set, 1)
                pool.wait_ge(s_zeros_set, 1)
                pool.wait_ge(consts_in, 64)
                for i in range(TICKS):
                    if i < NI:
                        it = items[i]
                        off, prev = it["off"], it["prev"]
                        pool.wait_ge(soft_ready, i + 1)
                        if it["diag"]:
                            d = soft[:, i % R, :, off:off + P]
                            pool.tensor_tensor(d, d, before[:, :].unsqueeze(1).broadcast_to([P, 2, P]), ALU.mult).then_inc(soft_masked, 1)
                            pool.wait_ge(soft_masked, n_diag[i + 1])
                        kk = it["kb"] % 2
                        dst, old, s_ = later[:, kk], later[:, 1 - kk], soft[:, i % R]
                        if i:
                            pool.wait_ge(sums_ready, i)
                        last = None
                        if prev > off:
                            last = pool.tensor_copy(dst[:, :, off:prev], s_[:, :, off:prev])
                        if prev < QC:
                            pool.wait_ge(later_ready, i)
                            last = pool.tensor_tensor(dst[:, :, prev:], old[:, :, prev:], s_[:, :, prev:], ALU.add)
                        last.then_inc(later_ready, 1)
                    j = i - 1
                    if 0 <= j < NI and items[j]["diag"]:
                        pool.wait_ge(prob_ready, j + 1)
                        d = prob[:, j % R, :, items[j]["off"]:items[j]["off"] + P]
                        pool.tensor_tensor(d, d, before[:, :].unsqueeze(1).broadcast_to([P, 2, P]), ALU.mult).then_inc(prob_masked, 1)
                    s = at(i + 1, SOFT)
                    if s is not None:
                        pool.wait_ge(s_soft_ready, s + 1)
                        page_sp = s_soft[:, s % 2]
                        pool.tensor_tensor(s_span[:, 0, :NPAGES, :], page_sp[:, 1:NPAGES + 1, :], page_sp[:, 2:NPAGES + 2, :], ALU.add).then_inc(s_span_ready, 1)
                        pool.wait_ge(s_span_ready, 3 * s + 1)
                        pool.tensor_tensor(s_span[:, 1, :NPAGES, :], s_span[:, 0, :NPAGES, :], s_span[:, 0, 2:NPAGES + 2, :], ALU.add).then_inc(s_span_ready, 1)
                        pool.wait_ge(s_span_ready, 3 * s + 2)
                        pool.tensor_tensor(s_span[:, 0, :NPAGES, :], s_span[:, 1, :NPAGES, :], s_span[:, 1, 4:NPAGES + 4, :], ALU.add).then_inc(s_span_ready, 1)
                        pool.wait_ge(s_span_ready, 3 * s + 3)
                        if s:
                            pool.wait_ge(s_sums_ready, s)
                            pool.wait_ge(s_after_ready, s)
                        pool.tensor_tensor(s_after[:, :, :], s_span[:, 0, :NPAGES, :], s_span[:, 0, 8:NPAGES + 8, :], ALU.add).then_inc(s_after_ready, 1)

            @block.scalar
            def _(act):
                act.wait_ge(consts_in, 64)
                for i in range(-1, TICKS):
                    if 0 <= i < NI:
                        off = items[i]["off"]
                        act.wait_ge(low_ready, i + 1)
                        act.activation(low[:, i % R, :, off:], low[:, i % R, :, off:], ACT.Exp).then_inc(exp_ready, 1)
                    j = i - 2
                    if 0 <= j < NI:
                        off, h = items[j]["off"], 2 * items[j]["hp"]
                        act.wait_ge(sums_ready, j + 1)
                        if j >= R:
                            act.wait_ge(pv_done, j - R + 1)
                        for par in range(2):
                            last = act.activation(prob[:, j % R, par, off:], pZ[:, j % RZ, par, off:], ACT.Exp, bias=bias[:, h + par:h + par + 1])
                        last.then_inc(prob_ready, 1)
                    s = at(i, PROB)
                    if s is not None:
                        act.wait_ge(s_logit_ready, s + 1)
                        if s >= 2:
                            act.wait_ge(s_v_used, NPC * (s - 1))
                        act.activation(s_prob[:, s % 2, :, :], s_logit[:, :, :], ACT.Exp).then_inc(s_prob_ready, 1)
                    s = at(i, LN)
                    if s is not None:
                        act.wait_ge(s_low_ready, s + 1)
                        act.activation(s_low[:, :, :], s_low[:, :, :], ACT.Exp).then_inc(s_exp_ready, 1)
                    if 0 <= i < NI:
                        off = items[i]["off"]
                        act.wait_ge(exp_ready, i + 1)
                        act.activation(low[:, i % R, :, off:], low[:, i % R, :, off:], ACT.Ln, bias=1.0).then_inc(ln_ready, 1)
                    if s is not None:
                        act.wait_ge(s_exp_ready, s + 1)
                        act.activation(s_low[:, :, :], s_low[:, :, :], ACT.Ln, bias=1.0).then_inc(s_ln_ready, 1)

            @block.tensor
            def _(pe):
                pe.wait_ge(consts_in, 64)
                pe.wait_ge(v_in, 16)
                for i in range(-1, TICKS):
                    j = i - 3
                    if 0 <= j < NI:
                        it = items[j]
                        off = it["off"]
                        pe.wait_ge(prob_ready, j + 1)
                        if it["diag"]:
                            pe.wait_ge(prob_masked, n_diag[j + 1])
                        n = it["hp"] * (S // QC) + it["c"]
                        if it["first"] and n:
                            pe.wait_ge(out_copied, n)
                        for par in range(2):
                            last = pe.matmul(pO[64 * par:64 * par + 64, off:], v[:, it["kb"], (2 * it["hp"] + par) * HD:(2 * it["hp"] + par + 1) * HD],
                                             prob[:, j % R, par, off:], start=it["first"], stop=it["last"], skip_group_check=True)
                        last.then_inc(pv_done, 1)
                    j = i - 1
                    if 0 <= j < NI:
                        it = items[j]
                        off, prev = it["off"], it["prev"]
                        pe.wait_ge(soft_ready, j + 1)
                        if it["diag"]:
                            pe.wait_ge(soft_masked, n_diag[j + 1])
                        for par in range(2):
                            last = pe.matmul(pZ[:, j % RZ, par, off:], ntri[:, :], soft[:, j % R, par, off:], start=False, stop=True, skip_group_check=True)
                        if not it["first"] and prev < QC:
                            pe.wait_ge(later_ready, j)
                            for par in range(2):
                                last = pe.matmul(pZ[:, j % RZ, par, prev:], nones[:, :], later[:, 1 - it["kb"] % 2, par, prev:],
                                                 start=False, stop=True, skip_group_check=True)
                        last.then_inc(sums_ready, 1)
                    j = i + 1
                    if j < NI:
                        it = items[j]
                        if j >= RZ:
                            pe.wait_ge(prob_ready, j - RZ + 1)
                        for par in range(2):
                            b = 64 * par
                            last = pe.matmul(pZ[:, j % RZ, par, it["off"]:], turned[b:b + 64, 4 + it["hp"], it["kb"] * P:(it["kb"] + 1) * P],
                                             turned[b:b + 64, it["hp"], it["c"] * QC + it["off"]:(it["c"] + 1) * QC],
                                             start=True, stop=True, skip_group_check=True)
                        last.then_inc(z_ready, 1)

                    for c in range(NPC):
                        s = at(i, VALUES[c])
                        if s is not None:
                            m = s * NPC + c
                            if c == 0:
                                pe.wait_ge(s_prob_ready, s + 1)
                            pe.wait_ge(vs_in[m % NVB], 16 * GP * (m // NVB + 1))
                            for hp in range(SBH // 2):
                                for j in range(GP):
                                    last = pe.matmul(s_out[:, s * 4 + hp, :, c],
                                                     vbuf[:, m % NVB, j, hp * P:(hp + 1) * P],
                                                     s_prob[:, s % 2, c * GP + j, 2 * hp:2 * hp + 2],
                                                     start=(hp == 0 and j == 0), stop=(j == GP - 1), skip_group_check=True)
                            last.then_inc(s_v_used, 1)
                    s = at(i, SUMS)
                    if s is not None:
                        pe.wait_ge(s_soft_ready, s + 1)
                        if s:
                            pe.wait_ge(s_logit_ready, s)
                        pe.wait_ge(s_after_ready, s + 1)
                        pe.matmul(s_sums, ntri[:, :], s_soft[:, s % 2, :NPAGES, :].rearrange("p a h -> p (a h)"), start=True, stop=False)
                        last = pe.matmul(s_sums, nones[:, :], s_after[:, :, :].rearrange("p a h -> p (a h)"), start=False, stop=True)
                        last.then_inc(s_sums_ready, 1)


def phase_sample_window(nc, a, o, sc, ident):
    NR = NS * NG * GH
    caches = (a["cache_win0_kv"], a["cache_win1_kv"], a["cache_win2_kv"])
    Q0, K0, V0 = 3 * SBW, 3 * SBW + DW, 3 * SBW + 2 * DW
    with ExitStack() as ctx:
        sb = lambda name, shape, dt=F32: ctx.enter_context(nc.sbuf_tensor(name, shape, dt))
        sem = sc["semaphore"]
        kv = sb("kv_win", [P, NS, NG, 2 * GW])
        q = sb("q_win", [P, NS, DW])
        new = sb("new_rows", [NS, 3 * DW])
        prod = sb("prod_win", [P, 2, GW])
        prodn = sb("prod_new", [NS, DW])
        z = sb("z_win", [P, NR])
        znew = sb("z_new", [NS, NG * GH])
        zt = sb("z_turned", [NR, P + 1])
        mde = sb("mde", [NR, 3])
        nmax = sb("nmax", [NR, 1])
        mden = sb("mden", [NS, NG * GH, 3])
        em = sb("em", [P, NS, NG * GH, NS])
        vnew = sb("v_new_part", [NS, NG, GW])
        packed = sb("packed_win", [NS, NG, GW + 2 * GH])
        pA = ctx.enter_context(nc.psum_tensor("pA_win", [P, 512], F32))
        pB = ctx.enter_context(nc.psum_tensor("pB_win", [P, 512], F32))
        pV = ctx.enter_context(nc.psum_tensor("pV_win", [P, 2, 512], F32))
        q_in = sem("w_q_in")
        new_in = sem("w_new_in")
        kv_in = [sem(f"w_kv_in{g}") for g in range(NG)]
        prod_ready = sem("w_prod_ready")
        z_ready = sem("w_z_ready")
        step = sem("w_step")
        znew_ready = sem("w_znew_ready")
        znew_out = sem("w_znew_out")
        znew_back = sem("w_znew_back")
        zt_psum = sem("w_zt_psum")
        nmax_ready = sem("w_nmax_ready")
        e_ready = sem("w_e_ready")
        mde_ready = sem("w_mde_ready")
        mde_out = sem("w_mde_out")
        mde_back = sem("w_mde_back")
        e_psum = sem("w_e_psum")
        em_zero = sem("w_em_zero")
        em_ready = sem("w_em_ready")
        pv_done = sem("w_pv_done")
        packed_ready = sem("w_packed_ready")
        packed_out = sem("w_packed_out")

        with nc.Block() as block:
            @block.sync
            def _(sp):
                sp.dma_start(new[:, :], sc["samp"][:, Q0:]).then_inc(new_in, 16)
                for s in range(NS):
                    sp.dma_start(q[:, s, :], sc["samp"][s:s + 1, Q0:Q0 + DW].broadcast_to([P, DW])).then_inc(q_in, 16)
                for g in range(NG):
                    for s in range(NS):
                        src = caches[g][0, s].rearrange("(p r) a h d -> p r (a h d)", r=DIL[g])[:, 0, :]
                        sp.dma_start(kv[:, s, g, :], src).then_inc(kv_in[g], 16)
                sp.wait_ge(znew_ready, 1)
                sp.dma_start(sc["znew"], znew[:, :]).then_inc(znew_out, 16)
                sp.wait_ge(znew_out, 16)
                sp.dma_start(zt[:, P:P + 1], sc["znew"].rearrange("s (n a) -> (s n) a", a=1)).then_inc(znew_back, 16)
                sp.wait_ge(mde_ready, 1)
                sp.dma_start(sc["mde"], mde[:, :]).then_inc(mde_out, 16)
                sp.wait_ge(mde_out, 16)
                sp.dma_start(mden[:, :, :], sc["mde"].rearrange("(s n) c -> s n c", s=NS)).then_inc(mde_back, 16)
                sp.wait_ge(packed_ready, 1)
                for g in range(NG):
                    sp.dma_start(sc["od"][g, S:T, :], packed[:, g, :]).then_inc(packed_out, 16)
                sp.wait_ge(packed_out, 16 * NG)

            @block.gpsimd
            def _(pool):
                pool.memset(em[:, :, :, :], 0.0).then_inc(em_zero, 1)

            @block.vector
            def _(dve):
                steps = [0]

                def chain(ins):
                    steps[0] += 1
                    ins.then_inc(step, 1)
                    dve.wait_ge(step, steps[0])

                dve.wait_ge(new_in, 16)
                chain(dve.tensor_tensor(prodn[:, :], new[:, :DW], new[:, DW:2 * DW], ALU.mult))
                dve.tensor_reduce(znew[:, :], prodn[:, :].rearrange("p (n d) -> p n d", d=HD), AX_X, ALU.add).then_inc(znew_ready, 1)
                dve.wait_ge(q_in, 16 * NS)
                k = 0
                for g in range(NG):
                    dve.wait_ge(kv_in[g], 16 * NS)
                    for s in range(NS):
                        dve.tensor_tensor(prod[:, k % 2, :], kv[:, s, g, :GW], q[:, s, g * GW:(g + 1) * GW], ALU.mult).then_inc(prod_ready, 1)
                        dve.wait_ge(prod_ready, k + 1)
                        c = (s * NG + g) * GH
                        dve.tensor_reduce(z[:, c:c + GH], prod[:, k % 2, :].rearrange("p (h d) -> p h d", d=HD), AX_X, ALU.add).then_inc(z_ready, 1)
                        k += 1
                dve.wait_ge(zt_psum, 1)
                chain(dve.tensor_copy(zt[:, :P], pA[:NR, :P]))
                dve.wait_ge(znew_back, 16)
                chain(dve.tensor_reduce(mde[:, 0:1], zt[:, :], AX_X, ALU.max))
                dve.tensor_scalar(nmax[:, :], mde[:, 0:1], -1.0, None, ALU.mult).then_inc(nmax_ready, 1)
                dve.wait_ge(e_ready, 1)
                dve.tensor_copy(mde[:, 2:3], zt[:, P:P + 1]).then_inc(mde_ready, 1)
                dve.wait_ge(e_psum, 1)
                dve.wait_ge(em_zero, 1)
                for s in range(NS):
                    last = dve.tensor_copy(em[:, s, :, s], pB[:, s * 12:(s + 1) * 12])
                last.then_inc(em_ready, 1)
                dve.wait_ge(mde_back, 16)
                w3 = mden[:, :, 2:3].broadcast_to([NS, NG * GH, HD])
                chain(dve.tensor_tensor(vnew[:, :, :].rearrange("p g (h d) -> p (g h) d", d=HD),
                                        new[:, 2 * DW:].rearrange("p (n d) -> p n d", d=HD), w3, ALU.mult))
                dve.wait_ge(pv_done, 1)
                for g in range(NG):
                    dve.tensor_tensor(packed[:, g, :GW], pV[:NS, g // 2, (g % 2) * GW:(g % 2 + 1) * GW], vnew[:, g, :], ALU.add)
                for k in range(2):
                    last = dve.tensor_copy(packed[:, :, GW + k * GH:GW + (k + 1) * GH],
                                           mden[:, :, k].rearrange("p (g h) -> p g h", h=GH))
                last.then_inc(packed_ready, 1)

            @block.scalar
            def _(act):
                act.wait_ge(nmax_ready, 1)
                act.activation(zt[:, :], zt[:, :], ACT.Exp, bias=nmax[:, :], accum_out=mde[:, 1:2]).then_inc(e_ready, 1)

            @block.tensor
            def _(pe):
                pe.wait_ge(z_ready, NS * NG)
                pe.transpose(pA[:NR, :P], z[:, :], ident[:, :]).then_inc(zt_psum, 1)
                pe.wait_ge(e_ready, 1)
                pe.transpose(pB[:, :NR], zt[:, :P], ident[:NR, :NR]).then_inc(e_psum, 1)
                pe.wait_ge(em_ready, 1)
                for g in range(NG):
                    pe.wait_ge(kv_in[g], 16 * NS)
                    for h in range(GH):
                        for s in range(NS):
                            last = pe.matmul(pV[:NS, g // 2, (g % 2) * GW + h * HD:(g % 2) * GW + (h + 1) * HD],
                                             em[:, s, g * GH + h, :], kv[:, s, g, GW + h * HD:GW + (h + 1) * HD],
                                             start=(s == 0), stop=(s == NS - 1))
                last.then_inc(pv_done, 1)


def phase_prompt_window(nc, a, o, sc, ident, turned, odT):
    STEP = [min(d, S // P) for d in DIL]
    items = []
    for g in range(NG):
        for r in range(STEP[g]):
            for b in range(S // STEP[g] // P):
                items.append(dict(g=g, r=r, b=b, nk=2 if b else 1))
    NI = len(items)
    PW = GW + 2 * GH
    PR = 4
    ER = 3

    def tokens(ap, it, first_block, blocks):
        v = ap.rearrange("p (l r) -> p r l", r=STEP[it["g"]])
        return v[:, it["r"], first_block * P:(first_block + blocks) * P]

    def token_rows(ap, it, block):
        v = ap.rearrange("(l r) n -> r l n", r=STEP[it["g"]])
        return v[it["r"], block * P:(block + 1) * P, :]

    with ExitStack() as ctx:
        sb = lambda name, shape, dt=F32: ctx.enter_context(nc.sbuf_tensor(name, shape, dt))
        sem = sc["semaphore"]
        band = sb("band", [P, 2 * P])
        pairs = sb("pairs", [P, P])
        v = sb("v_win", [P, 3, 2, GW])
        e = sb("e_win", [P, ER, GH, 2 * P])
        nmax = sb("nmax2", [P, ER, GH])
        eT = sb("eT", [P, 2, GH * 2 * P])
        packed = sb("packed", [P, PR, PW])
        comb = sb("comb", [P, 2, NG, PW])
        top = sb("top", [P, GH])
        wg = sb("wg", [P, NG, GH])
        wd = sb("wd", [P, NG, GH])
        den = sb("den", [P, GH])
        part = sb("part", [P, NG, GW])
        mixed = sb("mixed", [P, 2, GW])
        pS = ctx.enter_context(nc.psum_tensor("pS_d", [P, 2, 2, GH // 2, 2 * P], F32))
        pT = ctx.enter_context(nc.psum_tensor("pT_d", [P, GH * 2 * P], F32))
        pO = ctx.enter_context(nc.psum_tensor("pO_d", [P, 2, 512], F32))
        consts_in = sem("d_consts_in")
        v_in = [sem(f"d_v_in{i}") for i in range(3)]
        packed_out = [sem(f"d_packed_out{i}") for i in range(PR)]
        comb_in = [sem(f"d_comb_in{i}") for i in range(2)]
        s_ready = sem("d_s_ready")
        s_masked = sem("d_s_masked")
        step = sem("d_step")
        nmax_ready = sem("d_nmax_ready")
        e_ready = sem("d_e_ready")
        eT_psum = sem("d_eT_psum")
        eT_ready = sem("d_eT_ready")
        pv_done = sem("d_pv_done")
        packed_ready = sem("d_packed_ready")
        wg_sub = sem("d_wg_sub")
        wg_ready = sem("d_wg_ready")
        mixed_ready = sem("d_mixed_ready")
        mixed_psum = sem("d_mixed_psum")
        odT_ready = sem("d_odT_ready")
        v_value = [16 * sum(items[j]["nk"] for j in range(i % 3, i + 1, 3)) for i in range(NI)]
        out_value = [16 * (i // PR + 1) for i in range(NI)]

        with nc.Block() as block:
            @block.sync
            def _(sp):
                sp.dma_start(band[:, :], a["band"]).then_inc(consts_in, 16)
                sp.dma_start(pairs[:, :], a["pairs"]).then_inc(consts_in, 16)
                for i in range(NI + 3):
                    if i < NI:
                        it = items[i]
                        g = it["g"]
                        if i >= 3:
                            sp.wait_ge(pv_done, i - 2)
                        for k in range(it["nk"]):
                            rows = token_rows(sc["dv"][:, g * GW:(g + 1) * GW], it, it["b"] - it["nk"] + 1 + k)
                            sp.dma_start(v[:, i % 3, k, :], rows).then_inc(v_in[i % 3], 16)
                    j = i - 3
                    if j >= 0:
                        it = items[j]
                        sp.wait_ge(packed_ready, j + 1)
                        sp.dma_start(token_rows(sc["od"][it["g"], :S, :], it, it["b"]), packed[:, j % PR, :]).then_inc(packed_out[j % PR], 16)
                for k in range(PR):
                    sp.wait_ge(packed_out[k], out_value[max(i for i in range(NI) if i % PR == k)])
                for t in range(NT):
                    m = rows_of(t)
                    if t >= 2:
                        sp.wait_ge(mixed_ready, t - 1)
                    sp.dma_start(comb[:m, t % 2, :, :], sc["od"][:, t * P:t * P + m, :].rearrange("g t n -> t g n")).then_inc(comb_in[t % 2], 16)

            @block.tensor
            def _(pe):
                for i in range(-1, NI + 2):
                    if i + 1 < NI:
                        it = items[i + 1]
                        g, nk = it["g"], it["nk"]
                        if i >= 1:
                            pe.wait_ge(s_masked, i)
                        for h in range(GH):
                            b = 64 * (h % 2)
                            qt = tokens(turned[b:b + 64, 8 + 2 * g + h // 2, :], it, it["b"], 1)
                            kt = tokens(turned[b:b + 64, 14 + 2 * g + h // 2, :], it, it["b"] - nk + 1, nk)
                            last = pe.matmul(pS[:, (i + 1) % 2, h % 2, h // 2, :nk * P], qt, kt, start=True, stop=True)
                        last.then_inc(s_ready, 1)
                    j = i - 1
                    if 0 <= j < NI:
                        nk = items[j]["nk"]
                        pe.wait_ge(e_ready, j + 1)
                        if j >= 1:
                            pe.wait_ge(eT_ready, j)
                        for h in range(GH):
                            for k in range(nk):
                                last = pe.transpose(pT[:, (h * nk + k) * P:(h * nk + k + 1) * P], e[:, j % ER, h, k * P:(k + 1) * P], ident[:, :])
                        last.then_inc(eT_psum, 1)
                    j = i - 2
                    if j >= 0:
                        nk = items[j]["nk"]
                        pe.wait_ge(eT_ready, j + 1)
                        pe.wait_ge(v_in[j % 3], v_value[j])
                        if j >= 2:
                            pe.wait_ge(packed_ready, j - 1)
                        for h in range(GH):
                            for k in range(nk):
                                last = pe.matmul(pO[:, j % 2, h * HD:(h + 1) * HD], eT[:, j % 2, (h * nk + k) * P:(h * nk + k + 1) * P],
                                                 v[:, j % 3, k, h * HD:(h + 1) * HD], start=(k == 0), stop=(k == nk - 1))
                        last.then_inc(pv_done, 1)
                for t in range(NT):
                    m = rows_of(t)
                    pe.wait_ge(mixed_ready, t + 1)
                    if t >= 2:
                        pe.wait_ge(odT_ready, t - 1)
                    for c in range(2):
                        last = pe.transpose(pO[:, t % 2, c * P:c * P + m], mixed[:m, t % 2, c * P:(c + 1) * P], ident[:m, :m])
                    last.then_inc(mixed_psum, 1)

            @block.scalar
            def _(act):
                for i in range(NI + 1):
                    if i < NI:
                        nk = items[i]["nk"]
                        act.wait_ge(nmax_ready, i + 1)
                        if i >= PR:
                            act.wait_ge(packed_out[i % PR], out_value[i - PR])
                        for h in range(GH):
                            last = act.activation(e[:, i % ER, h, :nk * P], e[:, i % ER, h, :nk * P], ACT.Exp, bias=nmax[:, i % ER, h:h + 1],
                                                  accum_out=packed[:, i % PR, GW + GH + h:GW + GH + h + 1])
                        last.then_inc(e_ready, 1)
                    j = i - 1
                    if j >= 0:
                        nk = items[j]["nk"]
                        act.wait_ge(eT_psum, j + 1)
                        if j >= 2:
                            act.wait_ge(pv_done, j - 1)
                        act.activation(eT[:, j % 2, :GH * nk * P], pT[:, :GH * nk * P], ACT.Copy).then_inc(eT_ready, 1)
                for t in range(NT + 1):
                    if t < NT:
                        m = rows_of(t)
                        act.wait_ge(wg_sub, t + 1)
                        act.activation(wg[:m, :, :], wg[:m, :, :], ACT.Exp).then_inc(wg_ready, 1)
                    if t >= 1:
                        u = t - 1
                        m = rows_of(u)
                        act.wait_ge(mixed_psum, u + 1)
                        act.activation(odT[:, :, u * P:u * P + m], pO[:, u % 2, :2 * P].rearrange("p (c t) -> p c t", c=2)[:, :, :m],
                                       ACT.Copy).then_inc(odT_ready, 1)

            @block.vector
            def _(dve):
                steps = [0]

                def chain(ins):
                    steps[0] += 1
                    ins.then_inc(step, 1)
                    dve.wait_ge(step, steps[0])

                dve.wait_ge(consts_in, 32)
                for i in range(NI + 3):
                    if i < NI:
                        it = items[i]
                        nk = it["nk"]
                        if it["g"] == 2:
                            mask = pairs[:, :]
                        else:
                            mask = band[:, (2 - nk) * P:]
                        dve.wait_ge(s_ready, i + 1)
                        if i >= ER:
                            dve.wait_ge(eT_psum, i - ER + 1)
                        ev = e[:, i % ER, :, :nk * P]
                        dve.tensor_tensor(e[:, i % ER, :, :nk * P].rearrange("p (a b) n -> p b a n", b=2), pS[:, i % 2, :, :, :nk * P],
                                          mask.unsqueeze(1).unsqueeze(1).broadcast_to([P, 2, GH // 2, nk * P]), ALU.add).then_inc(s_masked, 1)
                        dve.wait_ge(s_masked, i + 1)
                        if i >= PR:
                            dve.wait_ge(packed_out[i % PR], out_value[i - PR])
                        chain(dve.tensor_reduce(packed[:, i % PR, GW:GW + GH], ev, AX_X, ALU.max))
                        dve.tensor_scalar(nmax[:, i % ER, :], packed[:, i % PR, GW:GW + GH], -1.0, None, ALU.mult).then_inc(nmax_ready, 1)
                    j = i - 3
                    if j >= 0:
                        dve.wait_ge(pv_done, j + 1)
                        dve.tensor_copy(packed[:, j % PR, :GW], pO[:, j % 2, :GW]).then_inc(packed_ready, 1)
                for t in range(NT):
                    m = rows_of(t)
                    cb = comb[:m, t % 2, :, :]
                    dve.wait_ge(comb_in[t % 2], 16 * (t // 2 + 1))
                    chain(dve.tensor_tensor(top[:m, :], cb[:, 0, GW:GW + GH], cb[:, 1, GW:GW + GH], ALU.max))
                    chain(dve.tensor_tensor(top[:m, :], top[:m, :], cb[:, 2, GW:GW + GH], ALU.max))
                    dve.tensor_tensor(wg[:m, :, :], cb[:, :, GW:GW + GH], top[:m, :].unsqueeze(1).broadcast_to([m, NG, GH]), ALU.subtract).then_inc(wg_sub, 1)
                    dve.wait_ge(wg_ready, t + 1)
                    chain(dve.tensor_tensor(wd[:m, :, :], wg[:m, :, :], cb[:, :, GW + GH:], ALU.mult))
                    chain(dve.tensor_tensor(den[:m, :], wd[:m, 0, :], wd[:m, 1, :], ALU.add))
                    chain(dve.tensor_tensor(den[:m, :], den[:m, :], wd[:m, 2, :], ALU.add))
                    chain(dve.reciprocal(den[:m, :], den[:m, :]))
                    chain(dve.tensor_tensor(wg[:m, :, :], wg[:m, :, :], den[:m, :].unsqueeze(1).broadcast_to([m, NG, GH]), ALU.mult))
                    for g in range(NG):
                        last = dve.tensor_tensor(part[:m, g, :].rearrange("p (h d) -> p h d", d=HD), cb[:, g, :GW].rearrange("p (h d) -> p h d", d=HD),
                                                 wg[:m, g, :].unsqueeze(2).broadcast_to([m, GH, HD]), ALU.mult)
                    chain(last)
                    if t >= 2:
                        dve.wait_ge(mixed_psum, t - 1)
                    chain(dve.tensor_tensor(part[:m, 0, :], part[:m, 0, :], part[:m, 1, :], ALU.add))
                    dve.tensor_tensor(mixed[:m, t % 2, :], part[:m, 0, :], part[:m, 2, :], ALU.add).then_inc(mixed_ready, 1)


def phase_gate(nc, a, o, sc, turned, oT, odT):
    NC = T // 3
    G0 = 3 * SBW + 3 * DW
    flat = turned[:, :, :].rearrange("p a b -> p (a b)")
    hT = flat[:, :KC * T].rearrange("p (c t) -> p c t", c=KC)
    mixT = flat[:, KC * T:2 * KC * T].rearrange("p (c t) -> p c t", c=KC)
    w_view = a["w_in"][0].rearrange("(p c) n -> p c n", c=KC)
    NI = KC * 3
    with ExitStack() as ctx:
        sb = lambda name, shape, dt=F32: ctx.enter_context(nc.sbuf_tensor(name, shape, dt))
        sem = sc["semaphore"]
        wg = sb("w_gates", [P, 2, 2, KC, 2 * P])
        wa = sb("w_a", [P, SBW // P, D])
        wb = sb("w_b", [P, GW // P, D])
        sig = sb("sig", [P, 2, 2, NC])
        half = sb("halves", [P, 2, 2, NC])
        zero = sb("zero", [P, D])
        pG = ctx.enter_context(nc.psum_tensor("pG", [P, 2, 4, 512], F32))
        h_in = sem("g_h_in")
        br_in = sem("g_br_in")
        w_loaded = [sem(f"g_w_loaded{i}") for i in range(2)]
        gates_ready = sem("g_gates_ready")
        br_ready = sem("g_br_ready")
        sig_ready = sem("g_sig_ready")
        half_ready = sem("g_half_ready")
        mix_ready = sem("g_mix_ready")
        zero_set = sem("g_zero_set")
        zero_out = sem("g_zero_out")
        with nc.Block() as block:
            @block.sync
            def _(sp):
                sp.dma_start(flat[:, :KC * T], sc["ht"]).then_inc(h_in, 16)
                for u in range(KC // 2):
                    if u >= 2:
                        sp.wait_ge(gates_ready, 6 * (u - 1))
                    for k in range(2):
                        c0 = G0 + k * D + u * 2 * P
                        sp.dma_start(wg[:, u % 2, k, :, :], w_view[:, :, c0:c0 + 2 * P]).then_inc(w_loaded[u % 2], 16)
                    if u == 0:
                        sp.dma_start(wa[:, :, :], a["w_br_a"][0].rearrange("(c p) n -> p c n", p=P)).then_inc(br_in, 16)
                        sp.dma_start(wb[:, :, :], a["w_br_b"][0].rearrange("(c p) n -> p c n", p=P)).then_inc(br_in, 16)
                spare = sc["y"][SURE * BLK:, :].rearrange("(n p a) d -> n p a d", p=P, n=WHOLE * BLK // P)
                sp.wait_ge(zero_set, 1)
                for n in range(spare.shape[0]):
                    sp.dma_start(spare[n], zero[:, :].unsqueeze(1).broadcast_to([P, spare.shape[2], D])).then_inc(zero_out, 16)
                sp.wait_ge(zero_out, 16 * spare.shape[0])

            @block.tensor
            def _(pe):
                pe.wait_ge(h_in, 16)
                for i in range(NI):
                    f, n = divmod(i, 3)
                    cols = slice(n * NC, (n + 1) * NC)
                    if n == 0 and f % 2 == 0:
                        pe.wait_ge(w_loaded[f // 2 % 2], 32 * (f // 4 + 1))
                    if i >= 2:
                        pe.wait_ge(half_ready, 2 * (i - 1))
                    for k in range(2):
                        for c in range(KC):
                            last = pe.matmul(pG[:, i % 2, k, :NC], wg[:, f // 2 % 2, k, c, (f % 2) * P:(f % 2 + 1) * P], hT[:, c, cols],
                                             start=(c == 0), stop=(c == KC - 1))
                    last.then_inc(gates_ready, 1)
                    if i == 0:
                        pe.wait_ge(br_in, 32)
                    for k, (w, x, nk) in enumerate(((wa, oT, SBW // P), (wb, odT, GW // P))):
                        for c in range(nk):
                            last = pe.matmul(pG[:, i % 2, 2 + k, :NC], w[:, c, f * P:(f + 1) * P], x[:, c, cols],
                                             start=(c == 0), stop=(c == nk - 1))
                    last.then_inc(br_ready, 1)

            @block.scalar
            def _(act):
                for i in range(NI):
                    act.wait_ge(gates_ready, i + 1)
                    if i >= 2:
                        act.wait_ge(half_ready, 2 * (i - 1))
                    for k in range(2):
                        last = act.activation(sig[:, i % 2, k, :], pG[:, i % 2, k, :NC], ACT.Sigmoid)
                    last.then_inc(sig_ready, 1)

            @block.vector
            def _(dve):
                for i in range(NI):
                    dve.wait_ge(br_ready, i + 1)
                    dve.wait_ge(sig_ready, i + 1)
                    if i >= 2:
                        dve.wait_ge(mix_ready, i - 1)
                    for k in range(2):
                        dve.tensor_tensor(half[:, i % 2, k, :], sig[:, i % 2, k, :], pG[:, i % 2, 2 + k, :NC], ALU.mult).then_inc(half_ready, 1)

            @block.gpsimd
            def _(pool):
                pool.memset(zero[:, :], 0.0).then_inc(zero_set, 1)
                for i in range(NI):
                    f, n = divmod(i, 3)
                    pool.wait_ge(half_ready, 2 * (i + 1))
                    pool.tensor_tensor(mixT[:, f, n * NC:(n + 1) * NC], half[:, i % 2, 0, :], half[:, i % 2, 1, :], ALU.add).then_inc(mix_ready, 1)


def phase_out(nc, a, o, sc, ident, turned, scores):
    flat = turned[:, :, :].rearrange("p a b -> p (a b)")
    h2T = flat[:, :KC * T].rearrange("p (c t) -> p c t", c=KC)
    mixT = flat[:, KC * T:2 * KC * T].rearrange("p (c t) -> p c t", c=KC)
    with ExitStack() as ctx:
        sb = lambda name, shape, dt=F32: ctx.enter_context(nc.sbuf_tensor(name, shape, dt))
        sem = sc["semaphore"]
        wo = sb("w_o", [P, KC, D])
        wr = sb("w_r", [P, KC, E])
        gain = sb("gain2", [P, D])
        x = sb("x_again", [P, 2, D])
        x1 = sb("x1", [P, 2, D])
        h2 = sb("h2", [P, 2, D])
        junk = sb("junk2", [P, D])
        zero = sb("zero_row", [1, D])
        ss = sb("ss2", [P, NT])
        rms = sb("rms2", [P, NT])
        rstd = sb("rstd2", [P, NT])
        eps = sb("eps2", [P, 1])
        pY = ctx.enter_context(nc.psum_tensor("pY", [P, 2, D], F32))
        pT = ctx.enter_context(nc.psum_tensor("pT2", [P, D], F32))
        pR = ctx.enter_context(nc.psum_tensor("pR", [P, 2, 512], F32))
        w_in = sem("o_w_in")
        x_in = [sem(f"o_x_in{i}") for i in range(2)]
        stored = [sem(f"o_stored{i}") for i in range(2)]
        zero_out = sem("o_zero_out")
        set_up = sem("o_set_up")
        step = sem("o_step")
        y_ready = sem("o_y_ready")
        x1_ready = sem("o_x1_ready")
        ss_ready = sem("o_ss_ready")
        rms_ready = sem("o_rms_ready")
        h2_ready = sem("o_h2_ready")
        h2T_psum = sem("o_h2T_psum")
        h2T_ready = sem("o_h2T_ready")
        logits_ready = sem("o_logits_ready")
        scores_ready = sem("o_scores_ready")
        with nc.Block() as block:
            @block.sync
            def _(sp):
                sp.dma_start(wo[:, :, :], a["w_out"][0].rearrange("(c p) n -> p c n", p=P)).then_inc(w_in, 16)
                sp.dma_start(gain[:, :], a["norm2_g"].broadcast_to([P, D])).then_inc(w_in, 16)
                sp.dma_start(wr[:, :, :], a["w_router"][0].rearrange("(p c) n -> p c n", c=KC)).then_inc(w_in, 16)
                sp.wait_ge(set_up, 3)
                sp.dma_start(sc["h2"][T:T + 1, :], zero[:, :]).then_inc(zero_out, 16)
                for t in range(NT + 1):
                    if t < NT:
                        m = rows_of(t)
                        if t >= 2:
                            sp.wait_ge(x1_ready, t - 1)
                        src = a["x_prompt"][0, t * P:t * P + P] if t < NT - 1 else a["x_sample"][:, 0]
                        sp.dma_start(x[:m, t % 2, :], src).then_inc(x_in[t % 2], 16)
                    if t >= 1:
                        u = t - 1
                        m = rows_of(u)
                        sp.wait_ge(h2_ready, u + 1)
                        sp.dma_start(sc["x1"][u * P:u * P + m, :], x1[:m, u % 2, :]).then_inc(stored[u % 2], 16)
                        sp.dma_start(sc["h2"][u * P:u * P + m, :], h2[:m, u % 2, :]).then_inc(stored[u % 2], 16)
                for i in range(2):
                    sp.wait_ge(stored[i], 32 * len(range(i, NT, 2)))
                sp.wait_ge(zero_out, 16)

            @block.gpsimd
            def _(pool):
                pool.memset(eps[:, :], EPS).then_inc(set_up, 1)
                pool.memset(zero[:, :], 0.0).then_inc(set_up, 1)
                pool.memset(scores[:, :, :], 0.5).then_inc(set_up, 1)

            @block.tensor
            def _(pe):
                pe.wait_ge(w_in, 48)
                for t in range(NT + 2):
                    if t < NT:
                        m = rows_of(t)
                        if t >= 2:
                            pe.wait_ge(x1_ready, t - 1)
                        for k in range(2):
                            for c in range(KC):
                                last = pe.matmul(pY[:m, t % 2, k * 512:(k + 1) * 512], mixT[:, c, t * P:t * P + m], wo[:, c, k * 512:(k + 1) * 512],
                                                 start=(c == 0), stop=(c == KC - 1))
                        last.then_inc(y_ready, 1)
                    u = t - 1
                    if 0 <= u < NT:
                        m = rows_of(u)
                        pe.wait_ge(h2_ready, u + 1)
                        if u >= 1:
                            pe.wait_ge(h2T_ready, u)
                        hv = h2[:m, u % 2, :].rearrange("p (q c) -> p c q", c=KC)
                        for c in range(KC):
                            last = pe.transpose(pT[:, c * P:c * P + m], hv[:, c, :], ident[:m, :m])
                        last.then_inc(h2T_psum, 1)
                    u = t - 2
                    if u >= 0:
                        m = rows_of(u)
                        pe.wait_ge(h2T_ready, u + 1)
                        for c in range(KC):
                            last = pe.matmul(pR[:m, u // 8, (u % 8) * E:(u % 8 + 1) * E], h2T[:, c, u * P:u * P + m], wr[:, c, :],
                                             start=(c == 0), stop=(c == KC - 1))
                        last.then_inc(logits_ready, 1)

            @block.scalar
            def _(act):
                act.wait_ge(set_up, 3)
                for t in range(NT + 1):
                    if t < NT:
                        m = rows_of(t)
                        act.wait_ge(x1_ready, t + 1)
                        act.activation(junk[:m, :], x1[:m, t % 2, :], ACT.Square, accum_out=ss[:m, t:t + 1]).then_inc(ss_ready, 1)
                        act.wait_ge(ss_ready, t + 1)
                        act.activation(rms[:m, t:t + 1], ss[:m, t:t + 1], ACT.Sqrt, scale=1.0 / D, bias=eps[:m, :]).then_inc(rms_ready, 1)
                    if t >= 1:
                        u = t - 1
                        m = rows_of(u)
                        act.wait_ge(h2T_psum, u + 1)
                        act.activation(h2T[:, :, u * P:u * P + m], pT[:, :].rearrange("p (c t) -> p c t", t=P)[:, :, :m], ACT.Copy).then_inc(h2T_ready, 1)
                act.wait_ge(logits_ready, NT)
                act.activation(scores[:, :8, :].rearrange("p t e -> p (t e)"), pR[:, 0, :], ACT.Sigmoid).then_inc(scores_ready, 1)
                act.activation(scores[:NS, 8, :], pR[:NS, 1, :E], ACT.Sigmoid).then_inc(scores_ready, 1)

            @block.vector
            def _(dve):
                steps = [0]

                def chain(ins):
                    steps[0] += 1
                    ins.then_inc(step, 1)
                    dve.wait_ge(step, steps[0])

                dve.wait_ge(w_in, 48)
                for t in range(NT):
                    m = rows_of(t)
                    dve.wait_ge(y_ready, t + 1)
                    dve.wait_ge(x_in[t % 2], 16 * (t // 2 + 1))
                    if t >= 2:
                        dve.wait_ge(stored[t % 2], 32 * (t // 2))
                    dve.tensor_tensor(x1[:m, t % 2, :], pY[:m, t % 2, :], x[:m, t % 2, :], ALU.add).then_inc(x1_ready, 1)
                    dve.wait_ge(rms_ready, t + 1)
                    chain(dve.reciprocal(rstd[:m, t:t + 1], rms[:m, t:t + 1]))
                    if t >= 2:
                        dve.wait_ge(h2T_psum, t - 1)
                    dve.scalar_tensor_tensor(h2[:m, t % 2, :], x1[:m, t % 2, :], rstd[:m, t:t + 1], gain[:m, :], ALU.mult, ALU.mult).then_inc(h2_ready, 1)


def phase_route(nc, a, o, sc, ident, turned, scores, dest, weight, expert_row, slot_token, slot_token_tail):
    NC = T // 3
    NF = DE // P
    NGU = 3 * NF
    EARLY = NGU // 2
    h2T = turned[:, :, :].rearrange("p a b -> p (a b)")[:, :KC * T].rearrange("p (c t) -> p c t", c=KC)
    with ExitStack() as ctx:
        sb = lambda name, shape, dt=F32: ctx.enter_context(nc.sbuf_tensor(name, shape, dt))
        sem = sc["semaphore"]
        rbias = sb("rbias", [P, E])
        before = sb("before_r", [P, P])
        ones = sb("ones_r", [P, P])
        earlier = sb("earlier", [P, EG, EG])
        valid = sb("valid", [P, NT])
        number = sb("number", [P, 1])
        tokid = sb("tokid", [P, NT], I32)
        sel = sb("sel", [P, NT, E])
        tops = sb("tops", [P, NT * EG, 8])
        grp = sb("grp", [P, NT, EG])
        gt = sb("gt", [P, NT, EG, EG])
        eq = sb("eq", [P, NT, EG, EG])
        rank = sb("rank", [P, NT, EG])
        gpen = sb("gpen", [P, NT, EG])
        best = sb("best", [P, NT, 8])
        marked = sb("marked", [P, NT, E])
        mask = sb("mask", [P, NT, E])
        w = sb("w_r8", [P, NT, E])
        wsum = sb("wsum", [P, NT])
        cum = sb("cum", [P, NT + 1, E])
        count = sb("count", [P, E])
        nblk = sb("nblk", [P, E])
        end = sb("end", [P, E])
        begin = sb("begin", [P, E])
        slot = sb("slot", [P, NT, E])
        d8 = sb("d8", [P, NT, 8])
        hit = sb("hit", [P, E])
        picked = sb("picked", [P, NT * TOPK, E])
        eb = sb("eb", [P, 2])
        ebi = sb("ebi", [P, 1], I32)
        turn_first = sb("turn_first", [P, NBLK // TURN])
        turn_used = sb("turn_used", [P, NBLK // TURN])
        turns = sb("turns", [P, 1])
        turnsi = sb("turnsi", [P, 1], I32)
        fill = sb("fill", [NBLK, BLK], I32)
        table = sb("table", [NBLK, BLK], I32)
        tablef = sb("tablef", [NBLK, BLK])
        pP = ctx.enter_context(nc.psum_tensor("pP_r", [P, 2, 512], F32))
        pC = ctx.enter_context(nc.psum_tensor("pC_r", [P, 512], F32))
        pT = ctx.enter_context(nc.psum_tensor("pT_r", [P, 512], F32))
        wgu = sb("ws_gu", [P, 2, KC, DE])
        wd = sb("ws_d", [P, NF, D])
        silu = sb("silu_s", [P, 2, NC])
        up = sb("up_s", [P, 2, NC])
        hid = sb("hid_s", [P, NF, T])
        x1 = sb("x1_again", [P, 2, D])
        x2 = sb("x2", [P, 2, D])
        pG = ctx.enter_context(nc.psum_tensor("pG_s", [P, 2, 2, 512], F32))
        pY = pG[:, :, :, :].rearrange("p a b n -> p a (b n)")
        w_in = sem("h_w_in")
        x_in = [sem(f"h_x_in{i}") for i in range(2)]
        stored = [sem(f"h_stored{i}") for i in range(2)]
        gu_ready = sem("h_gu_ready")
        silu_ready = sem("h_silu_ready")
        hid_ready = sem("h_hid_ready")
        hid_late = sem("h_hid_late")
        y_ready = sem("h_y_ready")
        x2_ready = sem("h_x2_ready")
        consts_in = sem("r_consts_in")
        fill_set = sem("r_fill_set")
        fill_out = sem("r_fill_out")
        step = sem("r_step")
        mask_ready = sem("r_mask_ready")
        cum_ready = sem("r_cum_ready")
        pos_ready = sem("r_pos_ready")
        dest_ready = sem("r_dest_ready")
        scattered = sem("r_scattered")
        eb_ready = sem("r_eb_ready")
        eb_out = sem("r_eb_out")
        eb_back = sem("r_eb_back")
        table_in = sem("r_table_in")
        tablef_ready = sem("r_tablef_ready")
        table_psum = sem("r_table_psum")
        slots_ready = sem("r_slots_ready")
        with nc.Block() as block:
            @block.sync
            def _(sp):
                for dst, src in ((before[:, :], a["before"]), (ones[:, :], a["ones"]), (earlier[:, :, :], a["earlier"]),
                                 (valid[:, :], a["valid"]), (number[:, :], a["number"]), (tokid[:, :], a["tokid"]), (turn_first[:, :], a["turn_first"]),
                                 (rbias[:, :], a["router_bias"].broadcast_to([P, E]))):
                    sp.dma_start(dst, src).then_inc(consts_in, 16)
                for k, name in enumerate(("w_s_gate", "w_s_up")):
                    sp.dma_start(wgu[:, k, :, :], a[name][0].rearrange("(p c) f -> p c f", c=KC)).then_inc(w_in, 16)
                sp.dma_start(wd[:, :, :], a["w_s_down"][0].rearrange("(c p) n -> p c n", p=P)).then_inc(w_in, 16)
                sp.wait_ge(fill_set, 1)
                sp.dma_start(sc["table"].rearrange("(b p) a -> b (p a)", b=NBLK), fill[:, :]).then_inc(fill_out, 16)
                sp.wait_ge(eb_ready, 2)
                sp.dma_start(sc["eb"][:, :NBLK].rearrange("a n -> n a"), ebi[:NBLK, :], allow_slow_non_contiguous=True).then_inc(eb_out, 16)
                sp.dma_start(sc["eb"][:, NBLK:], turnsi[0:1, :]).then_inc(eb_out, 16)
                sp.wait_ge(eb_out, 32)
                sp.dma_start(expert_row[:, :], sc["eb"]).then_inc(eb_back, 16)
                for t in range(NT + 1):
                    if t < NT:
                        m = rows_of(t)
                        if t >= 2:
                            sp.wait_ge(x2_ready, t - 1)
                        sp.dma_start(x1[:m, t % 2, :], sc["x1"][t * P:t * P + m, :]).then_inc(x_in[t % 2], 16)
                    if t >= 1:
                        u = t - 1
                        m = rows_of(u)
                        sp.wait_ge(x2_ready, u + 1)
                        sp.dma_start(sc["x2"][u * P:u * P + m, :], x2[:m, u % 2, :]).then_inc(stored[u % 2], 16)
                for i in range(2):
                    sp.wait_ge(stored[i], 16 * len(range(i, NT, 2)))
                sp.wait_ge(scattered, 16 * NT * TOPK)
                sp.dma_start(table[:, :], sc["table"].rearrange("(b p) a -> b (p a)", b=NBLK)).then_inc(table_in, 16)
                sp.wait_ge(eb_back, 16)

            @block.gpsimd
            def _(pool):
                pool.memset(fill[:, :], T).then_inc(fill_set, 1)
                for i in range(EARLY):
                    n, f = divmod(i, NF)
                    pool.wait_ge(silu_ready, i + 1)
                    pool.tensor_tensor(hid[:, f, n * NC:(n + 1) * NC], silu[:, i % 2, :], up[:, i % 2, :], ALU.mult).then_inc(hid_ready, 1)
                pool.wait_ge(consts_in, 8 * 16)
                pool.wait_ge(fill_out, 16)
                pool.wait_ge(dest_ready, 1)
                for t in range(NT):
                    m = rows_of(t)
                    for k in range(TOPK):
                        pool.indirect_dma_start(sc["table"], bass.IndirectOffsetOnAxis(ap=dest[:m, t * 8 + k:t * 8 + k + 1], axis=0),
                                                tokid[:m, t:t + 1], None).then_inc(scattered, 16)

            @block.scalar
            def _(act):
                for i in range(NGU):
                    act.wait_ge(gu_ready, i + 1)
                    if i >= 2:
                        if i - 2 < EARLY:
                            act.wait_ge(hid_ready, i - 1)
                        else:
                            act.wait_ge(hid_late, i - 1 - EARLY)
                    act.activation(silu[:, i % 2, :], pG[:, i % 2, 0, :NC], ACT.Silu)
                    act.activation(up[:, i % 2, :], pG[:, i % 2, 1, :NC], ACT.Copy).then_inc(silu_ready, 1)

            @block.tensor
            def _(pe):
                def gate_up(i):
                    n, f = divmod(i, NF)
                    if i >= 2:
                        pe.wait_ge(silu_ready, i - 1)
                    for k in range(2):
                        for c in range(KC):
                            last = pe.matmul(pG[:, i % 2, k, :NC], wgu[:, k, c, f * P:(f + 1) * P], h2T[:, c, n * NC:(n + 1) * NC],
                                             start=(c == 0), stop=(c == KC - 1))
                    last.then_inc(gu_ready, 1)

                pe.wait_ge(w_in, 48)
                for i in range(EARLY):
                    gate_up(i)
                pe.wait_ge(consts_in, 8 * 16)
                pe.wait_ge(cum_ready, 1)
                for t in range(NT):
                    out = pP[:, t // 8, (t % 8) * E:(t % 8 + 1) * E]
                    pe.matmul(out, before[:, :], mask[:, t, :], start=True, stop=False)
                    last = pe.matmul(out, ones[:, :], cum[:, t, :], start=False, stop=True)
                last = pe.matmul(pC[:, :E], ones[:, :], cum[:, NT, :], start=True, stop=True)
                last.then_inc(pos_ready, 1)
                for i in range(EARLY, NGU):
                    gate_up(i)
                pe.wait_ge(silu_ready, NGU)
                pe.wait_ge(hid_ready, EARLY)
                pe.wait_ge(hid_late, NGU - EARLY)
                for t in range(NT):
                    m = rows_of(t)
                    if t >= 2:
                        pe.wait_ge(x2_ready, t - 1)
                    for k in range(2):
                        for f in range(NF):
                            last = pe.matmul(pY[:m, t % 2, k * 512:(k + 1) * 512], hid[:, f, t * P:t * P + m], wd[:, f, k * 512:(k + 1) * 512],
                                             start=(f == 0), stop=(f == NF - 1))
                    last.then_inc(y_ready, 1)
                pe.wait_ge(tablef_ready, 1)
                pe.transpose(pT[:, :NBLK], tablef[:, :P], ident[:NBLK, :NBLK])
                pe.transpose(pT[:BLK - P, P:P + NBLK], tablef[:, P:], ident[:NBLK, :NBLK]).then_inc(table_psum, 1)

            @block.vector
            def _(dve):
                steps = [0]

                def chain(ins):
                    steps[0] += 1
                    ins.then_inc(step, 1)
                    dve.wait_ge(step, steps[0])

                dve.wait_ge(consts_in, 8 * 16)
                bc = lambda ap, shape: ap.broadcast_to(shape)
                chain(dve.tensor_tensor(sel[:, :, :], scores[:, :, :], bc(rbias[:, :].unsqueeze(1), [P, NT, E]), ALU.add))
                for j in range(NT * EG):
                    last = dve.max(tops[:, j, :], sel[:, j // EG, (j % EG) * PER:(j % EG + 1) * PER])
                chain(last)
                chain(dve.tensor_tensor(grp[:, :, :].rearrange("p t g -> p (t g)"), tops[:, :, 0], tops[:, :, 1], ALU.add))
                for t in range(NT):
                    this, other = bc(grp[:, t, :].unsqueeze(2), [P, EG, EG]), bc(grp[:, t, :].unsqueeze(1), [P, EG, EG])
                    dve.tensor_tensor(gt[:, t, :, :], other, this, ALU.is_gt)
                    last = dve.tensor_tensor(eq[:, t, :, :], other, this, ALU.is_equal)
                chain(last)
                chain(dve.tensor_tensor(eq[:, :, :, :], eq[:, :, :, :], bc(earlier[:, :, :].unsqueeze(1), [P, NT, EG, EG]), ALU.mult))
                chain(dve.tensor_tensor(gt[:, :, :, :], gt[:, :, :, :], eq[:, :, :, :], ALU.add))
                chain(dve.tensor_reduce(rank[:, :, :].rearrange("p t g -> p (t g)"), gt[:, :, :, :].rearrange("p t g h -> p (t g) h"), AX_X, ALU.add))
                chain(dve.tensor_scalar(rank[:, :, :], rank[:, :, :], float(TOPG), None, ALU.is_lt))
                chain(dve.tensor_scalar(gpen[:, :, :], rank[:, :, :], BIG, -BIG, ALU.mult, ALU.add))
                s4 = sel[:, :, :].rearrange("p t (g e) -> p (t g) e", e=PER)
                r4 = bc(rank[:, :, :].rearrange("p t g -> p (t g)").unsqueeze(2), [P, NT * EG, PER])
                g4 = bc(gpen[:, :, :].rearrange("p t g -> p (t g)").unsqueeze(2), [P, NT * EG, PER])
                chain(dve.tensor_tensor(s4, s4, r4, ALU.mult))
                chain(dve.tensor_tensor(s4, s4, g4, ALU.add))
                for t in range(NT):
                    last = dve.max(best[:, t, :], sel[:, t, :])
                chain(last)
                for t in range(NT):
                    last = dve.match_replace(marked[:, t, :], best[:, t, :], sel[:, t, :], BIG)
                chain(last)
                chain(dve.tensor_scalar(mask[:, :, :], marked[:, :, :], 0.5 * BIG, None, ALU.is_ge))
                chain(dve.tensor_tensor(mask[:, :, :], mask[:, :, :], bc(valid[:, :].unsqueeze(2), [P, NT, E]), ALU.mult))
                chain(dve.tensor_tensor(w[:, :, :], scores[:, :, :], mask[:, :, :], ALU.mult))
                chain(dve.tensor_reduce(wsum[:, :], w[:, :, :], AX_X, ALU.add))
                chain(dve.scalar_tensor_tensor(wsum[:, :], wsum[:, :], 1.0, valid[:, :], ALU.add, ALU.subtract))
                chain(dve.reciprocal(wsum[:, :], wsum[:, :]))
                chain(dve.tensor_tensor(w[:, :, :], w[:, :, :], bc(wsum[:, :].unsqueeze(2), [P, NT, E]), ALU.mult))
                chain(dve.tensor_scalar(w[:, :, :], w[:, :, :], 2.5, None, ALU.mult))
                chain(dve.memset(cum[:, 0, :], 0.0))
                for t in range(NT):
                    ins = dve.tensor_tensor(cum[:, t + 1, :], cum[:, t, :], mask[:, t, :], ALU.add)
                    if t < NT - 1:
                        chain(ins)
                ins.then_inc(cum_ready, 1)
                dve.wait_ge(pos_ready, 1)
                chain(dve.tensor_copy(count[:, :], pC[:, :E]))
                chain(dve.memset(nblk[:, :], 0.0))
                for j in range(-(-T // BLK)):
                    chain(dve.scalar_tensor_tensor(nblk[:, :], count[:, :], float(j * BLK), nblk[:, :], ALU.is_gt, ALU.add))
                chain(dve.tensor_tensor_scan(end[:, :], ones[:, :E], nblk[:, :], 0.0, ALU.mult, ALU.add))
                chain(dve.tensor_scalar(hit[:, :], end[:, :], number[:, 0:1], None, ALU.is_le))
                chain(dve.tensor_reduce(eb[:, 0:1], hit[:, :], AX_X, ALU.add))
                chain(dve.tensor_scalar(eb[:, 1:2], eb[:, 0:1], float(E - 1), None, ALU.min))
                chain(dve.tensor_scalar(turn_used[:, :], turn_first[:, :], end[:, E - 1:E], None, ALU.is_lt))
                chain(dve.tensor_reduce(turns[:, :], turn_used[:, :], AX_X, ALU.add))
                dve.tensor_copy(ebi[:, :], eb[:, 1:2]).then_inc(eb_ready, 1)
                dve.tensor_scalar(turnsi[:, :], turns[:, :], -2.0, None, ALU.add).then_inc(eb_ready, 1)
                chain(dve.tensor_tensor(begin[:, :], end[:, :], nblk[:, :], ALU.subtract))
                chain(dve.tensor_scalar(begin[:, :], begin[:, :], float(BLK), 1.0, ALU.mult, ALU.add))
                chain(dve.tensor_tensor(slot[:, :8, :], pP[:, 0, :].rearrange("p (t e) -> p t e", e=E), bc(begin[:, :].unsqueeze(1), [P, 8, E]), ALU.add))
                chain(dve.tensor_tensor(slot[:, 8, :], pP[:, 1, :E], begin[:, :], ALU.add))
                chain(dve.tensor_tensor(slot[:, :, :], slot[:, :, :], mask[:, :, :], ALU.mult))
                for t in range(NT):
                    last = dve.max(d8[:, t, :], slot[:, t, :])
                chain(last)
                dve.tensor_scalar(dest[:, :], d8[:, :, :].rearrange("p t k -> p (t k)"), -1.0, None, ALU.add).then_inc(dest_ready, 1)

                def late_hid(i):
                    n, f = divmod(i, NF)
                    dve.wait_ge(silu_ready, i + 1)
                    dve.tensor_tensor(hid[:, f, n * NC:(n + 1) * NC], silu[:, i % 2, :], up[:, i % 2, :], ALU.mult).then_inc(hid_late, 1)

                late_hid(EARLY)
                for t in range(NT):
                    for k in range(TOPK):
                        j = t * TOPK + k
                        dve.scalar_tensor_tensor(picked[:, j, :], slot[:, t, :], d8[:, t, k:k + 1], w[:, t, :], ALU.is_equal, ALU.mult,
                                                 accum_out=weight[:, j:j + 1])
                for i in range(EARLY + 1, NGU):
                    late_hid(i)
                for t in range(NT):
                    m = rows_of(t)
                    dve.wait_ge(y_ready, t + 1)
                    dve.wait_ge(x_in[t % 2], 16 * (t // 2 + 1))
                    if t >= 2:
                        dve.wait_ge(stored[t % 2], 16 * (t // 2))
                    dve.tensor_tensor(x2[:m, t % 2, :], pY[:m, t % 2, :], x1[:m, t % 2, :], ALU.add).then_inc(x2_ready, 1)
                dve.wait_ge(table_in, 16)
                dve.tensor_copy(tablef[:, :], table[:, :]).then_inc(tablef_ready, 1)
                dve.wait_ge(table_psum, 1)
                dve.tensor_copy(slot_token[:, :], pT[:, :NBLK]).then_inc(slots_ready, 1)
                dve.tensor_copy(slot_token_tail[:, :], pT[:BLK - P, P:P + NBLK]).then_inc(slots_ready, 1)
                dve.wait_ge(slots_ready, 2)


def phase_experts(nc, a, o, sc, ident, expert_row, slot_token, slot_token_tail):
    U = TURN
    NF = DE // P
    TAIL = BLK - P
    SKIP = P - TAIL
    CH = (3, 3, 2)
    C0 = (0, 3, 6)
    w_views = [a[n][0].rearrange("e (p c) f -> e p (c f)", p=P) for n in ("w_e_gate", "w_e_up", "w_e_down")]
    with ExitStack() as ctx:
        sb = lambda name, shape, dt=F32: ctx.enter_context(nc.sbuf_tensor(name, shape, dt))
        sem = sc["semaphore"]
        w = sb("w_e", [P, 2, 3, KC * DE])
        whi = sb("w_e_hi", [P, 2, NF * D], F32R)
        wlo = sb("w_e_lo", [P, 2, NF * D], F32R)
        index = sb("index", [P, 2, 2], I32)
        rows = sb("rows", [P, 2, D])
        tail = sb("rows_tail", [TAIL, 2, D])
        xT = sb("xT", [P, 2, KC, BLK])
        silu = sb("silu_e", [P, NF, BLK])
        hid = sb("hid_e", [P, NF, BLK])
        hhi = sb("hid_hi", [P, 2, NF, BLK], F32R)
        hlo = sb("hid_lo", [P, 2, NF, BLK], F32R)
        y = sb("y_e", [P, 2, D])
        pX = ctx.enter_context(nc.psum_tensor("pX", [P, 2, 512], F32))
        pG = ctx.enter_context(nc.psum_tensor("pG_e", [P, 2, 512], F32))
        pY = ctx.enter_context(nc.psum_tensor("pY_e", [P, 2, D], F32))
        w_in = [[sem(f"e_w_in{k}{i}") for i in range(2)] for k in range(3)]
        rows_in = [sem(f"e_rows_in{i}") for i in range(2)]
        y_out = sem("e_y_out")
        index_ready = sem("e_index_ready")
        x_psum = sem("e_x_psum")
        xT_ready = sem("e_xT_ready")
        whi_ready = sem("e_whi_ready")
        wlo_ready = sem("e_wlo_ready")
        gu_ready = sem("e_gu_ready")
        silu_ready = sem("e_silu_ready")
        hid_ready = sem("e_hid_ready")
        hhi_ready = sem("e_hhi_ready")
        hlo_ready = sem("e_hlo_ready")
        y_ready = sem("e_y_ready")
        y_copied = sem("e_y_copied")

        def seen(it, j, back):
            return not isinstance(it, int) or it * U + j >= back

        with nc.Block() as block:
            def load_last(eng):
                assert T * TOPK > 2 * U * BLK
                return eng.value_load(expert_row[0:1, NBLK:NBLK + 1], min_val=1, max_val=NBLK // U - 2) + 1

            @block.sync
            def _(sp):
                def body(it):
                    for j in range(U):
                        r = j % 2
                        e = sp.value_load(expert_row[0:1, bass.ds(it * U + j, 1)], min_val=0, max_val=E - 1)
                        for k in range(3):
                            if seen(it, j, 2):
                                sp.wait_ge(wlo_ready if k == 2 else gu_ready, it * U + (j - 1))
                            sp.dma_start(w[:, r, k, :], w_views[k][bass.ds(e, 1)].rearrange("e p n -> (e p) n")).then_inc(w_in[k][r], 16)
                body(0)
                with sp.Fori(1, load_last(sp) + 1) as it:
                    body(it)

            @block.gpsimd
            def _(pool):
                def body(it):
                    for j in range(U):
                        r = j % 2
                        if seen(it, j, 2):
                            pool.wait_ge(x_psum, it * (3 * U) + 3 * (j - 1))
                        pool.tensor_copy(index[:, r, 0:1], slot_token[:, bass.ds(it * U + j, 1)]).then_inc(index_ready, 1)
                        pool.tensor_copy(index[:TAIL, r, 1:2], slot_token_tail[:, bass.ds(it * U + j, 1)]).then_inc(index_ready, 1)
                        pool.wait_ge(index_ready, it * (2 * U) + 2 * (j + 1))
                        pool.nop(nofuse=True)
                        pool.indirect_dma_start(rows[:, r, :], None, sc["h2"], bass.IndirectOffsetOnAxis(ap=index[:, r, 0:1], axis=0)).then_inc(rows_in[r], 16)
                        pool.indirect_dma_start(tail[:, r, :], None, sc["h2"], bass.IndirectOffsetOnAxis(ap=index[:TAIL, r, 1:2], axis=0)).then_inc(rows_in[r], 16)
                body(0)
                with pool.Fori(1, load_last(pool) + 1) as it:
                    body(it)

            @block.tensor
            def _(pe):
                def turn_rows(it, j, q):
                    r = j % 2
                    if q == 0:
                        pe.wait_ge(rows_in[r], it * (U * 16) + 32 * (j // 2 + 1))
                    if seen(it, j, 1) or q == 2:
                        pe.wait_ge(xT_ready, it * (3 * U) + (3 * j + q - 1))
                    for c in range(CH[q]):
                        for src, t0, n in ((rows, 0, P), (tail, P, TAIL)):
                            v = src[:, r, :].rearrange("p (q c) -> p c q", c=KC)
                            last = pe.transpose(pX[:, (3 * r + q) % 2, c * BLK + t0:c * BLK + t0 + n], v[:, C0[q] + c, :], ident[:n, :n])
                    last.then_inc(x_psum, 1)

                def gate_up(it, j, turn_next):
                    r = j % 2
                    pe.wait_ge(xT_ready, it * (3 * U) + (3 * j + 3))
                    if seen(it, j, 1):
                        pe.wait_ge(hid_ready, it * U + j)
                    for k in range(2):
                        pe.wait_ge(w_in[k][r], it * (U * 8) + 16 * (j // 2 + 1))
                        for f in range(NF):
                            wv = w[:, r, k, :].rearrange("p (c q f) -> p c f q", c=KC, f=NF)
                            for c in range(KC):
                                last = pe.matmul(pG[:, k, f * BLK:(f + 1) * BLK], wv[:, c, f, :], xT[:, r, c, :], start=(c == 0), stop=(c == KC - 1))
                            if k == 1 and f == NF - 1:
                                last.then_inc(gu_ready, 1)
                            elif turn_next:
                                turn_rows(it, j + 1, 2 * k + f)

                def down(it, j):
                    r = j % 2
                    pe.wait_ge(hlo_ready, it * U + (j + 1))
                    pe.wait_ge(wlo_ready, it * U + (j + 1))
                    if seen(it, j, 1):
                        pe.wait_ge(y_copied, it * (2 * U) + 2 * j)
                    for s in range(2):
                        for h in range(2):
                            n = 0
                            for ht, wt in ((hhi, whi), (hhi, wlo), (hlo, whi)):
                                for f in range(NF):
                                    last = pe.matmul(pY[:, s, h * 512:(h + 1) * 512], ht[:, r, f, s * TAIL:s * TAIL + P],
                                                     wt[:, r, f * D + h * 512:f * D + (h + 1) * 512], start=(n == 0), stop=(n == 3 * NF - 1))
                                    n += 1
                    last.then_inc(y_ready, 1)

                def body(it, which):
                    for j in range(U):
                        gate_up(it, j, which != "last" or j < U - 1)
                        if which != "first" or j > 0:
                            down(it, j - 1)
                for q in range(3):
                    turn_rows(0, 0, q)
                body(0, "first")
                last = load_last(pe)
                with pe.Fori(1, last) as it:
                    body(it, "middle")
                body(last, "last")
                down(last, U - 1)

            @block.scalar
            def _(act):
                def w_high(it, j):
                    r = j % 2
                    act.wait_ge(w_in[2][r], it * (U * 8) + 16 * (j // 2 + 1))
                    if seen(it, j, 2):
                        act.wait_ge(y_ready, it * U + (j - 1))
                    act.activation(whi[:, r, :], w[:, r, 2, :], ACT.Copy).then_inc(whi_ready, 1)

                def gate(it, j):
                    r = j % 2
                    act.wait_ge(gu_ready, it * U + (j + 1))
                    act.activation(silu[:, :, :].rearrange("p f t -> p (f t)"), pG[:, 0, :NF * BLK], ACT.Silu).then_inc(silu_ready, 1)

                def hid_high(it, j):
                    r = j % 2
                    act.wait_ge(hid_ready, it * U + (j + 1))
                    if seen(it, j, 2):
                        act.wait_ge(y_ready, it * U + (j - 1))
                    act.activation(hhi[:, r, :, :], hid[:, :, :], ACT.Copy).then_inc(hhi_ready, 1)

                def put(it, j):
                    act.wait_ge(y_ready, it * U + (j + 1))
                    if seen(it, j, 1):
                        act.wait_ge(y_out, it * (U * 32) + 32 * j)
                    act.activation(y[:, 0, :], pY[:, 0, :], ACT.Copy).then_inc(y_copied, 1)
                    act.activation(y[SKIP:, 1, :], pY[SKIP:, 1, :], ACT.Copy).then_inc(y_copied, 1)
                    act.wait_ge(y_copied, it * (2 * U) + 2 * (j + 1))
                    act.dma_start(sc["y"][bass.ds(it * (U * BLK) + j * BLK, P), :], y[:, 0, :]).then_inc(y_out, 16)
                    act.dma_start(sc["y"][bass.ds(it * (U * BLK) + (j * BLK + P), TAIL), :], y[SKIP:, 1, :]).then_inc(y_out, 16)

                def body(it, which):
                    for j in range(U):
                        w_high(it, j)
                        gate(it, j)
                        hid_high(it, j)
                        if which != "first" or j > 0:
                            put(it, j - 1)
                body(0, "first")
                last = load_last(act)
                with act.Fori(1, last + 1) as it:
                    body(it, "middle")
                put(last, U - 1)
                act.wait_ge(y_out, last * (U * 32) + U * 32)
                act.nop(nofuse=True)

            @block.vector
            def _(dve):
                def take_rows(it, j, q):
                    r = j % 2
                    dve.wait_ge(x_psum, it * (3 * U) + (3 * j + q + 1))
                    if seen(it, j, 2):
                        dve.wait_ge(gu_ready, it * U + (j - 1))
                    dve.tensor_copy(xT[:, r, C0[q]:C0[q] + CH[q], :],
                                    pX[:, (3 * r + q) % 2, :CH[q] * BLK].rearrange("p (c t) -> p c t", t=BLK)).then_inc(xT_ready, 1)

                def w_low(it, j):
                    r = j % 2
                    dve.wait_ge(whi_ready, it * U + (j + 1))
                    if seen(it, j, 2):
                        dve.wait_ge(y_ready, it * U + (j - 1))
                    dve.tensor_tensor(wlo[:, r, :], w[:, r, 2, :], whi[:, r, :].bitcast(F32), ALU.subtract).then_inc(wlo_ready, 1)

                def gate(it, j):
                    r = j % 2
                    dve.wait_ge(silu_ready, it * U + (j + 1))
                    if seen(it, j, 1):
                        dve.wait_ge(hlo_ready, it * U + j)
                    dve.tensor_tensor(hid[:, :, :].rearrange("p f t -> p (f t)"), silu[:, :, :].rearrange("p f t -> p (f t)"),
                                      pG[:, 1, :NF * BLK], ALU.mult).then_inc(hid_ready, 1)
                    dve.wait_ge(hhi_ready, it * U + (j + 1))
                    if seen(it, j, 2):
                        dve.wait_ge(y_ready, it * U + (j - 1))
                    dve.tensor_tensor(hlo[:, r, :, :], hid[:, :, :], hhi[:, r, :, :].bitcast(F32), ALU.subtract).then_inc(hlo_ready, 1)

                def body(it, which):
                    for j in range(U):
                        ahead = which != "last" or j < U - 1
                        if ahead:
                            take_rows(it, j + 1, 0)
                        w_low(it, j)
                        if ahead:
                            take_rows(it, j + 1, 1)
                            take_rows(it, j + 1, 2)
                        gate(it, j)
                for q in range(3):
                    take_rows(0, 0, q)
                body(0, "first")
                last = load_last(dve)
                with dve.Fori(1, last) as it:
                    body(it, "middle")
                body(last, "last")


def phase_combine(nc, a, o, sc, dest, weight):
    R = 8
    with ExitStack() as ctx:
        sb = lambda name, shape, dt=F32: ctx.enter_context(nc.sbuf_tensor(name, shape, dt))
        sem = sc["semaphore"]
        part = sb("part_y", [P, R, D])
        acc = sb("acc_y", [P, 2, D])
        acc_in = [sem(f"c_acc_in{i}") for i in range(2)]
        part_in = [sem(f"c_part_in{i}") for i in range(R)]
        out_stored = [sem(f"c_out_stored{i}") for i in range(2)]
        added = sem("c_added")
        with nc.Block() as block:
            @block.sync
            def _(sp):
                for t in range(NT + 1):
                    if t < NT:
                        m = rows_of(t)
                        if t >= 2:
                            sp.wait_ge(out_stored[t % 2], 16 * (t // 2))
                        sp.dma_start(acc[:m, t % 2, :], sc["x2"][t * P:t * P + m, :]).then_inc(acc_in[t % 2], 16)
                    if t >= 1:
                        u = t - 1
                        m = rows_of(u)
                        sp.wait_ge(added, TOPK * (u + 1))
                        dst = o[0][0, u * P:u * P + P] if u < NT - 1 else o[1][:, 0]
                        sp.dma_start(dst, acc[:m, u % 2, :]).then_inc(out_stored[u % 2], 16)
                for i in range(2):
                    sp.wait_ge(out_stored[i], 16 * len(range(i, NT, 2)))

            @block.gpsimd
            def _(pool):
                for t in range(NT):
                    m = rows_of(t)
                    for k in range(TOPK):
                        n = t * TOPK + k
                        if n >= R:
                            pool.wait_ge(added, n - R + 1)
                        pool.indirect_dma_start(part[:m, n % R, :], None, sc["y"],
                                                bass.IndirectOffsetOnAxis(ap=dest[:m, n:n + 1], axis=0)).then_inc(part_in[n % R], 16)

            @block.vector
            def _(dve):
                for t in range(NT):
                    m = rows_of(t)
                    dve.wait_ge(acc_in[t % 2], 16 * (t // 2 + 1))
                    for k in range(TOPK):
                        n = t * TOPK + k
                        dve.wait_ge(part_in[n % R], 16 * (n // R + 1))
                        dve.scalar_tensor_tensor(acc[:m, t % 2, :], part[:m, n % R, :], weight[:m, n:n + 1], acc[:m, t % 2, :],
                                                 ALU.mult, ALU.add).then_inc(added, 1)
                        dve.wait_ge(added, n + 1)


_INS = ['x_prompt', 'x_sample', 'cache_sb_kv', 'page_table', 'cache_win0_kv', 'cache_win1_kv', 'cache_win2_kv',
        'norm1_g', 'w_in', 'qn_g', 'kn_g', 'sb_bias', 'w_br_a', 'w_br_b', 'w_out', 'norm2_g', 'w_router', 'router_bias',
        'w_e_gate', 'w_e_up', 'w_e_down', 'w_s_gate', 'w_s_up', 'w_s_down']
_OUTS = ([(1, S, D), (NS, 1, D), (1, 1, S, 2, SBH, HD), (1, NS, 1, 2, SBH, HD)]
         + [s for w in WIN for s in ((1, 1, min(w, S), 2, GH, HD), (1, NS, w, 2, GH, HD))])


def shape_constants():
    c = {}
    i, j = np.arange(P)[:, None], np.arange(P)[None, :]
    c["ident"] = (i == j).astype(np.float32)
    c["ntri"] = -(i >= j).astype(np.float32)
    c["nones"] = -np.ones((P, P), np.float32)
    c["ones"] = np.ones((P, P), np.float32)
    g = np.arange(EG)
    c["earlier"] = np.broadcast_to((g[None, :] < g[:, None]).astype(np.float32), (P, EG, EG)).copy()
    tok = np.arange(NT)[None, :] * P + i
    c["valid"] = (tok < T).astype(np.float32)
    c["tokid"] = tok.astype(np.int32)
    c["turn_first"] = np.broadcast_to(np.arange(0, NBLK, TURN, dtype=np.float32), (P, NBLK // TURN)).copy()
    c["number"] = i.astype(np.float32)
    c["before"] = (i < j).astype(np.float32)
    jj = np.arange(2 * P)[None, :]
    c["band"] = np.where((jj >= i) & (jj <= i + P), 0, -BIG).astype(np.float32)
    share = DIL[2] // (S // P)
    c["pairs"] = np.where((i % share == j % share) & (j <= i), 0, -BIG).astype(np.float32)
    half = HD // 2
    inv = np.float32(10000.0) ** (-np.arange(half, dtype=np.float32) / np.float32(half))
    pos = np.zeros(NT * P, np.float32)
    pos[:S] = np.arange(S)
    pos[S:] = PAST
    ang = pos[:, None] * inv.astype(np.float32)[None, :]
    c["cos"] = np.cos(ang).astype(np.float32).reshape(NT, P, half).transpose(1, 0, 2).copy()
    c["sin"] = np.sin(ang).astype(np.float32).reshape(NT, P, half).transpose(1, 0, 2).copy()
    return c


def kernel(**inputs):
    import concourse.bacc as _bacc
    from concourse.bass_utils import run_bass_kernel_spmd as _run

    nc = _bacc.Bacc("TRN2", target_bir_lowering=False, num_devices=1)
    arrays, a = {}, {}
    given = {name: np.ascontiguousarray(inputs[name]) for name in _INS}
    given.update(shape_constants())
    for name, arr in given.items():
        arrays[f"in_{name}"] = arr
        a[name] = nc.dram_tensor(f"in_{name}", arr.shape, mybir.dt.from_np(arr.dtype), kind="ExternalInput").ap()
    o = [nc.dram_tensor(f"out_{i}", shape, F32, kind="ExternalOutput").ap() for i, shape in enumerate(_OUTS)]
    build(nc, a, o)
    r = _run(nc, [arrays], core_ids=[0])
    return tuple(r.results[0][f"out_{i}"] for i in range(len(_OUTS)))
```
